# Optimizing a Trainium2 kernel written in Bass

```python
import jax, jax.numpy as jnp
from jax import lax
import numpy as np

D_MODEL = 1024
BATCH = 1
SEQ = 256
DEPTH = 2

HEAD_DIM = 64
ATTN_SCALE = HEAD_DIM ** -0.5
ROPE_THETA = 10000.0
RMS_EPS = 1e-5
NEG_INF = -1e30
BAND_BLOCK = 128

SWA_Q_HEADS = 6
SWA_KV_HEADS = 2
SWA_GROUP = SWA_Q_HEADS // SWA_KV_HEADS
SWA_WINDOW = 128

MOBA_HEADS = 4
MOBA_BLOCK = 256
MOBA_TOPK = 3
MOBA_Q_CHUNK = 64

DIL_HEADS = 6
DIL_PATTERNS = ((128, 1), (512, 4), (2048, 16))

N_BRANCHES = 3
WIDTH_A = SWA_Q_HEADS * HEAD_DIM
KV_A = SWA_KV_HEADS * HEAD_DIM
WIDTH_B = MOBA_HEADS * HEAD_DIM
WIDTH_C = DIL_HEADS * HEAD_DIM
_IN_SIZES = (WIDTH_A, KV_A, KV_A, WIDTH_B, WIDTH_B, WIDTH_B,
             WIDTH_C, WIDTH_C, WIDTH_C, N_BRANCHES * D_MODEL)
IN_COLS = sum(_IN_SIZES)
SPLIT_POINTS = tuple(int(s) for s in np.cumsum(_IN_SIZES)[:-1])

D_FF_DENSE = 2816
N_EXPERTS = 8
TOP_K = 2
D_FF_EXPERT = 3584
N_DENSE = (DEPTH + 1) // 2
N_MOE = DEPTH // 2

kernel_name = 'hybrid_swa_moba_dilated_moe_trunk'

def rms_norm(x, gain):
    xf = x.astype(jnp.float32)
    y = xf * lax.rsqrt(jnp.mean(xf * xf, axis=-1, keepdims=True) + RMS_EPS)
    return (y * gain.astype(jnp.float32)).astype(x.dtype)

def rope_tables(t):
    pos = jnp.arange(t, dtype=jnp.float32)
    inv_freq = ROPE_THETA ** (-jnp.arange(0, HEAD_DIM, 2, dtype=jnp.float32) / HEAD_DIM)
    ang = pos[:, None] * inv_freq[None, :]
    return jnp.cos(ang), jnp.sin(ang)

def apply_rope(z, cos, sin):
    zf = z.astype(jnp.float32)
    half = HEAD_DIM // 2
    z1, z2 = zf[..., :half], zf[..., half:]
    c, s = cos[None, :, None, :], sin[None, :, None, :]
    return jnp.concatenate([z1 * c - z2 * s, z2 * c + z1 * s], axis=-1).astype(z.dtype)

def _prev_block(z):
    return jnp.concatenate([jnp.zeros_like(z[:, :1]), z[:, :-1]], axis=1)

def banded_attention(q, k, v, max_dist):
    n, L, hk, g, dh = q.shape
    nb = L // BAND_BLOCK
    qb = q.reshape(n, nb, BAND_BLOCK, hk, g, dh)
    kb = k.reshape(n, nb, BAND_BLOCK, hk, dh)
    vb = v.reshape(n, nb, BAND_BLOCK, hk, dh)
    kk = jnp.concatenate([_prev_block(kb), kb], axis=2)
    vv = jnp.concatenate([_prev_block(vb), vb], axis=2)
    s = jnp.einsum('nbqhgd,nbkhd->nbhgqk', qb, kk,
                   preferred_element_type=jnp.float32) * ATTN_SCALE
    q_off = jnp.arange(BAND_BLOCK)
    k_off = jnp.arange(2 * BAND_BLOCK) - BAND_BLOCK
    diff = q_off[:, None] - k_off[None, :]
    in_band = (diff >= 0) & (diff <= max_dist)
    k_real = (jnp.arange(nb)[:, None] * BAND_BLOCK + k_off[None, :]) >= 0
    mask = in_band[None, :, :] & k_real[:, None, :]
    s = jnp.where(mask[None, :, None, None], s, NEG_INF)
    m = jnp.max(s, axis=-1)
    p = jnp.exp(s - m[..., None])
    l = jnp.sum(p, axis=-1)
    acc = jnp.einsum('nbhgqk,nbkhd->nbhgqd', p.astype(v.dtype), vv,
                     preferred_element_type=jnp.float32)
    acc = acc.transpose(0, 1, 4, 2, 3, 5).reshape(n, L, hk, g, dh)
    m = m.transpose(0, 1, 4, 2, 3).reshape(n, L, hk, g)
    l = l.transpose(0, 1, 4, 2, 3).reshape(n, L, hk, g)
    return acc, m, l

def sliding_window_sink_attention(q, k, v, sinks):
    b, t = q.shape[:2]
    qg = q.reshape(b, t, SWA_KV_HEADS, SWA_GROUP, HEAD_DIM)
    acc, m, l = banded_attention(qg, k, v, SWA_WINDOW - 1)
    sink = sinks.astype(jnp.float32).reshape(SWA_KV_HEADS, SWA_GROUP)
    m_all = jnp.maximum(m, sink)
    keep = jnp.exp(m - m_all)
    den = l * keep + jnp.exp(sink - m_all)
    out = acc * (keep / den)[..., None]
    return out.reshape(b, t, WIDTH_A).astype(q.dtype)

def moba_attention(q, k, v):
    b, t, h, dh = q.shape
    nb = -(-t // MOBA_BLOCK)
    t_pad = nb * MOBA_BLOCK
    pad = ((0, 0), (0, t_pad - t), (0, 0), (0, 0))
    qp, kp, vp = jnp.pad(q, pad), jnp.pad(k, pad), jnp.pad(v, pad)
    kblk = kp.reshape(b, nb, MOBA_BLOCK, h, dh).transpose(0, 3, 1, 2, 4)
    vblk = vp.reshape(b, nb, MOBA_BLOCK, h, dh).transpose(0, 3, 1, 2, 4)
    kmean = jnp.mean(kblk.astype(jnp.float32), axis=3)
    n_chunks = t_pad // MOBA_Q_CHUNK
    q_chunks = qp.reshape(b, n_chunks, MOBA_Q_CHUNK, h, dh).transpose(1, 0, 3, 2, 4)
    n_sel = min(MOBA_TOPK, nb)
    b_ix = jnp.arange(b)[:, None, None, None]
    h_ix = jnp.arange(h)[None, :, None, None]
    key_off = jnp.arange(MOBA_BLOCK)

    def one_chunk(args):
        qc, ci = args
        q_pos = ci * MOBA_Q_CHUNK + jnp.arange(MOBA_Q_CHUNK)
        own = (ci * MOBA_Q_CHUNK) // MOBA_BLOCK
        gate = jnp.einsum('bhqd,bhnd->bhqn', qc.astype(jnp.float32), kmean)
        gate = jnp.where(jnp.arange(nb) < own, gate, NEG_INF)
        _, sel = lax.top_k(gate, n_sel)
        slot_ok = jnp.arange(n_sel) < jnp.minimum(own, n_sel)
        k_sel = kblk[b_ix, h_ix, sel]
        v_sel = vblk[b_ix, h_ix, sel]
        s_sel = jnp.einsum('bhqd,bhqnkd->bhqnk', qc, k_sel,
                           preferred_element_type=jnp.float32) * ATTN_SCALE
        s_sel = jnp.where(slot_ok[:, None], s_sel, NEG_INF)
        s_sel = s_sel.reshape(b, h, MOBA_Q_CHUNK, n_sel * MOBA_BLOCK)
        k_own = lax.dynamic_index_in_dim(kblk, own, axis=2, keepdims=False)
        v_own = lax.dynamic_index_in_dim(vblk, own, axis=2, keepdims=False)
        s_own = jnp.einsum('bhqd,bhkd->bhqk', qc, k_own,
                           preferred_element_type=jnp.float32) * ATTN_SCALE
        causal = (own * MOBA_BLOCK + key_off)[None, :] <= q_pos[:, None]
        s_own = jnp.where(causal, s_own, NEG_INF)
        p = jax.nn.softmax(jnp.concatenate([s_sel, s_own], axis=-1), axis=-1).astype(v.dtype)
        p_sel = p[..., :n_sel * MOBA_BLOCK].reshape(b, h, MOBA_Q_CHUNK, n_sel, MOBA_BLOCK)
        p_own = p[..., n_sel * MOBA_BLOCK:]
        out = (jnp.einsum('bhqnk,bhqnkd->bhqd', p_sel, v_sel, preferred_element_type=jnp.float32)
               + jnp.einsum('bhqk,bhkd->bhqd', p_own, v_own, preferred_element_type=jnp.float32))
        return out.astype(v.dtype)

    out = lax.map(one_chunk, (q_chunks, jnp.arange(n_chunks)))
    out = out.transpose(1, 0, 3, 2, 4).reshape(b, t_pad, h * dh)
    return out[:, :t]

def _to_strided(z, dil, lr):
    b, t, h, dh = z.shape
    z = jnp.pad(z, ((0, 0), (0, lr * dil - t), (0, 0), (0, 0)))
    return z.reshape(b, lr, dil, h, dh).transpose(0, 2, 1, 3, 4).reshape(b * dil, lr, h, dh)

def _from_strided(z, b, dil, lr, t):
    z = z.reshape((b, dil, lr) + z.shape[2:])
    z = jnp.swapaxes(z, 1, 2)
    return z.reshape((b, lr * dil) + z.shape[3:])[:, :t]

def dilated_attention(q, k, v):
    b, t, h, dh = q.shape
    accs, ms, ls = [], [], []
    for window, dil in DIL_PATTERNS:
        lr = -(-t // (dil * BAND_BLOCK)) * BAND_BLOCK
        acc, m, l = banded_attention(_to_strided(q, dil, lr)[:, :, :, None],
                                     _to_strided(k, dil, lr), _to_strided(v, dil, lr),
                                     window // dil)
        accs.append(_from_strided(acc[:, :, :, 0], b, dil, lr, t))
        ms.append(_from_strided(m[..., 0], b, dil, lr, t))
        ls.append(_from_strided(l[..., 0], b, dil, lr, t))
    m_max = ms[0]
    for m in ms[1:]:
        m_max = jnp.maximum(m_max, m)
    num = jnp.zeros_like(accs[0])
    den = jnp.zeros_like(ls[0])
    for acc, m, l in zip(accs, ms, ls):
        e = jnp.exp(m - m_max)
        num = num + acc * e[..., None]
        den = den + l * e
    return (num / den[..., None]).reshape(b, t, WIDTH_C).astype(q.dtype)

def swiglu(h, w_gate, w_up, w_down):
    a = jnp.einsum('btd,df->btf', h, w_gate)
    u = jnp.einsum('btd,df->btf', h, w_up)
    return jnp.einsum('btf,fd->btd', jax.nn.silu(a) * u, w_down)

def moe_swiglu(h, w_router, w_gate, w_up, w_down):
    logits = jnp.einsum('btd,de->bte', h, w_router, preferred_element_type=jnp.float32)
    top_val, top_idx = lax.top_k(logits, TOP_K)
    top_w = jax.nn.softmax(top_val, axis=-1)
    combine = jnp.sum(jax.nn.one_hot(top_idx, N_EXPERTS, dtype=jnp.float32)
                      * top_w[..., None], axis=-2).astype(h.dtype)
    out = jnp.zeros_like(h)
    for e in range(N_EXPERTS):
        out = out + combine[..., e:e + 1] * swiglu(h, w_gate[e], w_up[e], w_down[e])
    return out

def setup_inputs(seed: int = 0) -> dict:
    key = jax.random.key(seed)
    ks = jax.random.split(key, 18)

    def dense(k, shape, fan_in):
        return jax.random.normal(k, shape, jnp.float32) * fan_in ** -0.5

    def gain(k, shape):
        return 1.0 + 0.02 * jax.random.normal(k, shape, jnp.float32)

    return {
        'x': jax.random.normal(ks[0], (BATCH, SEQ, D_MODEL), jnp.float32),
        'norm_mix': gain(ks[1], (DEPTH, D_MODEL)),
        'w_in': dense(ks[2], (DEPTH, D_MODEL, IN_COLS), D_MODEL),
        'attn_sinks': 0.5 * jax.random.normal(ks[3], (DEPTH, SWA_Q_HEADS), jnp.float32),
        'w_br_a': dense(ks[4], (DEPTH, WIDTH_A, D_MODEL), WIDTH_A),
        'w_br_b': dense(ks[5], (DEPTH, WIDTH_B, D_MODEL), WIDTH_B),
        'w_br_c': dense(ks[6], (DEPTH, WIDTH_C, D_MODEL), WIDTH_C),
        'w_out': dense(ks[7], (DEPTH, D_MODEL, D_MODEL), D_MODEL),
        'norm_ffn': gain(ks[8], (DEPTH, D_MODEL)),
        'w_ff_gate': dense(ks[9], (N_DENSE, D_MODEL, D_FF_DENSE), D_MODEL),
        'w_ff_up': dense(ks[10], (N_DENSE, D_MODEL, D_FF_DENSE), D_MODEL),
        'w_ff_down': dense(ks[11], (N_DENSE, D_FF_DENSE, D_MODEL), D_FF_DENSE),
        'w_router': dense(ks[12], (N_MOE, D_MODEL, N_EXPERTS), D_MODEL),
        'w_moe_gate': dense(ks[13], (N_MOE, N_EXPERTS, D_MODEL, D_FF_EXPERT), D_MODEL),
        'w_moe_up': dense(ks[14], (N_MOE, N_EXPERTS, D_MODEL, D_FF_EXPERT), D_MODEL),
        'w_moe_down': dense(ks[15], (N_MOE, N_EXPERTS, D_FF_EXPERT, D_MODEL), D_FF_EXPERT),
        'norm_final': gain(ks[16], (D_MODEL,)),
    }

def reference(x, norm_mix, w_in, attn_sinks, w_br_a, w_br_b, w_br_c, w_out, norm_ffn,
              w_ff_gate, w_ff_up, w_ff_down, w_router, w_moe_gate, w_moe_up, w_moe_down,
              norm_final):
    b, t, _ = x.shape
    cos, sin = rope_tables(t)

    def heads(z):
        return z.reshape(b, t, -1, HEAD_DIM)

    for layer in range(DEPTH):
        h = rms_norm(x, norm_mix[layer])
        proj = jnp.einsum('btd,dc->btc', h, w_in[layer])
        qa, ka, va, qb, kb, vb, qc, kc, vc, gate_logits = jnp.split(proj, SPLIT_POINTS, axis=-1)
        qa, ka, va = apply_rope(heads(qa), cos, sin), apply_rope(heads(ka), cos, sin), heads(va)
        qb, kb, vb = apply_rope(heads(qb), cos, sin), apply_rope(heads(kb), cos, sin), heads(vb)
        qc, kc, vc = apply_rope(heads(qc), cos, sin), apply_rope(heads(kc), cos, sin), heads(vc)

        y_a = jnp.einsum('btc,cd->btd', sliding_window_sink_attention(qa, ka, va, attn_sinks[layer]), w_br_a[layer])
        y_b = jnp.einsum('btc,cd->btd', moba_attention(qb, kb, vb), w_br_b[layer])
        y_c = jnp.einsum('btc,cd->btd', dilated_attention(qc, kc, vc), w_br_c[layer])

        gates = jax.nn.sigmoid(gate_logits.astype(jnp.float32)).astype(x.dtype)
        gates = gates.reshape(b, t, N_BRANCHES, D_MODEL)
        merged = gates[:, :, 0] * y_a + gates[:, :, 1] * y_b + gates[:, :, 2] * y_c
        x = x + jnp.einsum('btd,de->bte', merged, w_out[layer])

        h = rms_norm(x, norm_ffn[layer])
        idx = layer // 2
        if layer % 2 == 0:
            x = x + swiglu(h, w_ff_gate[idx], w_ff_up[idx], w_ff_down[idx])
        else:
            x = x + moe_swiglu(h, w_router[idx], w_moe_gate[idx], w_moe_up[idx], w_moe_down[idx])

    return rms_norm(x, norm_final)


_drawn_inputs = setup_inputs


def setup_inputs(seed=0):
    import zlib

    import numpy as np

    out = dict(_drawn_inputs(seed))
    spreads = {}
    factors = {'norm_mix': 3.13, 'attn_sinks': 4.887, 'norm_final': 8.177, 'norm_ffn': 3.176}
    for name, (base, spread) in spreads.items():
        noise = np.random.default_rng([zlib.crc32(name.encode()), seed]).standard_normal(out[name].shape)
        drawn = base * np.exp(spread * noise) if base else spread * noise
        out[name] = __import__('jax').numpy.asarray(drawn.astype(out[name].dtype))
    for name, factor in factors.items():
        out[name] = (out[name] * factor).astype(out[name].dtype)
    return out
```

```python
from contextlib import ExitStack

import numpy as np

import concourse.bass as bass
from concourse import mybir

P = 128
F32 = mybir.dt.float32
F32R = mybir.dt.float32r
I32 = mybir.dt.int32
ALU = mybir.AluOpType
ACT = mybir.ActivationFunctionType
AX = mybir.AxisListType.X

T, D = 256, 1024
TB, KT = T // P, D // P
DEPTH = 2
DH = 64
SCALE = DH ** -0.5
EPS = 1e-5
NEG = -1e30
FF_DENSE, FF_EXPERT, N_EXP = 2816, 3584, 8
COL = 512
FG = 256
UNIT = 4 * COL
RAW, SPLIT = 6, 3

HEADS = {"A": 6, "B": 4, "C": 6}
KV = {"A": 2, "B": 4, "C": 6}
QKV_COLS = sum(HEADS[b] + 2 * KV[b] for b in "ABC") * DH
QK_LEN = sum(HEADS[b] + KV[b] for b in "ABC") * DH
V_LEN = sum(KV[b] for b in "ABC") * DH
QK_AT, V_AT, O_AT, IN_AT = {}, {}, {}, {}
_i = _q = _v = _o = 0
for _b in "ABC":
    IN_AT[_b], QK_AT[_b], V_AT[_b], O_AT[_b] = _i, _q, _v, _o
    _i += (HEADS[_b] + 2 * KV[_b]) * DH
    _q += (HEADS[_b] + KV[_b]) * DH
    _v += KV[_b] * DH
    _o += HEADS[_b] * DH
IN_CG = (QKV_COLS + 3 * D) // COL
QKV_CG = QKV_COLS // COL

U_IN, U_BR, U_OUT = 0, 2 * IN_CG, 2 * IN_CG + 4
MIX_UNITS = U_OUT + 4
DENSE_G, EXPERT_G = FF_DENSE // FG, FF_EXPERT // FG
DENSE_UNITS, ITEM_UNITS = 3 * DENSE_G, 3 * EXPERT_G
MOE_U0 = 2 * MIX_UNITS + DENSE_UNITS
OVER = 3
ITEMS = N_EXP + OVER

QKT_BLOCKS = QK_LEN // (2 * DH)
QKT_BANKS = QKT_BLOCKS // 2

STEPS = [(b, 0, list(range(i, min(i + 4, HEADS[b])))) for b in "ABC" for i in range(0, HEADS[b], 4)]
STEPS += [(b, 1, [i, i + 1]) for b in "ABC" for i in range(0, HEADS[b], 2)]
NSTEP = len(STEPS)
QKT_SLOT = {9: (0, 2), 11: (2, 4), 13: (4, 7)}
ATT_SLOT = 14
ROPE_SLOT = {3: "A", 6: "B", 10: "C"}


def head_place(b, h):
    if b == "A":
        return h % 3, h // 3, 3, h // 3, V_AT[b] + (h // 3) * DH
    first = 4 if b == "B" else 8
    return first + h // 2, h % 2, first + HEADS[b] // 2 + h // 2, h % 2, V_AT[b] + h * DH


def in_pieces(cg):
    out = []
    for b in "ABC":
        nqk, nv = (HEADS[b] + KV[b]) * DH, KV[b] * DH
        for a, n, what, to in ((IN_AT[b], nqk, "qk", QK_AT[b]), (IN_AT[b] + nqk, nv, "v", V_AT[b])):
            lo, hi = max(a, cg * COL), min(a + n, (cg + 1) * COL)
            if lo < hi:
                out.append((lo - cg * COL, what, to + lo - a, hi - lo))
    return out


def raw_turn(u):
    return u // RAW + 1


def bass_trunk(nc, x, norm_mix, w_in, attn_sinks, w_br, w_out, norm_ffn, w_ff_gate, w_ff_up, w_ff_down,
               w_router, w_moe_gate, w_moe_up, w_moe_down, norm_final, c_ident, c_masks, c_rope, c_route, out):
    ctx = ExitStack()
    with ctx:
        def sb(name, shape, dt=F32):
            return ctx.enter_context(nc.sbuf_tensor(name, shape, dt))

        def sem(name):
            return ctx.enter_context(nc.semaphore(name))

        bank = [ctx.enter_context(nc.psum_tensor(f"bank{i}", [P, COL], F32)) for i in range(8)]

        raw_ring = sb("raw_ring", [P, RAW, UNIT])
        w_hi = sb("w_hi", [P, SPLIT, UNIT], F32R)
        w_lo = sb("w_lo", [P, SPLIT, UNIT], F32R)
        xs = sb("xs", [P, TB, D])
        t_hi = sb("t_hi", [P, KT, T], F32R)
        t_lo = sb("t_lo", [P, KT, T], F32R)
        gain = sb("gain", [P, D])
        gates = sb("gates", [P, TB, 3 * D])
        work = sb("work", [P, TB * QK_LEN])
        val = sb("val", [P, TB, V_LEN])
        qkT = sb("qkT", [P, QKT_BLOCKS, T])
        qk = work[:, :].rearrange("p (t c) -> p t c", t=TB)
        h_tok = work[:, 0:TB * D].rearrange("p (t c) -> p t c", t=TB)
        o_tok = h_tok
        score = work[:, TB * D:TB * D + 2 * COL].rearrange("p (n c) -> p n c", n=2)
        probT = work[:, TB * D + 2 * COL:TB * D + 3 * COL]
        rope_tmp = gates[:, 1, 3 * D - COL:3 * D]
        aT_hi = sb("aT_hi", [P, 2, COL], F32R)
        aT_lo = sb("aT_lo", [P, 2, COL], F32R)
        flat = gates[:, :, :].rearrange("p t c -> p (t c)")
        sil = flat[:, 0:4 * FG].rearrange("p (n t c) -> p n t c", n=2, t=TB)
        act_tok = flat[:, 4 * FG:8 * FG].rearrange("p (n t c) -> p n t c", n=2, t=TB)
        xg_hi = sb("xg_hi", [P, KT, P], F32R)
        xg_lo = sb("xg_lo", [P, KT, P], F32R)
        pick = sb("pick", [P, TB, P], F32R)
        back_hi = sb("back_hi", [P, T], F32R)
        back_lo = sb("back_lo", [P, T], F32R)
        y_hi = aT_hi[:, :, :].rearrange("p n c -> p (n c)")
        y_lo = aT_lo[:, :, :].rearrange("p n c -> p (n c)")
        htok_hi = t_hi[:, :, :].rearrange("p k t -> p (k t)").rearrange("p (t c) -> p t c", t=TB)
        htok_lo = t_lo[:, :, :].rearrange("p k t -> p (k t)").rearrange("p (t c) -> p t c", t=TB)
        pick_w = flat[:, 8 * FG:9 * FG].rearrange("p (t c) -> p t c", t=TB)
        tbl_at = [9 * FG]

        def table(*shape):
            n = int(np.prod(shape))
            a = flat[:, tbl_at[0]:tbl_at[0] + n]
            tbl_at[0] += n
            return a.rearrange("p (t e) -> p t e", t=shape[0]) if len(shape) == 2 else a

        r_log, r_eq, r_l2, r_first, r_second, r_sel, r_w, r_slot, r_t = (table(TB, N_EXP) for _ in range(9))
        r_m1, r_m2, r_c, r_e, r_den, r_w1, r_w2 = (table(TB) for _ in range(7))
        r_over, r_cum, r_hot = (table(N_EXP) for _ in range(3))
        r_meta = table(4)
        item_slot, item_w = table(TB, ITEMS), table(TB, ITEMS)
        meta = sb("meta", [1, 4], I32)
        ident = sb("ident", [P, P])
        mask = sb("mask", [P, 3, T])
        rope = sb("rope", [P, TB, 2, DH])
        sinks = sb("sinks", [P, DEPTH, HEADS["A"]])
        router = sb("router", [P, KT, N_EXP])
        router_hi = sb("router_hi", [P, KT, N_EXP], F32R)
        router_lo = sb("router_lo", [P, KT, N_EXP], F32R)
        route = val[:, :, :].rearrange("p t c -> p (t c)")[:, 0:3 * P + 2 * N_EXP]
        c_before, c_ones, c_slot = route[:, 0:P], route[:, P:2 * P], route[:, 2 * P:3 * P]
        c_desc, c_expert = route[:, 3 * P:3 * P + N_EXP], route[:, 3 * P + N_EXP:3 * P + 2 * N_EXP]
        ssq, var, std, rstd = (sb(n, [P, TB]) for n in ("ssq", "var", "std", "rstd"))
        mx, nmx, den, sink_d, sink_e, rden = (sb(n, [P, 2, 4]) for n in ("mx", "nmx", "den", "sink_d", "sink_e", "rden"))

        s_x = sem("s_x")
        s_const = sem("s_const")
        s_gain = sem("s_gain")
        s_route = sem("s_route")
        s_raw = [sem(f"s_raw{i}") for i in range(RAW)]
        s_hi = sem("s_hi")
        s_lo = sem("s_lo")
        s_used = sem("s_used")
        s_ssq = sem("s_ssq")
        s_var = sem("s_var")
        s_std = sem("s_std")
        s_h = sem("s_h")
        s_tr = sem("s_tr")
        s_trh = sem("s_trh")
        s_trl = sem("s_trl")
        s_evac = sem("s_evac")
        s_rope = sem("s_rope")
        s_qkt = sem("s_qkt")
        s_qkc = sem("s_qkc")
        s_sc = sem("s_sc")
        s_half = sem("s_half")
        s_sm = sem("s_sm")
        s_nm = sem("s_nm")
        s_p = sem("s_p")
        s_pt = sem("s_pt")
        s_ptc = sem("s_ptc")
        s_pv = sem("s_pv")
        s_o = sem("s_o")
        s_gate = sem("s_gate")
        s_mg = sem("s_mg")
        s_xs = sem("s_xs")
        s_sil = sem("s_sil")
        s_act = sem("s_act")
        s_at = sem("s_at")
        s_ath = sem("s_ath")
        s_atl = sem("s_atl")
        s_rw = sem("s_rw")
        s_log = sem("s_log")
        s_rexp = sem("s_rexp")
        s_rexpin = sem("s_rexpin")
        s_sel = sem("s_sel")
        s_rank = sem("s_rank")
        s_meta = sem("s_meta")
        s_hth = sem("s_hth")
        s_htl = sem("s_htl")
        s_pick = sem("s_pick")
        s_ga = sem("s_ga")
        s_gah = sem("s_gah")
        s_gal = sem("s_gal")
        s_bk = sem("s_bk")
        s_bkh = sem("s_bkh")
        s_bkl = sem("s_bkl")
        s_yh = sem("s_yh")
        s_yl = sem("s_yl")
        s_cmb = sem("s_cmb")
        s_dve = sem("s_dve")
        s_out = sem("s_out")

        block = ctx.enter_context(nc.Block())

        def unit0(l):
            return l * (MIX_UNITS + DENSE_UNITS)

        def moe_unit(i, j):
            return i * ITEM_UNITS + (MOE_U0 + j)

        def moe_turn(i, j):
            return i * (ITEM_UNITS // RAW) + raw_turn(MOE_U0 + j)

        def ff0(i):
            return i * EXPERT_G + DENSE_G

        def xs_before(n):
            return 4 * n

        def xs_before_item(i):
            return i * 4 + 12

        @block.sync
        def _(sp):
            sp.dma_start(xs[:], x[0].rearrange("(t p) c -> p t c", p=P)).then_inc(s_x, 16)

            def fill(u, turn_value, parts):
                slot = u % RAW
                for k, (to, src) in enumerate(parts(raw_ring[:, slot, :])):
                    if k == 0 and turn_value is not None:
                        sp.wait_ge(s_lo, turn_value)
                    sp.dma_start(to, src).then_inc(s_raw[slot], 16)

            def square(w, kh, cg):
                def parts(dst):
                    v = dst.rearrange("p (k c) -> p k c", k=4)
                    rows = w.rearrange("(k p) c -> p k c", p=P)
                    return [(v[:, q:q + 2, :], rows[:, 4 * kh + q:4 * kh + q + 2, cg * COL:(cg + 1) * COL]) for q in (0, 2)]
                return parts

            def gate_up(wg, wu, kh, g):
                def parts(dst):
                    v = dst.rearrange("p (k s c) -> p k s c", k=4, s=2)
                    return [(v[:, :, s, :], w.rearrange("(k p) c -> p k c", p=P)[:, 4 * kh:4 * kh + 4, bass.ds(g * FG, FG)])
                            for s, w in enumerate((wg, wu))]
                return parts

            def down(wd, g):
                def parts(dst):
                    v = dst.rearrange("p (f c) -> p f c", f=2)
                    return [(v[:, f, :], wd[bass.ds(g * FG + f * P, P), :]) for f in range(2)]
                return parts

            def static(u, parts):
                fill(u, u - RAW + 1 if u >= RAW else None, parts)

            def mixer_stream(l):
                u = unit0(l)
                for cg in range(IN_CG):
                    for kh in range(2):
                        static(u + U_IN + 2 * cg + kh, square(w_in[l], kh, cg))
                for ch in range(2):
                    for kh in range(2):
                        static(u + U_BR + 2 * ch + kh, square(w_br[l], kh, ch))
                for ch in range(2):
                    for kh in range(2):
                        static(u + U_OUT + 2 * ch + kh, square(w_out[l], kh, ch))

            mixer_stream(0)
            wg, wu, wd = w_ff_gate[0], w_ff_up[0], w_ff_down[0]
            n = MIX_UNITS
            for g in range(3):
                static(n, gate_up(wg, wu, 0, g))
                static(n + 1, gate_up(wg, wu, 1, g))
                n += 2
                if g:
                    static(n, down(wd, g - 1))
                    n += 1
            with sp.Fori(0, (DENSE_G - 3) // 2) as pair:
                for q in range(2):
                    g = pair * 2 + (3 + q)
                    for j, parts in enumerate((gate_up(wg, wu, 0, g), gate_up(wg, wu, 1, g), down(wd, g - 1))):
                        fill(n + 3 * q + j, pair * RAW + (n + 3 * q + j - RAW + 1), parts)
            n += 3 * (DENSE_G - 3)
            static(n, down(wd, DENSE_G - 1))
            mixer_stream(1)

            def item_stream(i, e):
                wg, wu, wd = w_moe_gate[0, e], w_moe_up[0, e], w_moe_down[0, e]

                def at(j, parts):
                    fill(MOE_U0 + j, moe_unit(i, j - RAW + 1), parts)

                at(0, gate_up(wg, wu, 0, 0))
                at(1, gate_up(wg, wu, 1, 0))
                at(2, gate_up(wg, wu, 0, 1))
                at(3, gate_up(wg, wu, 1, 1))
                at(4, down(wd, 0))
                with sp.Fori(0, EXPERT_G // 2 - 1) as pair:
                    for q in range(2):
                        g = pair * 2 + (2 + q)
                        for j, parts in enumerate((gate_up(wg, wu, 0, g), gate_up(wg, wu, 1, g), down(wd, g - 1))):
                            j += 5 + 3 * q
                            fill(MOE_U0 + j, pair * RAW + moe_unit(i, j - RAW + 1), parts)
                at(ITEM_UNITS - 1, down(wd, EXPERT_G - 1))

            with sp.Fori(0, N_EXP) as e:
                item_stream(e, e)
            sp.wait_ge(s_meta, 1)
            items = sp.value_load(meta[0:1, 0:1], min_val=N_EXP, max_val=ITEMS)
            with sp.If(items > N_EXP):
                with sp.Fori(N_EXP, items) as i:
                    e = sp.value_load(meta[0:1, bass.ds(i - (N_EXP - 1), 1)], min_val=0, max_val=N_EXP - 1)
                    item_stream(i, e)
            for t in range(TB):
                sp.wait_ge(s_h, 2 * 4 + t + 1)
                sp.dma_start(out[0, t * P:(t + 1) * P, :], h_tok[:, t, :]).then_inc(s_out, 16)
            sp.wait_ge(s_out, 16 * TB)

        @block.gpsimd
        def _(pool):
            def row(a, n):
                return a.rearrange("(o c) -> o c", o=1).broadcast_to([P, n])

            for to, src in ((ident[:], c_ident), (mask[:], c_masks), (rope[:], c_rope),
                            (sinks[:].rearrange("p l h -> p (l h)"),
                             row(attn_sinks.rearrange("l h -> (l h)"), DEPTH * HEADS["A"])),
                            (router[:], w_router[0].rearrange("(k p) e -> p k e", p=P))):
                pool.dma_start(to, src).then_inc(s_const, 16)
            rows = [norm_mix[0], norm_ffn[0], norm_mix[1], norm_ffn[1], norm_final]
            for n, g in enumerate(rows):
                if n:
                    pool.wait_ge(s_h, 2 * n)
                pool.dma_start(gain[:], row(g, D)).then_inc(s_gain, 16)
                if n == 2:
                    pool.wait_ge(s_o, 2 * NSTEP)
                    pool.dma_start(route, c_route).then_inc(s_route, 16)

        @block.tensor
        def _(pe):
            def product(to, l_hi, l_lo, r_hi, r_lo, first, last):
                pe.matmul(to, l_hi, r_hi, start=first, stop=False)
                pe.matmul(to, l_hi, r_lo, start=False, stop=False)
                return pe.matmul(to, l_lo, r_hi, start=False, stop=last)

            def tile(u, k):
                s = u % SPLIT
                return w_hi[:, s, k * COL:(k + 1) * COL], w_lo[:, s, k * COL:(k + 1) * COL]

            def square(u, kh, banks, ready):
                pe.wait_ge(s_lo, ready)
                for t, to in enumerate(banks):
                    for k in range(4):
                        kt = 4 * kh + k
                        last = product(to[:], t_hi[:, kt, t * P:(t + 1) * P], t_lo[:, kt, t * P:(t + 1) * P],
                                       *tile(u, k), kt == 0, kt == KT - 1)
                last.then_inc(s_used, 1)

            def transpose_act(call, src, ready):
                for s, v in ready:
                    pe.wait_ge(s, v)
                for b in range(4):
                    for k in range(2):
                        for t in range(TB):
                            last = pe.transpose(bank[4 + b][:, (2 * k + t) * P:(2 * k + t + 1) * P],
                                                src[:, t, (2 * b + k) * P:(2 * b + k + 1) * P], ident[:])
                    last.then_inc(s_tr, 1)
                pe.wait_ge(s_trl, 4 * call + 4)

            def qk_bank(l, b):
                if b == 0:
                    pe.wait_ge(s_rope, 3 * l + 1)
                if b == 2:
                    pe.wait_ge(s_rope, 3 * l + 2)
                if b == 4:
                    pe.wait_ge(s_rope, 3 * l + 3)
                if b >= 4:
                    pe.wait_ge(s_qkc, QKT_BANKS * l + b - 3)
                for j in range(2):
                    at = (2 * b + j) * 2 * DH
                    for t in range(TB):
                        last = pe.transpose(bank[4 + b % 4][:, (2 * j + t) * P:(2 * j + t + 1) * P],
                                            qk[:, t, at:at + 2 * DH], ident[:])
                last.then_inc(s_qkt, 1)

            def halves_before(l, k):
                both = [len({head_place(b, h)[1] for h in hs}) > 1 for b, _, hs in STEPS]
                return l * sum(both) + sum(both[:k])

            def scores(l, k):
                br, t, heads = STEPS[k]
                n = (t + 1) * P
                if k == 0:
                    pe.wait_ge(s_qkc, QKT_BANKS * (l + 1))
                if k >= 2:
                    pe.wait_ge(s_sm, NSTEP * l + k - 1)
                places = [(j, *head_place(br, h)[:4]) for j, h in enumerate(heads)]
                for n_issued, (j, qb, qh, kb, kh) in enumerate(sorted(places, key=lambda p: p[2])):
                    if n_issued and qh != half:
                        last.then_inc(s_half, 1)
                        pe.wait_ge(s_half, halves_before(l, k) + 1)
                    half = qh
                    last = pe.matmul(bank[4 + k % 2][:, j * n:(j + 1) * n], qkT[qh * DH:(qh + 1) * DH, qb, t * P:(t + 1) * P],
                                     qkT[kh * DH:(kh + 1) * DH, kb, 0:n], start=True, stop=True)
                last.then_inc(s_sc, 1)

            def prob_transpose(l, k):
                _, t, heads = STEPS[k]
                pe.wait_ge(s_p, NSTEP * l + k + 1)
                if k:
                    pe.wait_ge(s_ptc, NSTEP * l + k)
                for b in range(len(heads) * (t + 1)):
                    last = pe.transpose(bank[6][:, b * P:(b + 1) * P], score[:, k % 2, b * P:(b + 1) * P], ident[:])
                last.then_inc(s_pt, 1)

            def weigh_values(l, k):
                br, t, heads = STEPS[k]
                pe.wait_ge(s_ptc, NSTEP * l + k + 1)
                if k:
                    pe.wait_ge(s_o, NSTEP * l + k)
                for j, h in enumerate(heads):
                    v = head_place(br, h)[4]
                    for kb in range(t + 1):
                        b = j * (t + 1) + kb
                        last = pe.matmul(bank[7][:, j * DH:(j + 1) * DH], probT[:, b * P:(b + 1) * P],
                                         val[:, kb, v:v + DH], start=kb == 0, stop=kb == t)
                last.then_inc(s_pv, 1)

            def attention_round(l, r):
                if r < NSTEP:
                    scores(l, r)
                if 0 <= r - 1 < NSTEP:
                    prob_transpose(l, r - 1)
                if 0 <= r - 2 < NSTEP:
                    weigh_values(l, r - 2)

            def mixer(l):
                u = unit0(l)
                transpose_act(4 * l, h_tok, [(s_h, 4 * l + 2)] + ([(s_const, 80)] if l == 0 else []))
                for j in range(2 * IN_CG):
                    cg = j // 2
                    if j % 2 == 0 and cg >= 2:
                        pe.wait_ge(s_evac, 2 * IN_CG * l + 2 * (cg - 2) + 2)
                    square(u + j, j % 2, [bank[(2 * cg + t) % 4] for t in range(TB)], u + j + 1)
                    if j in QKT_SLOT:
                        for b in range(*QKT_SLOT[j]):
                            qk_bank(l, b)
                    if j >= ATT_SLOT:
                        for r in (2 * (j - ATT_SLOT), 2 * (j - ATT_SLOT) + 1):
                            attention_round(l, r)
                transpose_act(4 * l + 1, o_tok, [(s_o, NSTEP * (l + 1)), (s_evac, 2 * IN_CG * (l + 1))])
                bounds = (0, 3, 5, 8)
                for j in range(4):
                    ch, kh = j // 2, j % 2
                    pe.wait_ge(s_lo, u + U_BR + j + 1)
                    for t in range(TB):
                        if ch and kh == 0:
                            pe.wait_ge(s_mg, 4 * l + 1 + t)
                        for kt in range(4 * kh, 4 * kh + 4):
                            br = next(b for b in range(3) if kt < bounds[b + 1])
                            if ch and kt == 5 and t == 0:
                                pe.wait_ge(s_mg, 4 * l + 2)
                            last = product(bank[(6 * ch + 3 * t + br) % 8][:], t_hi[:, kt, t * P:(t + 1) * P],
                                           t_lo[:, kt, t * P:(t + 1) * P], *tile(u + U_BR + j, kt % 4),
                                           kt == bounds[br], kt == bounds[br + 1] - 1)
                    last.then_inc(s_used, 1)
                transpose_act(4 * l + 2, gates, [(s_mg, 4 * l + 4)])
                for j in range(4):
                    square(u + U_OUT + j, j % 2, [bank[2 * (j // 2) + t] for t in range(TB)], u + U_OUT + j + 1)

            def gate_up(u, kh, par, tbs, l_hi, l_lo, ready):
                pe.wait_ge(s_lo, ready)
                for t in range(tbs):
                    for k in range(4):
                        kt = 4 * kh + k
                        last = product(bank[2 * par + t if tbs > 1 else par][:], l_hi[:, kt, t * P:(t + 1) * P],
                                       l_lo[:, kt, t * P:(t + 1) * P], *tile(u, k), kt == 0, kt == KT - 1)
                last.then_inc(s_used, 1)

            def act_transpose(par, tbs, ready):
                pe.wait_ge(s_act, ready)
                for f in range(2):
                    for t in range(tbs):
                        last = pe.transpose(bank[2 * par if tbs > 1 else par][:, (tbs * f + t) * P:(tbs * f + t + 1) * P],
                                            act_tok[:, par, t, f * P:(f + 1) * P], ident[:])
                last.then_inc(s_at, 1)

            def down(u, par, tbs, acc, ready_a, ready, first, last_group):
                pe.wait_ge(s_atl, ready_a)
                pe.wait_ge(s_lo, ready)
                for t in range(tbs):
                    for ch in range(2):
                        for f in range(2):
                            a = (tbs * f + t) * P
                            last = product(acc(t, ch)[:], aT_hi[:, par, a:a + P], aT_lo[:, par, a:a + P],
                                           *tile(u, 2 * f + ch), first and f == 0, last_group and f == 1)
                last.then_inc(s_used, 1)

            def group(u, uval, par, tbs, acc, l_hi, l_lo, done, k, first):
                gate_up(u, 0, par, tbs, l_hi, l_lo, uval + 1)
                if k:
                    act_transpose(1 - par, tbs, done)
                gate_up(u + 1, 1, par, tbs, l_hi, l_lo, uval + 2)
                if k:
                    down(u + 2, 1 - par, tbs, acc, done, uval + 3, first, False)

            mixer(0)
            transpose_act(3, h_tok, [(s_h, 4)])

            def acc2(t, ch):
                return bank[4 + 2 * t + ch]

            n = MIX_UNITS
            for g in range(3):
                group(n, n, g % 2, TB, acc2, t_hi, t_lo, g, g, g == 1)
                n += 3 if g else 2
            with pe.Fori(0, (DENSE_G - 3) // 2) as pair:
                for q in range(2):
                    group(n + 3 * q, pair * RAW + (n + 3 * q), (3 + q) % 2, TB, acc2, t_hi, t_lo, pair * 2 + (3 + q), 1, False)
            n += 3 * (DENSE_G - 3)
            act_transpose((DENSE_G - 1) % 2, TB, DENSE_G)
            down(n, (DENSE_G - 1) % 2, TB, acc2, DENSE_G, n + 1, False, True)

            mixer(1)
            transpose_act(7, h_tok, [(s_h, 8)])
            pe.wait_ge(s_rw, 2)
            for t in range(TB):
                for kt in range(KT):
                    last = product(bank[0][:, t * N_EXP:(t + 1) * N_EXP], t_hi[:, kt, t * P:(t + 1) * P],
                                   t_lo[:, kt, t * P:(t + 1) * P], router_hi[:, kt, :], router_lo[:, kt, :],
                                   kt == 0, kt == KT - 1)
            last.then_inc(s_log, 1)
            pe.wait_ge(s_sel, 1)
            pe.wait_ge(s_route, 16)
            E = N_EXP
            pe.matmul(bank[1][:, 0:E], c_before, r_sel[:, 0, :], start=True, stop=True)
            pe.matmul(bank[1][:, E:2 * E], c_ones, r_sel[:, 0, :], start=True, stop=False)
            pe.matmul(bank[1][:, E:2 * E], c_before, r_sel[:, 1, :], start=False, stop=True)
            pe.matmul(bank[1][:, 2 * E:3 * E], c_ones, r_sel[:, 0, :], start=True, stop=False)
            pe.matmul(bank[1][:, 2 * E:3 * E], c_ones, r_sel[:, 1, :], start=False, stop=True).then_inc(s_rank, 1)
            pe.wait_ge(s_htl, 1)

            def acc1(t, ch):
                return bank[2 + ch]

            def item(i):
                base = MOE_U0
                pe.wait_ge(s_pick, i + 1)
                pe.wait_ge(s_xs, xs_before_item(i))
                for b in range(2):
                    for j in range(4):
                        d = 4 * b + j
                        to = bank[4 + b][:, j * P:(j + 1) * P]
                        for t in range(TB):
                            pe.matmul(to, htok_hi[:, t, d * P:(d + 1) * P], pick[:, t, :], start=t == 0, stop=False)
                            last = pe.matmul(to, htok_lo[:, t, d * P:(d + 1) * P], pick[:, t, :], start=False, stop=t == 1)
                    last.then_inc(s_ga, 1)
                for t in range(TB):
                    last = pe.transpose(bank[6][:, t * P:(t + 1) * P], pick_w[:, t, :], ident[:])
                last.then_inc(s_bk, 1)
                pe.wait_ge(s_gal, i * 2 + 2)
                group(base, moe_unit(i, 0), 0, 1, acc1, xg_hi, xg_lo, ff0(i), 0, False)
                group(base + 2, moe_unit(i, 2), 1, 1, acc1, xg_hi, xg_lo, ff0(i) + 1, 1, True)
                with pe.Fori(0, EXPERT_G // 2 - 1) as pair:
                    for q in range(2):
                        group(base + 5 + 3 * q, pair * RAW + moe_unit(i, 5 + 3 * q), q, 1, acc1, xg_hi, xg_lo,
                              pair * 2 + (ff0(i) + (2 + q)), 1, False)
                act_transpose(1, 1, ff0(i + 1))
                down(base + ITEM_UNITS - 1, 1, 1, acc1, ff0(i + 1), moe_unit(i, ITEM_UNITS), False, True)
                pe.wait_ge(s_yl, i * 2 + 2)
                pe.wait_ge(s_bkl, i + 1)
                for t in range(TB):
                    for ch in range(2):
                        product(bank[4 + 2 * t + ch][:], back_hi[:, t * P:(t + 1) * P], back_lo[:, t * P:(t + 1) * P],
                                y_hi[:, ch * COL:(ch + 1) * COL], y_lo[:, ch * COL:(ch + 1) * COL],
                                True, True).then_inc(s_cmb, 1)

            with pe.Fori(0, N_EXP) as i:
                item(i)
            pe.wait_ge(s_meta, 1)
            items = pe.value_load(meta[0:1, 0:1], min_val=N_EXP, max_val=ITEMS)
            with pe.If(items > N_EXP):
                with pe.Fori(N_EXP, items) as i:
                    item(i)

        @block.scalar
        def _(act):
            def split(u, turns, used):
                act.wait_ge(s_raw[u % RAW], turns)
                if used is not None:
                    act.wait_ge(s_used, used)
                act.copy(w_hi[:, u % SPLIT, :], raw_ring[:, u % RAW, :]).then_inc(s_hi, 1)

            def static(u):
                if u < MOE_U0:
                    split(u, 32 * raw_turn(u), u - SPLIT + 1 if u >= SPLIT else None)

            def norm(n, xs_value):
                if n == 0:
                    act.wait_ge(s_x, 16)
                else:
                    act.wait_ge(s_xs, xs_value)
                for t in range(TB):
                    act.activation(h_tok[:, t, :], xs[:, t, :], ACT.Square, accum_out=ssq[:, t:t + 1]).then_inc(s_ssq, 1)
                act.wait_ge(s_var, n + 1)
                act.activation(std[:], var[:], ACT.Sqrt).then_inc(s_std, 1)

            def round_transposed(call):
                for b in range(4):
                    act.wait_ge(s_tr, 4 * call + b + 1)
                    act.copy(t_hi[:, 2 * b:2 * b + 2, :].rearrange("p k t -> p (k t)"), bank[4 + b][:]).then_inc(s_trh, 1)

            def project_copy(l, cg, used):
                act.wait_ge(s_used, used)
                for t in range(TB):
                    src = bank[(2 * cg + t) % 4]
                    if cg < QKV_CG:
                        for a, what, to, n in in_pieces(cg):
                            dst, src_a = (qk if what == "qk" else val)[:, t, to:to + n], src[:, a:a + n]
                            if cg == 0:
                                nq = HEADS["A"] * DH
                                act.copy(dst[:, 0:nq].rearrange("p (i s c) -> p s i c", s=2, c=DH),
                                         src_a[:, 0:nq].rearrange("p (s i c) -> p s i c", s=2, c=DH))
                                dst, src_a = dst[:, nq:n], src_a[:, nq:n]
                            last = act.copy(dst, src_a)
                    else:
                        if cg == IN_CG - 1 and t == 1:
                            act.wait_ge(s_rope, 3 * l + 3)
                        a = (cg - QKV_CG) * COL
                        last = act.copy(gates[:, t, a:a + COL], src[:])
                    last.then_inc(s_evac, 1)

            def qk_copy(l, b):
                act.wait_ge(s_qkt, QKT_BANKS * l + b + 1)
                act.copy(qkT[:, 2 * b:2 * b + 2, :].rearrange("p k t -> p (k t)"), bank[4 + b % 4][:]).then_inc(s_qkc, 1)

            def exponentials(l, k):
                br, t, heads = STEPS[k]
                n = (t + 1) * P
                act.wait_ge(s_nm, NSTEP * l + k + 1)
                for j in range(len(heads)):
                    s = score[:, k % 2, j * n:(j + 1) * n]
                    last = act.activation(s, s, ACT.Exp, bias=nmx[:, k % 2, j:j + 1], accum_out=den[:, k % 2, j:j + 1])
                if br == "A":
                    nh = len(heads)
                    last = act.activation(sink_e[:, k % 2, 0:nh], sink_d[:, k % 2, 0:nh], ACT.Exp)
                last.then_inc(s_p, 1)

            def prob_copy(l, k):
                _, t, heads = STEPS[k]
                n = len(heads) * (t + 1) * P
                act.wait_ge(s_pt, NSTEP * l + k + 1)
                if k:
                    act.wait_ge(s_pv, NSTEP * l + k)
                act.copy(probT[:, 0:n], bank[6][:, 0:n]).then_inc(s_ptc, 1)

            def mixer(l):
                u = unit0(l)
                norm(2 * l, xs_before(2 * l))
                round_transposed(4 * l)
                for j in range(2 * IN_CG):
                    if j % 2 == 1:
                        project_copy(l, j // 2, u + j + 1)
                    if j in QKT_SLOT:
                        for b in range(*QKT_SLOT[j]):
                            qk_copy(l, b)
                    if j >= ATT_SLOT:
                        for r in (2 * (j - ATT_SLOT), 2 * (j - ATT_SLOT) + 1):
                            if r < NSTEP:
                                exponentials(l, r)
                            if 0 <= r - 1 < NSTEP:
                                prob_copy(l, r - 1)
                    static(u + j + SPLIT)
                round_transposed(4 * l + 1)
                for ch in range(2):
                    for t in range(TB):
                        g = gates[:, t, :].rearrange("p (b c) -> p b c", b=3)[:, :, ch * COL:(ch + 1) * COL]
                        act.activation(g, g, ACT.Sigmoid).then_inc(s_gate, 1)
                for j in range(U_BR, U_OUT):
                    static(u + j + SPLIT)
                round_transposed(4 * l + 2)
                for j in range(U_OUT, MIX_UNITS):
                    static(u + j + SPLIT)

            def silu(par, tbs, used):
                act.wait_ge(s_used, used)
                for t in range(tbs):
                    last = act.activation(sil[:, par, t, :], bank[2 * par + t if tbs > 1 else par][:, 0:FG], ACT.Silu)
                last.then_inc(s_sil, 1)

            def round_act(par, tbs, ready):
                n = 2 * tbs * P
                act.wait_ge(s_at, ready)
                act.copy(aT_hi[:, par, 0:n], bank[2 * par if tbs > 1 else par][:, 0:n]).then_inc(s_ath, 1)

            def turn(split_at, k, par, tbs, uval, done, last=False):
                if k:
                    round_act(1 - par, tbs, done)
                split_at(3)
                silu(par, tbs, uval + 2)
                if not last:
                    split_at(4)
                    if k:
                        split_at(5)

            for u in range(SPLIT):
                static(u)
            act.wait_ge(s_const, 80)
            act.copy(router_hi[:], router[:]).then_inc(s_rw, 1)
            mixer(0)
            norm(1, xs_before(1))
            round_transposed(3)
            n = MIX_UNITS
            for g in range(3):
                turn(lambda j: static(n + j), g, g % 2, TB, n, g)
                n += 3 if g else 2
            with act.Fori(0, (DENSE_G - 3) // 2) as pair:
                for q in range(2):
                    v = n + 3 * q
                    turn(lambda j: split(v + j, pair * 32 + 32 * raw_turn(v + j), pair * RAW + (v + j - SPLIT + 1)),
                         1, (3 + q) % 2, TB, pair * RAW + v, pair * 2 + (3 + q))
            n += 3 * (DENSE_G - 3)
            round_act((DENSE_G - 1) % 2, TB, DENSE_G)
            static(n + SPLIT)
            mixer(1)
            norm(3, xs_before(3))
            round_transposed(7)
            act.wait_ge(s_log, 1)
            act.copy(htok_hi, h_tok).then_inc(s_hth, 1)
            act.wait_ge(s_rexpin, 1)
            act.activation(r_e, r_c, ACT.Exp).then_inc(s_rexp, 1)

            def item(i):
                def split_at(j, pair=None):
                    turns, used = moe_turn(i, j) * 32, moe_unit(i, j - SPLIT + 1)
                    if pair is not None:
                        turns, used = pair * 32 + turns, pair * RAW + used
                    split(MOE_U0 + j, turns, used)

                for j in range(SPLIT):
                    split_at(j)
                for b in range(2):
                    act.wait_ge(s_ga, i * 2 + (b + 1))
                    act.copy(xg_hi[:, 4 * b:4 * b + 4, :].rearrange("p k t -> p (k t)"), bank[4 + b][:]).then_inc(s_gah, 1)
                act.wait_ge(s_bk, i + 1)
                act.copy(back_hi[:], bank[6][:, 0:T]).then_inc(s_bkh, 1)
                turn(split_at, 0, 0, 1, moe_unit(i, 0), ff0(i))
                turn(lambda j: split_at(2 + j), 1, 1, 1, moe_unit(i, 2), ff0(i) + 1)
                with act.Fori(0, EXPERT_G // 2 - 2) as pair:
                    for q in range(2):
                        v = 5 + 3 * q
                        turn(lambda j: split_at(v + j, pair), 1, q, 1, pair * RAW + moe_unit(i, v), pair * 2 + (ff0(i) + (2 + q)))
                for q in range(2):
                    v = ITEM_UNITS - 7 + 3 * q
                    turn(lambda j: split_at(v + j), 1, q, 1, moe_unit(i, v), ff0(i) + (EXPERT_G - 2 + q), last=q == 1)
                round_act(1, 1, ff0(i + 1))
                act.wait_ge(s_used, moe_unit(i, ITEM_UNITS))
                for ch in range(2):
                    act.copy(y_hi[:, ch * COL:(ch + 1) * COL], bank[2 + ch][:]).then_inc(s_yh, 1)

            with act.Fori(0, N_EXP) as i:
                item(i)
            act.wait_ge(s_meta, 1)
            items = act.value_load(meta[0:1, 0:1], min_val=N_EXP, max_val=ITEMS)
            with act.If(items > N_EXP):
                with act.Fori(N_EXP, items) as i:
                    item(i)
            norm(4, xs_before_item(items))

        @block.vector
        def _(dve):
            steps = [0]

            def link(ins):
                steps[0] += 1
                ins.then_inc(s_dve, 1)
                dve.wait_ge(s_dve, steps[0])

            def each(a, n):
                return a.rearrange("p (k o) -> p k o", o=1).broadcast_to([P, a.shape[1], n])

            def over(a, n):
                return a.rearrange("p (o k) -> p o k", o=1).broadcast_to([P, n, a.shape[1]])

            def split(u, rounded):
                dve.wait_ge(s_hi, rounded)
                s = u % SPLIT
                dve.tensor_tensor(w_lo[:, s, :], raw_ring[:, u % RAW, :], w_hi[:, s, :].bitcast(F32),
                                  ALU.subtract).then_inc(s_lo, 1)

            def static(u):
                if u < MOE_U0:
                    split(u, u + 1)

            def norm(n):
                dve.wait_ge(s_ssq, 2 * n + 2)
                dve.tensor_scalar(var[:], ssq[:], 1.0 / D, EPS, ALU.mult, ALU.add).then_inc(s_var, 1)
                dve.wait_ge(s_std, n + 1)
                link(dve.reciprocal(rstd[:], std[:]))
                dve.wait_ge(s_gain, 16 * (n + 1))
                for t in range(TB):
                    dve.scalar_tensor_tensor(out=h_tok[:, t, :], in0=xs[:, t, :], scalar=rstd[:, t:t + 1], in1=gain[:],
                                             op0=ALU.mult, op1=ALU.mult).then_inc(s_h, 1)

            def split_transposed(call):
                for b in range(4):
                    dve.wait_ge(s_trh, 4 * call + b + 1)
                    to = slice(2 * b, 2 * b + 2)
                    dve.tensor_tensor(t_lo[:, to, :].rearrange("p k t -> p (k t)"), bank[4 + b][:],
                                      t_hi[:, to, :].bitcast(F32).rearrange("p k t -> p (k t)"),
                                      ALU.subtract).then_inc(s_trl, 1)

            def apply_rope(l, br):
                end = IN_AT[br] + (HEADS[br] + KV[br]) * DH
                dve.wait_ge(s_evac, 2 * IN_CG * l + 2 * -(-end // COL))
                heads = HEADS[br] + KV[br]
                n = 8 if heads == 8 else heads // 2
                half = DH // 2
                for t in range(TB):
                    for a in range(QK_AT[br], QK_AT[br] + heads * DH, n * DH):
                        z = qk[:, t, a:a + n * DH].rearrange("p (n c) -> p n c", n=n)
                        tmp = rope_tmp[:, 0:n * DH].rearrange("p (n c) -> p n c", n=n)
                        cos, sin = rope[:, t, 0, :], rope[:, t, 1, :]
                        dve.tensor_tensor(tmp[:, :, 0:half], z[:, :, half:DH], over(sin[:, 0:half], n), ALU.mult)
                        link(dve.tensor_tensor(tmp[:, :, half:DH], z[:, :, 0:half], over(sin[:, half:DH], n), ALU.mult))
                        link(dve.tensor_tensor(z, z, over(cos, n), ALU.mult))
                        link(dve.tensor_tensor(z, z, tmp, ALU.add))
                dve.sem_inc(s_rope, 1)

            def mask_and_max(l, k):
                br, t, heads = STEPS[k]
                nh, n, b = len(heads), (t + 1) * P, k % 2
                dve.wait_ge(s_sc, NSTEP * l + k + 1)
                if k >= 2:
                    dve.wait_ge(s_pt, NSTEP * l + k - 1)
                s = score[:, b, 0:nh * n].rearrange("p (h c) -> p h c", h=nh)
                raw = bank[4 + b][:, 0:nh * n].rearrange("p (h c) -> p h c", h=nh)
                dve.scalar_tensor_tensor(out=s, in0=raw, scalar=SCALE, in1=over(mask[:, "ABC".index(br), T - n:T], nh),
                                         op0=ALU.mult, op1=ALU.add).then_inc(s_sm, 1)
                dve.wait_ge(s_sm, NSTEP * l + k + 1)
                link(dve.tensor_reduce(mx[:, b, 0:nh], s, AX, ALU.max))
                if br == "A":
                    sk = sinks[:, l, heads[0]:heads[0] + nh]
                    link(dve.tensor_tensor(mx[:, b, 0:nh], mx[:, b, 0:nh], sk, ALU.max))
                    dve.tensor_tensor(sink_d[:, b, 0:nh], sk, mx[:, b, 0:nh], ALU.subtract)
                dve.tensor_scalar(nmx[:, b, 0:nh], mx[:, b, 0:nh], -1.0, None, ALU.mult).then_inc(s_nm, 1)

            def reciprocals(l, k):
                br, t, heads = STEPS[k]
                nh, b = len(heads), k % 2
                dve.wait_ge(s_p, NSTEP * l + k + 1)
                if k >= 2:
                    dve.wait_ge(s_o, NSTEP * l + k - 1)
                if br == "A":
                    link(dve.tensor_tensor(den[:, b, 0:nh], den[:, b, 0:nh], sink_e[:, b, 0:nh], ALU.add))
                link(dve.reciprocal(rden[:, b, 0:nh], den[:, b, 0:nh]))

            def outputs(l, k):
                br, t, heads = STEPS[k]
                nh, b = len(heads), k % 2
                dve.wait_ge(s_pv, NSTEP * l + k + 1)
                a = O_AT[br] + heads[0] * DH
                dve.tensor_tensor(o_tok[:, t, a:a + nh * DH].rearrange("p (h c) -> p h c", h=nh),
                                  bank[7][:, 0:nh * DH].rearrange("p (h c) -> p h c", h=nh),
                                  each(rden[:, b, 0:nh], DH), ALU.mult).then_inc(s_o, 1)

            def merge(l, ch, t):
                dve.wait_ge(s_gate, 4 * l + 2 * ch + t + 1)
                g = [gates[:, t, b * D + ch * COL:b * D + (ch + 1) * COL] for b in range(3)]
                for b in range(3):
                    last = dve.tensor_tensor(g[b], g[b], bank[(6 * ch + 3 * t + b) % 8][:], ALU.mult)
                link(last)
                link(dve.tensor_tensor(g[0], g[0], g[1], ALU.add))
                dve.tensor_tensor(g[0], g[0], g[2], ALU.add).then_inc(s_mg, 1)

            def add_to_stream(t, ch, src):
                a = xs[:, t, ch * COL:(ch + 1) * COL]
                dve.tensor_tensor(a, a, src[:], ALU.add).then_inc(s_xs, 1)

            def mixer(l):
                u = unit0(l)
                norm(2 * l)
                split_transposed(4 * l)
                for j in range(2 * IN_CG):
                    if j in ROPE_SLOT:
                        apply_rope(l, ROPE_SLOT[j])
                    if j >= ATT_SLOT:
                        for r in (2 * (j - ATT_SLOT), 2 * (j - ATT_SLOT) + 1):
                            if r < NSTEP:
                                mask_and_max(l, r)
                            if 0 <= r - 1 < NSTEP:
                                reciprocals(l, r - 1)
                            if 0 <= r - 2 < NSTEP:
                                outputs(l, r - 2)
                    static(u + j + SPLIT)
                split_transposed(4 * l + 1)
                for j in range(U_BR, U_OUT):
                    static(u + j + SPLIT)
                    if (j - U_BR) % 2:
                        dve.wait_ge(s_used, u + j + 1)
                        for t in range(TB):
                            merge(l, (j - U_BR) // 2, t)
                split_transposed(4 * l + 2)
                for j in range(U_OUT, MIX_UNITS):
                    static(u + j + SPLIT)
                    if (j - U_OUT) % 2:
                        dve.wait_ge(s_used, u + j + 1)
                        for t in range(TB):
                            add_to_stream(t, (j - U_OUT) // 2, bank[2 * ((j - U_OUT) // 2) + t])

            def times_up(par, tbs, done):
                dve.wait_ge(s_sil, done)
                for t in range(tbs):
                    last = dve.tensor_tensor(act_tok[:, par, t, :], sil[:, par, t, :],
                                             bank[2 * par + t if tbs > 1 else par][:, FG:2 * FG], ALU.mult)
                last.then_inc(s_act, 1)

            def split_act(par, tbs, ready):
                n = 2 * tbs * P
                dve.wait_ge(s_ath, ready)
                dve.tensor_tensor(aT_lo[:, par, 0:n], bank[2 * par if tbs > 1 else par][:, 0:n],
                                  aT_hi[:, par, 0:n].bitcast(F32), ALU.subtract).then_inc(s_atl, 1)

            def turn(split_at, k, par, tbs, done, last=False):
                if k:
                    split_act(1 - par, tbs, done)
                split_at(3)
                times_up(par, tbs, done + 1)
                if not last:
                    split_at(4)
                    if k:
                        split_at(5)

            for u in range(SPLIT):
                static(u)
            dve.wait_ge(s_rw, 1)
            dve.tensor_tensor(router_lo[:], router[:], router_hi[:].bitcast(F32), ALU.subtract).then_inc(s_rw, 1)
            mixer(0)
            norm(1)
            split_transposed(3)
            n = MIX_UNITS
            for g in range(3):
                turn(lambda j: static(n + j), g, g % 2, TB, g)
                n += 3 if g else 2
            with dve.Fori(0, (DENSE_G - 3) // 2) as pair:
                for q in range(2):
                    v = n + 3 * q
                    turn(lambda j: split(v + j, pair * RAW + (v + j + 1)), 1, (3 + q) % 2, TB, pair * 2 + (3 + q))
            n += 3 * (DENSE_G - 3)
            split_act((DENSE_G - 1) % 2, TB, DENSE_G)
            static(n + SPLIT)
            dve.wait_ge(s_used, n + 1)
            for t in range(TB):
                for ch in range(2):
                    add_to_stream(t, ch, bank[4 + 2 * t + ch])
            mixer(1)
            norm(3)
            split_transposed(7)

            E = N_EXP
            dve.wait_ge(s_log, 1)
            dve.wait_ge(s_route, 16)
            link(dve.tensor_copy(r_log.rearrange("p t e -> p (t e)"), bank[0][:, 0:TB * E]))
            for src, top, chosen in ((r_log, r_m1, r_first), (r_l2, r_m2, r_second)):
                link(dve.tensor_reduce(top, src, AX, ALU.max))
                link(dve.tensor_tensor(r_eq, src, each(top, E), ALU.is_equal))
                link(dve.tensor_tensor(r_t, r_eq, over(c_desc, TB), ALU.mult))
                link(dve.tensor_reduce(r_den, r_t, AX, ALU.max))
                link(dve.tensor_tensor(chosen, r_t, each(r_den, E), ALU.is_equal))
                if src is r_log:
                    link(dve.scalar_tensor_tensor(out=r_l2, in0=r_first, scalar=-3e38, in1=r_log, op0=ALU.mult, op1=ALU.add))
            dve.tensor_tensor(r_sel, r_first, r_second, ALU.add).then_inc(s_sel, 1)
            dve.tensor_tensor(r_c, r_m2, r_m1, ALU.subtract).then_inc(s_rexpin, 1)
            dve.wait_ge(s_rexp, 1)
            link(dve.tensor_scalar(r_den, r_e, 1.0, None, ALU.add))
            link(dve.reciprocal(r_w1, r_den))
            link(dve.tensor_tensor(r_w2, r_e, r_w1, ALU.mult))
            dve.tensor_tensor(r_first, r_first, each(r_w1, E), ALU.mult)
            link(dve.tensor_tensor(r_second, r_second, each(r_w2, E), ALU.mult))
            link(dve.tensor_tensor(r_w, r_first, r_second, ALU.add))
            dve.wait_ge(s_rank, 1)
            rank = bank[1][:, 0:TB * E].rearrange("p (t e) -> p t e", t=TB)
            link(dve.scalar_tensor_tensor(out=r_t, in0=rank, scalar=1.0, in1=r_sel, op0=ALU.add, op1=ALU.mult))
            dve.tensor_scalar(item_slot[:, :, 0:E], r_t, -1.0, None, ALU.add)
            dve.tensor_scalar(r_slot, r_t, -1.0 - P, None, ALU.add)
            dve.tensor_copy(item_w[:, :, 0:E], r_w)
            link(dve.tensor_scalar(r_over, bank[1][:, 2 * E:3 * E], float(P), None, ALU.is_gt))
            link(dve.tensor_tensor_scan(r_cum, c_ones[:, 0:E], r_over, 0.0, ALU.mult, ALU.add))
            dve.tensor_scalar(r_meta[:, 0:1], r_cum[:, E - 1:E], float(E), None, ALU.add)
            for j in range(OVER):
                link(dve.scalar_tensor_tensor(out=r_hot, in0=r_cum, scalar=float(j + 1), in1=r_over,
                                              op0=ALU.is_equal, op1=ALU.mult))
                for src, to in ((r_slot, item_slot), (r_w, item_w)):
                    link(dve.tensor_tensor(r_t, src, over(r_hot, TB), ALU.mult))
                    link(dve.tensor_reduce(to[:, :, E + j], r_t, AX, ALU.add))
                link(dve.tensor_tensor(r_hot, r_hot, c_expert, ALU.mult))
                link(dve.tensor_reduce(r_meta[:, 1 + j:2 + j], r_hot, AX, ALU.add))
            dve.tensor_copy(meta[:], r_meta[0:1, :]).then_inc(s_meta, 1)
            dve.wait_ge(s_hth, 1)
            dve.tensor_tensor(htok_lo, h_tok, htok_hi.bitcast(F32), ALU.subtract).then_inc(s_htl, 1)
            dve.wait_ge(s_htl, 1)

            def item(i):
                def split_at(j, pair=None):
                    rounded = moe_unit(i, j + 1)
                    split(MOE_U0 + j, rounded if pair is None else pair * RAW + rounded)

                for t in range(TB):
                    slot, w = item_slot[:, t, bass.ds(i, 1)], item_w[:, t, bass.ds(i, 1)]
                    dve.tensor_scalar(pick[:, t, :], c_slot, slot, None, ALU.is_equal)
                    last = dve.tensor_scalar(pick_w[:, t, :], c_slot, slot, w, ALU.is_equal, ALU.mult)
                last.then_inc(s_pick, 1)
                for j in range(SPLIT):
                    split_at(j)
                for b in range(2):
                    dve.wait_ge(s_gah, i * 2 + (b + 1))
                    to = slice(4 * b, 4 * b + 4)
                    dve.tensor_tensor(xg_lo[:, to, :].rearrange("p k t -> p (k t)"), bank[4 + b][:],
                                      xg_hi[:, to, :].bitcast(F32).rearrange("p k t -> p (k t)"),
                                      ALU.subtract).then_inc(s_gal, 1)
                dve.wait_ge(s_bkh, i + 1)
                dve.tensor_tensor(back_lo[:], bank[6][:, 0:T], back_hi[:].bitcast(F32), ALU.subtract).then_inc(s_bkl, 1)
                turn(split_at, 0, 0, 1, ff0(i))
                turn(lambda j: split_at(2 + j), 1, 1, 1, ff0(i) + 1)
                with dve.Fori(0, EXPERT_G // 2 - 2) as pair:
                    for q in range(2):
                        v = 5 + 3 * q
                        turn(lambda j: split_at(v + j, pair), 1, q, 1, pair * 2 + (ff0(i) + (2 + q)))
                for q in range(2):
                    v = ITEM_UNITS - 7 + 3 * q
                    turn(lambda j: split_at(v + j), 1, q, 1, ff0(i) + (EXPERT_G - 2 + q), last=q == 1)
                split_act(1, 1, ff0(i + 1))
                for ch in range(2):
                    dve.wait_ge(s_yh, i * 2 + (ch + 1))
                    a = slice(ch * COL, (ch + 1) * COL)
                    dve.tensor_tensor(y_lo[:, a], bank[2 + ch][:], y_hi[:, a].bitcast(F32), ALU.subtract).then_inc(s_yl, 1)
                for t in range(TB):
                    for ch in range(2):
                        dve.wait_ge(s_cmb, i * 4 + (2 * t + ch + 1))
                        add_to_stream(t, ch, bank[4 + 2 * t + ch])

            with dve.Fori(0, N_EXP) as i:
                item(i)
            dve.wait_ge(s_meta, 1)
            items = dve.value_load(meta[0:1, 0:1], min_val=N_EXP, max_val=ITEMS)
            with dve.If(items > N_EXP):
                with dve.Fori(N_EXP, items) as i:
                    item(i)
            norm(4)


def _constants():
    i, j = np.arange(P)[:, None] + P, np.arange(T)[None, :]
    gap = i - j
    inside = {
        "A": ((gap >= 0) & (gap <= 127)).astype(np.float64),
        "B": (gap >= 0).astype(np.float64),
        "C": ((gap >= 0) & (gap <= 128)).astype(np.float64) + ((gap >= 0) & (gap % 4 == 0)) + ((gap >= 0) & (gap % 16 == 0)),
    }
    masks = np.stack([np.where(m > 0, np.log(np.maximum(m, 1.0)), NEG) for m in inside.values()], axis=1)
    pos = np.arange(T, dtype=np.float32)
    inv = np.float32(10000.0) ** (-np.arange(0, DH, 2, dtype=np.float32) / np.float32(DH))
    ang = pos[:, None] * inv[None, :]
    cos, sin = np.cos(ang), np.sin(ang)
    tables = np.stack([np.concatenate([cos, cos], 1), np.concatenate([-sin, sin], 1)], axis=1)
    tables = tables.reshape(TB, P, 2, DH).transpose(1, 0, 2, 3)
    k = np.arange(P)
    before = (k[:, None] < k[None, :])
    e = np.arange(N_EXP)
    route = np.concatenate([before, np.ones((P, P)), np.tile(k, (P, 1)), np.tile(N_EXP - e, (P, 1)), np.tile(e, (P, 1))], axis=1)
    f = np.float32
    return (np.eye(P, dtype=f), np.ascontiguousarray(masks.astype(f)), np.ascontiguousarray(tables.astype(f)),
            np.ascontiguousarray(route.astype(f)))


def kernel(x, norm_mix, w_in, attn_sinks, w_br_a, w_br_b, w_br_c, w_out, norm_ffn, w_ff_gate, w_ff_up, w_ff_down,
           w_router, w_moe_gate, w_moe_up, w_moe_down, norm_final):
    import concourse.bacc as _bacc
    from concourse.bass_utils import run_bass_kernel_spmd as _run

    ident, masks, tables, route = _constants()
    ins = {
        "x": x, "norm_mix": norm_mix, "w_in": w_in, "attn_sinks": attn_sinks,
        "w_br": np.concatenate([np.asarray(w_br_a), np.asarray(w_br_b), np.asarray(w_br_c)], axis=1),
        "w_out": w_out, "norm_ffn": norm_ffn, "w_ff_gate": w_ff_gate, "w_ff_up": w_ff_up, "w_ff_down": w_ff_down,
        "w_router": w_router, "w_moe_gate": w_moe_gate, "w_moe_up": w_moe_up, "w_moe_down": w_moe_down,
        "norm_final": norm_final, "c_ident": ident, "c_masks": masks, "c_rope": tables, "c_route": route,
    }
    nc = _bacc.Bacc("TRN2", target_bir_lowering=False, num_devices=1)
    arrays, args = {}, []
    for name, a in ins.items():
        a = np.ascontiguousarray(a)
        arrays[f"in_{name}"] = a
        args.append(nc.dram_tensor(f"in_{name}", a.shape, mybir.dt.from_np(a.dtype), kind="ExternalInput").ap())
    args.append(nc.dram_tensor("out_0", (1, T, D), F32, kind="ExternalOutput").ap())
    bass_trunk(nc, *args)
    r = _run(nc, [arrays], core_ids=[0])
    return r.results[0]["out_0"]
```

```python
from contextlib import ExitStack

import numpy as np

import concourse.bass as bass
from concourse import mybir

P = 128
F32 = mybir.dt.float32
F32R = mybir.dt.float32r
I32 = mybir.dt.int32
ALU = mybir.AluOpType
ACT = mybir.ActivationFunctionType
AX = mybir.AxisListType.X

T, D = 256, 1024
TB, KT = T // P, D // P
DEPTH = 2
DH = 64
SCALE = DH ** -0.5
EPS = 1e-5
NEG = -1e30
FF_DENSE, FF_EXPERT, N_EXP = 2816, 3584, 8
COL = 512
FG = 256
UNIT = 4 * COL
RAW, SPLIT = 6, 3

HEADS = {"A": 6, "B": 4, "C": 6}
KV = {"A": 2, "B": 4, "C": 6}
QKV_COLS = sum(HEADS[b] + 2 * KV[b] for b in "ABC") * DH
QK_LEN = sum(HEADS[b] + KV[b] for b in "ABC") * DH
V_LEN = sum(KV[b] for b in "ABC") * DH
QK_AT, V_AT, O_AT, IN_AT = {}, {}, {}, {}
_i = _q = _v = _o = 0
for _b in "ABC":
    IN_AT[_b], QK_AT[_b], V_AT[_b], O_AT[_b] = _i, _q, _v, _o
    _i += (HEADS[_b] + 2 * KV[_b]) * DH
    _q += (HEADS[_b] + KV[_b]) * DH
    _v += KV[_b] * DH
    _o += HEADS[_b] * DH
IN_CG = (QKV_COLS + 3 * D) // COL
QKV_CG = QKV_COLS // COL

U_IN, U_BR, U_OUT = 0, 2 * IN_CG, 2 * IN_CG + 4
MIX_UNITS = U_OUT + 4
DENSE_G, EXPERT_G = FF_DENSE // FG, FF_EXPERT // FG
DENSE_UNITS, ITEM_UNITS = 3 * DENSE_G, 3 * EXPERT_G
MOE_U0 = 2 * MIX_UNITS + DENSE_UNITS
OVER = 3
ITEMS = N_EXP + OVER
TAIL = ITEM_UNITS - 4

QKT_BLOCKS = QK_LEN // (2 * DH)
QKT_BANKS = QKT_BLOCKS // 2

STEPS = [(b, 0, list(range(i, min(i + 4, HEADS[b])))) for b in "ABC" for i in range(0, HEADS[b], 4)]
STEPS += [(b, 1, [i, i + 1]) for b in "ABC" for i in range(0, HEADS[b], 2)]
LAG_PT, LAG_PV = 2, 3
NSTEP = len(STEPS)
QKT_SLOT = {9: (0, 2), 11: (2, 4), 13: (4, 7)}
ATT_SLOT = 14
ROPE_SLOT = {3: "A", 6: "B", 10: "C"}


def head_place(b, h):
    if b == "A":
        return h % 3, h // 3, 3, h // 3, V_AT[b] + (h // 3) * DH
    first = 4 if b == "B" else 8
    return first + h // 2, h % 2, first + HEADS[b] // 2 + h // 2, h % 2, V_AT[b] + h * DH


def in_pieces(cg):
    out = []
    for b in "ABC":
        nqk, nv = (HEADS[b] + KV[b]) * DH, KV[b] * DH
        for a, n, what, to in ((IN_AT[b], nqk, "qk", QK_AT[b]), (IN_AT[b] + nqk, nv, "v", V_AT[b])):
            lo, hi = max(a, cg * COL), min(a + n, (cg + 1) * COL)
            if lo < hi:
                out.append((lo - cg * COL, what, to + lo - a, hi - lo))
    return out


def raw_turn(u):
    return u // RAW + 1


def bass_trunk(nc, x, norm_mix, w_in, attn_sinks, w_br, w_out, norm_ffn, w_ff_gate, w_ff_up, w_ff_down,
               w_router, w_moe_gate, w_moe_up, w_moe_down, norm_final, c_ident, c_masks, c_rope, c_route, out):
    ctx = ExitStack()
    with ctx:
        def sb(name, shape, dt=F32):
            return ctx.enter_context(nc.sbuf_tensor(name, shape, dt))

        def sem(name):
            return ctx.enter_context(nc.semaphore(name))

        bank = [ctx.enter_context(nc.psum_tensor(f"bank{i}", [P, COL], F32)) for i in range(8)]

        raw_ring = sb("raw_ring", [P, RAW, UNIT])
        w_hi = sb("w_hi", [P, SPLIT, UNIT], F32R)
        w_lo = sb("w_lo", [P, SPLIT, UNIT], F32R)
        xs = sb("xs", [P, TB, D])
        t_hi = sb("t_hi", [P, KT, T], F32R)
        t_lo = sb("t_lo", [P, KT, T], F32R)
        gates = sb("gates", [P, TB, 3 * D])
        work = sb("work", [P, TB * QK_LEN])
        val = sb("val", [P, TB, V_LEN])
        qkT = sb("qkT", [P, QKT_BLOCKS, T])
        qk = work[:, :].rearrange("p (t c) -> p t c", t=TB)
        h_tok = work[:, 0:TB * D].rearrange("p (t c) -> p t c", t=TB)
        o_tok = h_tok
        probT = work[:, TB * D + 2 * COL:TB * D + 3 * COL]
        score3 = sb("score3", [P, COL])
        score = [work[:, TB * D:TB * D + COL], work[:, TB * D + COL:TB * D + 2 * COL], score3[:, :]]
        qkT_flat = qkT[:, :, :].rearrange("p k t -> p (k t)")
        gain = qkT_flat[:, 0:D]
        squares = qkT_flat[:, D:3 * D]
        rope_tmp = gates[:, 1, 3 * D - COL:3 * D]
        aT_hi = sb("aT_hi", [P, 2, COL], F32R)
        aT_lo = sb("aT_lo", [P, 2, COL], F32R)
        flat = gates[:, :, :].rearrange("p t c -> p (t c)")
        sil = flat[:, 0:4 * FG].rearrange("p (n t c) -> p n t c", n=2, t=TB)
        act_tok = flat[:, 4 * FG:8 * FG].rearrange("p (n t c) -> p n t c", n=2, t=TB)
        xg_hi = sb("xg_hi", [P, KT, P], F32R)
        xg_lo = sb("xg_lo", [P, KT, P], F32R)
        pick = sb("pick", [P, TB, P], F32R)
        back_hi = sb("back_hi", [P, T], F32R)
        back_lo = sb("back_lo", [P, T], F32R)
        y_hi = aT_hi[:, :, :].rearrange("p n c -> p (n c)")
        y_lo = aT_lo[:, :, :].rearrange("p n c -> p (n c)")
        htok_hi = t_hi[:, :, :].rearrange("p k t -> p (k t)").rearrange("p (t c) -> p t c", t=TB)
        htok_lo = t_lo[:, :, :].rearrange("p k t -> p (k t)").rearrange("p (t c) -> p t c", t=TB)
        pick_w = flat[:, 8 * FG:9 * FG].rearrange("p (t c) -> p t c", t=TB)
        tbl_at = [9 * FG]

        def table(*shape):
            n = int(np.prod(shape))
            a = flat[:, tbl_at[0]:tbl_at[0] + n]
            tbl_at[0] += n
            return a.rearrange("p (t e) -> p t e", t=shape[0]) if len(shape) == 2 else a

        r_log, r_eq, r_l2, r_first, r_second, r_sel, r_w, r_rank, r_slot, r_t = (table(TB, N_EXP) for _ in range(10))
        r_m1, r_m2, r_c, r_e, r_den, r_w1, r_w2 = (table(TB) for _ in range(7))
        r_over, r_cum, r_hot = (table(N_EXP) for _ in range(3))
        r_meta = table(4)
        item_slot, item_w = table(TB, ITEMS), table(TB, ITEMS)
        meta = sb("meta", [1, 4], I32)
        ident = sb("ident", [P, P])
        mask = sb("mask", [P, 3, T])
        rope = sb("rope", [P, TB, 2, DH])
        sinks = sb("sinks", [P, DEPTH, HEADS["A"]])
        router = sb("router", [P, KT, N_EXP])
        router_hi = sb("router_hi", [P, KT, N_EXP], F32R)
        router_lo = sb("router_lo", [P, KT, N_EXP], F32R)
        route = val[:, :, :].rearrange("p t c -> p (t c)")[:, 0:3 * P + 2 * N_EXP]
        c_before, c_ones, c_slot = route[:, 0:P], route[:, P:2 * P], route[:, 2 * P:3 * P]
        c_desc, c_expert = route[:, 3 * P:3 * P + N_EXP], route[:, 3 * P + N_EXP:3 * P + 2 * N_EXP]
        ssq = sb("ssq", [P, 2, TB])
        ssum, var, std, rstd = (sb(n, [P, TB]) for n in ("ssum", "var", "std", "rstd"))
        mx, nmx, den, sink_d, sink_e, rden = (sb(n, [P, 4, 4]) for n in ("mx", "nmx", "den", "sink_d", "sink_e", "rden"))

        s_x = sem("s_x")
        s_ident = sem("s_ident")
        s_const = sem("s_const")
        s_gain0 = sem("s_gain0")
        s_gain = sem("s_gain")
        s_route = sem("s_route")
        s_raw = [sem(f"s_raw{i}") for i in range(RAW)]
        s_hi = sem("s_hi")
        s_lo = sem("s_lo")
        s_used = sem("s_used")
        s_ssq = sem("s_ssq")
        s_var = sem("s_var")
        s_std = sem("s_std")
        s_rstd = sem("s_rstd")
        s_xg = sem("s_xg")
        s_y = sem("s_y")
        s_tr = sem("s_tr")
        s_trh = sem("s_trh")
        s_trl = sem("s_trl")
        s_evac = sem("s_evac")
        s_rope = sem("s_rope")
        s_qkt = sem("s_qkt")
        s_qkc = sem("s_qkc")
        s_sc = sem("s_sc")
        s_half = sem("s_half")
        s_sm = sem("s_sm")
        s_nm = sem("s_nm")
        s_p = sem("s_p")
        s_pt = sem("s_pt")
        s_ptc = sem("s_ptc")
        s_pv = sem("s_pv")
        s_o = sem("s_o")
        s_gate = sem("s_gate")
        s_mg = sem("s_mg")
        s_xs = sem("s_xs")
        s_sil = sem("s_sil")
        s_act = sem("s_act")
        s_at = sem("s_at")
        s_ath = sem("s_ath")
        s_atl = sem("s_atl")
        s_rw = sem("s_rw")
        s_log = sem("s_log")
        s_rexp = sem("s_rexp")
        s_rexpin = sem("s_rexpin")
        s_sel = sem("s_sel")
        s_rank = sem("s_rank")
        s_meta = sem("s_meta")
        s_hth = sem("s_hth")
        s_htl = sem("s_htl")
        s_pick = sem("s_pick")
        s_pickw = sem("s_pickw")
        s_ga = sem("s_ga")
        s_gah = sem("s_gah")
        s_gal = sem("s_gal")
        s_bk = sem("s_bk")
        s_bkh = sem("s_bkh")
        s_bkl = sem("s_bkl")
        s_yh = sem("s_yh")
        s_yl = sem("s_yl")
        s_cmb = sem("s_cmb")
        s_dh = sem("s_dh")
        s_dve = sem("s_dve")
        s_out = sem("s_out")

        def tr_bank(call, b):
            return bank[(4, 5, 6, 7)[b] if call % 4 == 1 else (4, 5, 2, 3)[b]]

        out_bank = [[bank[6], bank[7]], [bank[0], bank[1]]]

        def norm_call(n):
            return 4 * (n // 2) + 3 * (n % 2)

        block = ctx.enter_context(nc.Block())

        def unit0(l):
            return l * (MIX_UNITS + DENSE_UNITS)

        def moe_unit(i, j):
            return i * ITEM_UNITS + (MOE_U0 + j)

        def moe_turn(i, j):
            return i * (ITEM_UNITS // RAW) + raw_turn(MOE_U0 + j)

        def ff0(i):
            return i * EXPERT_G + DENSE_G

        def xs_before(n):
            return 4 * n

        def xs_before_item(i):
            return i * 4 + 12

        @block.sync
        def _(sp):
            def row(a, n):
                return a.rearrange("(o c) -> o c", o=1).broadcast_to([P, n])

            sp.dma_start(xs[:], x[0].rearrange("(t p) c -> p t c", p=P)).then_inc(s_x, 16)
            sp.dma_start(gain, row(norm_mix[0], D)).then_inc(s_gain0, 16)
            sp.dma_start(ident[:], c_ident).then_inc(s_ident, 16)

            def fill(u, turn_value, parts):
                slot = u % RAW
                for k, (to, src) in enumerate(parts(raw_ring[:, slot, :])):
                    if k == 0 and turn_value is not None:
                        sp.wait_ge(s_lo, turn_value)
                    sp.dma_start(to, src).then_inc(s_raw[slot], 16)

            def square(w, kh, cg):
                def parts(dst):
                    v = dst.rearrange("p (k c) -> p k c", k=4)
                    rows = w.rearrange("(k p) c -> p k c", p=P)
                    return [(v[:, q:q + 2, :], rows[:, 4 * kh + q:4 * kh + q + 2, cg * COL:(cg + 1) * COL]) for q in (0, 2)]
                return parts

            def gate_up(wg, wu, kh, g):
                def parts(dst):
                    v = dst.rearrange("p (k s c) -> p k s c", k=4, s=2)
                    return [(v[:, :, s, :], w.rearrange("(k p) c -> p k c", p=P)[:, 4 * kh:4 * kh + 4, bass.ds(g * FG, FG)])
                            for s, w in enumerate((wg, wu))]
                return parts

            def down(wd, g):
                def parts(dst):
                    v = dst.rearrange("p (f c) -> p f c", f=2)
                    return [(v[:, f, :], wd[bass.ds(g * FG + f * P, P), :]) for f in range(2)]
                return parts

            def static(u, parts):
                fill(u, u - RAW + 1 if u >= RAW else None, parts)

            def mixer_stream(l):
                u = unit0(l)
                for cg in range(IN_CG):
                    if l == 0 and cg == 2:
                        for to, src in ((rope[:], c_rope), (mask[:], c_masks),
                                        (sinks[:].rearrange("p l h -> p (l h)"),
                                         row(attn_sinks.rearrange("l h -> (l h)"), DEPTH * HEADS["A"])),
                                        (router[:], w_router[0].rearrange("(k p) e -> p k e", p=P))):
                            sp.dma_start(to, src).then_inc(s_const, 16)
                    for kh in range(2):
                        static(u + U_IN + 2 * cg + kh, square(w_in[l], kh, cg))
                for ch in range(2):
                    for kh in range(2):
                        static(u + U_BR + 2 * ch + kh, square(w_br[l], kh, ch))
                for kh in range(2):
                    for ch in range(2):
                        static(u + U_OUT + 2 * kh + ch, square(w_out[l], kh, ch))

            mixer_stream(0)
            wg, wu, wd = w_ff_gate[0], w_ff_up[0], w_ff_down[0]
            n = MIX_UNITS
            for g in range(3):
                static(n, gate_up(wg, wu, 0, g))
                static(n + 1, gate_up(wg, wu, 1, g))
                n += 2
                if g:
                    static(n, down(wd, g - 1))
                    n += 1
            with sp.Fori(0, (DENSE_G - 3) // 2) as pair:
                for q in range(2):
                    g = pair * 2 + (3 + q)
                    for j, parts in enumerate((gate_up(wg, wu, 0, g), gate_up(wg, wu, 1, g), down(wd, g - 1))):
                        fill(n + 3 * q + j, pair * RAW + (n + 3 * q + j - RAW + 1), parts)
            n += 3 * (DENSE_G - 3)
            static(n, down(wd, DENSE_G - 1))
            mixer_stream(1)

            def item_stream(i, e):
                wg, wu, wd = w_moe_gate[0, e], w_moe_up[0, e], w_moe_down[0, e]

                def at(j, parts):
                    fill(MOE_U0 + j, moe_unit(i, j - RAW + 1), parts)

                at(0, gate_up(wg, wu, 0, 0))
                at(1, gate_up(wg, wu, 1, 0))
                at(2, gate_up(wg, wu, 0, 1))
                at(3, gate_up(wg, wu, 1, 1))
                at(4, down(wd, 0))
                with sp.Fori(0, EXPERT_G // 2 - 1) as pair:
                    for q in range(2):
                        g = pair * 2 + (2 + q)
                        for j, parts in enumerate((gate_up(wg, wu, 0, g), gate_up(wg, wu, 1, g), down(wd, g - 1))):
                            j += 5 + 3 * q
                            fill(MOE_U0 + j, pair * RAW + moe_unit(i, j - RAW + 1), parts)
                at(ITEM_UNITS - 1, down(wd, EXPERT_G - 1))

            with sp.Fori(0, N_EXP) as e:
                item_stream(e, e)
            sp.wait_ge(s_meta, 1)
            items = sp.value_load(meta[0:1, 0:1], min_val=N_EXP, max_val=ITEMS)
            with sp.If(items > N_EXP):
                with sp.Fori(N_EXP, items) as i:
                    e = sp.value_load(meta[0:1, bass.ds(i - (N_EXP - 1), 1)], min_val=0, max_val=N_EXP - 1)
                    item_stream(i, e)
            for t in range(TB):
                sp.wait_ge(s_y, t + 1)
                sp.dma_start(out[0, t * P:(t + 1) * P, :], h_tok[:, t, :]).then_inc(s_out, 16)
            sp.wait_ge(s_out, 16 * TB)

        @block.gpsimd
        def _(pool):
            def row(a, n):
                return a.rearrange("(o c) -> o c", o=1).broadcast_to([P, n])

            for n, g in ((1, norm_ffn[0]), (2, norm_mix[1]), (3, norm_ffn[1]), (4, norm_final)):
                pool.wait_ge(s_xg, 4 * n)
                if n % 2:
                    pool.wait_ge(s_o, NSTEP * (n + 1) // 2)
                pool.dma_start(gain, row(g, D)).then_inc(s_gain, 16)
                if n == 3:
                    pool.dma_start(route, c_route).then_inc(s_route, 16)

        @block.tensor
        def _(pe):
            def product(to, l_hi, l_lo, r_hi, r_lo, first, last):
                pe.matmul(to, l_hi, r_hi, start=first, stop=False)
                pe.matmul(to, l_hi, r_lo, start=False, stop=False)
                return pe.matmul(to, l_lo, r_hi, start=False, stop=last)

            def tile(u, k):
                s = u % SPLIT
                return w_hi[:, s, k * COL:(k + 1) * COL], w_lo[:, s, k * COL:(k + 1) * COL]

            def square(u, kh, banks, after_half=None):
                pe.wait_ge(s_lo, u + 1)
                for t, to in enumerate(banks):
                    for k in range(4):
                        kt = 4 * kh + k
                        last = product(to[:], t_hi[:, kt, t * P:(t + 1) * P], t_lo[:, kt, t * P:(t + 1) * P],
                                       *tile(u, k), kt == 0, kt == KT - 1)
                    if t == TB - 1:
                        last.then_inc(s_used, 1)
                    if after_half:
                        after_half(t)

            def transpose_act(call, half, src):
                for b in (2 * half, 2 * half + 1):
                    for k in range(2):
                        for t in range(TB):
                            last = pe.transpose(tr_bank(call, b)[:, (2 * k + t) * P:(2 * k + t + 1) * P],
                                                src[:, t, (2 * b + k) * P:(2 * b + k + 1) * P], ident[:])
                    last.then_inc(s_tr, 1)

            def transpose_stream(n):
                for half in range(2):
                    pe.wait_ge(s_xg, 4 * n + 2 * half + 2)
                    transpose_act(norm_call(n), half, h_tok)
                pe.wait_ge(s_trl, 4 * norm_call(n) + 2)

            def qk_bank(l, b):
                if b == 0:
                    pe.wait_ge(s_rope, 3 * l + 1)
                if b == 2:
                    pe.wait_ge(s_rope, 3 * l + 2)
                if b == 4:
                    pe.wait_ge(s_rope, 3 * l + 3)
                if b >= 4:
                    pe.wait_ge(s_qkc, QKT_BANKS * l + b - 3)
                for j in range(2):
                    at = (2 * b + j) * 2 * DH
                    for t in range(TB):
                        last = pe.transpose(bank[4 + b % 4][:, (2 * j + t) * P:(2 * j + t + 1) * P],
                                            qk[:, t, at:at + 2 * DH], ident[:])
                last.then_inc(s_qkt, 1)

            def halves_before(l, k):
                both = [len({head_place(b, h)[1] for h in hs}) > 1 for b, _, hs in STEPS]
                return l * sum(both) + sum(both[:k])

            def scores(l, k):
                br, t, heads = STEPS[k]
                n = (t + 1) * P
                if k == 0:
                    pe.wait_ge(s_qkc, QKT_BANKS * (l + 1))
                if k >= 2:
                    pe.wait_ge(s_sm, NSTEP * l + k - 1)
                places = [(j, *head_place(br, h)[:4]) for j, h in enumerate(heads)]
                for n_issued, (j, qb, qh, kb, kh) in enumerate(sorted(places, key=lambda p: p[2])):
                    if n_issued and qh != half:
                        last.then_inc(s_half, 1)
                        pe.wait_ge(s_half, halves_before(l, k) + 1)
                    half = qh
                    last = pe.matmul(bank[4 + k % 2][:, j * n:(j + 1) * n], qkT[qh * DH:(qh + 1) * DH, qb, t * P:(t + 1) * P],
                                     qkT[kh * DH:(kh + 1) * DH, kb, 0:n], start=True, stop=True)
                last.then_inc(s_sc, 1)

            def prob_transpose(l, k):
                _, t, heads = STEPS[k]
                pe.wait_ge(s_p, NSTEP * l + k + 1)
                if k:
                    pe.wait_ge(s_ptc, NSTEP * l + k)
                for b in range(len(heads) * (t + 1)):
                    last = pe.transpose(bank[6][:, b * P:(b + 1) * P], score[k % 3][:, b * P:(b + 1) * P], ident[:])
                last.then_inc(s_pt, 1)

            def weigh_values(l, k):
                br, t, heads = STEPS[k]
                pe.wait_ge(s_ptc, NSTEP * l + k + 1)
                if k:
                    pe.wait_ge(s_o, NSTEP * l + k)
                for j, h in enumerate(heads):
                    v = head_place(br, h)[4]
                    for kb in range(t + 1):
                        b = j * (t + 1) + kb
                        last = pe.matmul(bank[7][:, j * DH:(j + 1) * DH], probT[:, b * P:(b + 1) * P],
                                         val[:, kb, v:v + DH], start=kb == 0, stop=kb == t)
                last.then_inc(s_pv, 1)

            def attention_round(l, r):
                if r < NSTEP:
                    scores(l, r)
                if 0 <= r - LAG_PV < NSTEP:
                    weigh_values(l, r - LAG_PV)
                if 0 <= r - LAG_PT < NSTEP:
                    prob_transpose(l, r - LAG_PT)

            def mixer(l):
                u = unit0(l)
                if l == 0:
                    pe.wait_ge(s_ident, 16)
                transpose_stream(2 * l)
                for j in range(2 * IN_CG):
                    cg = j // 2
                    if j == 1:
                        pe.wait_ge(s_trl, 16 * l + 4)
                    if j % 2 == 0 and cg >= 2:
                        pe.wait_ge(s_evac, 2 * IN_CG * l + 2 * (cg - 2) + 2)
                    after = (lambda t: attention_round(l, 2 * (j - ATT_SLOT) + t)) if j >= ATT_SLOT else None
                    square(u + j, j % 2, [bank[(2 * cg + t) % 4] for t in range(TB)], after)
                    if j in QKT_SLOT:
                        for b in range(*QKT_SLOT[j]):
                            qk_bank(l, b)
                pe.wait_ge(s_o, NSTEP * (l + 1))
                pe.wait_ge(s_evac, 2 * IN_CG * (l + 1))
                transpose_act(4 * l + 1, 0, o_tok)
                transpose_act(4 * l + 1, 1, o_tok)
                bounds = (0, 3, 5, 8)
                for j in range(4):
                    ch, kh = j // 2, j % 2
                    if j < 2:
                        pe.wait_ge(s_trl, 16 * l + 4 + 2 * kh + 2)
                    pe.wait_ge(s_lo, u + U_BR + j + 1)
                    for t in range(TB):
                        if ch and t == 1 and kh == 0:
                            pe.wait_ge(s_mg, 4 * l + 1)
                        if ch and kh == 1:
                            pe.wait_ge(s_mg, 4 * l + 1 + t)
                        for kt in range(4 * kh, 4 * kh + 4):
                            br = next(b for b in range(3) if kt < bounds[b + 1])
                            last = product(bank[(6 * ch + 3 * t + br) % 8][:], t_hi[:, kt, t * P:(t + 1) * P],
                                           t_lo[:, kt, t * P:(t + 1) * P], *tile(u + U_BR + j, kt % 4),
                                           kt == bounds[br], kt == bounds[br + 1] - 1)
                    last.then_inc(s_used, 1)
                for kh in range(2):
                    pe.wait_ge(s_mg, 4 * l + 2 * kh + 2)
                    transpose_act(4 * l + 2, kh, gates)
                    pe.wait_ge(s_trl, 16 * l + 8 + 2 * kh + 2)
                    for ch in range(2):
                        if kh == 0:
                            pe.wait_ge(s_mg, 4 * l + 3 + ch)
                        square(u + U_OUT + 2 * kh + ch, kh, out_bank[ch])

            def gate_up(u, kh, par, tbs, l_hi, l_lo, ready):
                pe.wait_ge(s_lo, ready)
                for t in range(tbs):
                    for k in range(4):
                        kt = 4 * kh + k
                        last = product(bank[2 * par + t if tbs > 1 else par][:], l_hi[:, kt, t * P:(t + 1) * P],
                                       l_lo[:, kt, t * P:(t + 1) * P], *tile(u, k), kt == 0, kt == KT - 1)
                last.then_inc(s_used, 1)

            def act_transpose(par, tbs, ready):
                pe.wait_ge(s_act, ready)
                for f in range(2):
                    for t in range(tbs):
                        last = pe.transpose(bank[2 * par if tbs > 1 else par][:, (tbs * f + t) * P:(tbs * f + t + 1) * P],
                                            act_tok[:, par, t, f * P:(f + 1) * P], ident[:])
                last.then_inc(s_at, 1)

            def down(u, par, tbs, acc, ready_a, ready, first, last_group, halves=False):
                pe.wait_ge(s_atl, ready_a)
                pe.wait_ge(s_lo, ready)
                for ch in range(2):
                    for t in range(tbs):
                        for f in range(2):
                            a = (tbs * f + t) * P
                            last = product(acc(t, ch)[:], aT_hi[:, par, a:a + P], aT_lo[:, par, a:a + P],
                                           *tile(u, 2 * f + ch), first and f == 0, last_group and f == 1)
                    if halves and ch == 0:
                        last.then_inc(s_dh, 1)
                last.then_inc(s_used, 1)

            def group(u, uval, par, tbs, acc, l_hi, l_lo, done, k, first, parts=None):
                gate_up(u, 0, par, tbs, l_hi, l_lo, uval + 1)
                if parts is not None:
                    pe.wait_ge(s_trl, parts)
                if k:
                    act_transpose(1 - par, tbs, done)
                gate_up(u + 1, 1, par, tbs, l_hi, l_lo, uval + 2)
                if k:
                    down(u + 2, 1 - par, tbs, acc, done, uval + 3, first, False)

            mixer(0)
            transpose_stream(1)

            def acc2(t, ch):
                return bank[4 + 2 * ch + t]

            n = MIX_UNITS
            for g in range(3):
                group(n, n, g % 2, TB, acc2, t_hi, t_lo, g, g, g == 1, 4 * 3 + 4 if g == 0 else None)
                n += 3 if g else 2
            with pe.Fori(0, (DENSE_G - 3) // 2) as pair:
                for q in range(2):
                    group(n + 3 * q, pair * RAW + (n + 3 * q), (3 + q) % 2, TB, acc2, t_hi, t_lo, pair * 2 + (3 + q), 1, False)
            n += 3 * (DENSE_G - 3)
            act_transpose((DENSE_G - 1) % 2, TB, DENSE_G)
            down(n, (DENSE_G - 1) % 2, TB, acc2, DENSE_G, n + 1, False, True, halves=True)

            mixer(1)
            transpose_stream(3)
            pe.wait_ge(s_trl, 4 * 7 + 4)
            pe.wait_ge(s_rw, 2)
            for t in range(TB):
                for kt in range(KT):
                    last = product(bank[0][:, t * N_EXP:(t + 1) * N_EXP], t_hi[:, kt, t * P:(t + 1) * P],
                                   t_lo[:, kt, t * P:(t + 1) * P], router_hi[:, kt, :], router_lo[:, kt, :],
                                   kt == 0, kt == KT - 1)
            last.then_inc(s_log, 1)
            pe.wait_ge(s_sel, 1)
            pe.wait_ge(s_route, 16)
            E = N_EXP
            pe.matmul(bank[7][:, 0:E], c_before, r_sel[:, 0, :], start=True, stop=True)
            pe.matmul(bank[7][:, E:2 * E], c_ones, r_sel[:, 0, :], start=True, stop=False)
            pe.matmul(bank[7][:, E:2 * E], c_before, r_sel[:, 1, :], start=False, stop=True)
            pe.matmul(bank[7][:, 2 * E:3 * E], c_ones, r_sel[:, 0, :], start=True, stop=False)
            pe.matmul(bank[7][:, 2 * E:3 * E], c_ones, r_sel[:, 1, :], start=False, stop=True).then_inc(s_rank, 1)
            pe.wait_ge(s_htl, TB)

            def acc1(t, ch):
                return bank[2 + ch]

            def gather(i):
                pe.wait_ge(s_pick, i + 1)
                for b in range(2):
                    for j in range(4):
                        d = 4 * b + j
                        to = bank[4 + b][:, j * P:(j + 1) * P]
                        for t in range(TB):
                            pe.matmul(to, htok_hi[:, t, d * P:(d + 1) * P], pick[:, t, :], start=t == 0, stop=False)
                            last = pe.matmul(to, htok_lo[:, t, d * P:(d + 1) * P], pick[:, t, :], start=False, stop=t == 1)
                    last.then_inc(s_ga, 1)

            def first_group(i, j):
                pe.wait_ge(s_gal, i * 2 + 2)
                group(MOE_U0 + j, moe_unit(i, 0), 0, 1, acc1, xg_hi, xg_lo, ff0(i), 0, False)

            def head(i):
                pe.wait_ge(s_xs, xs_before_item(i))
                gather(i)
                first_group(i, 0)

            def middle(i):
                group(MOE_U0 + 2, moe_unit(i, 2), 1, 1, acc1, xg_hi, xg_lo, ff0(i) + 1, 1, True)
                pe.wait_ge(s_xs, xs_before_item(i))
                pe.wait_ge(s_pickw, i + 1)
                for t in range(TB):
                    last = pe.transpose(bank[4][:, t * P:(t + 1) * P], pick_w[:, t, :], ident[:])
                last.then_inc(s_bk, 1)
                with pe.Fori(0, EXPERT_G // 2 - 1) as pair:
                    for q in range(2):
                        group(MOE_U0 + 5 + 3 * q, pair * RAW + moe_unit(i, 5 + 3 * q), q, 1, acc1, xg_hi, xg_lo,
                              pair * 2 + (ff0(i) + (2 + q)), 1, False)

            def last_down(i):
                act_transpose(1, 1, ff0(i + 1))
                down(MOE_U0 + ITEM_UNITS - 1, 1, 1, acc1, ff0(i + 1), moe_unit(i, ITEM_UNITS), False, True)

            def combine(i):
                pe.wait_ge(s_yl, i * 2 + 2)
                pe.wait_ge(s_bkl, i + 1)
                for t in range(TB):
                    for ch in range(2):
                        product(bank[4 + 2 * t + ch][:], back_hi[:, t * P:(t + 1) * P], back_lo[:, t * P:(t + 1) * P],
                                y_hi[:, ch * COL:(ch + 1) * COL], y_lo[:, ch * COL:(ch + 1) * COL],
                                True, True).then_inc(s_cmb, 1)

            head(0)
            with pe.Fori(0, N_EXP - 1) as i:
                middle(i)
                pe.wait_ge(s_bkl, i + 1)
                gather(i + 1)
                last_down(i)
                first_group(i + 1, ITEM_UNITS)
                combine(i)
            middle(N_EXP - 1)
            last_down(N_EXP - 1)
            combine(N_EXP - 1)
            pe.wait_ge(s_meta, 1)
            items = pe.value_load(meta[0:1, 0:1], min_val=N_EXP, max_val=ITEMS)
            with pe.If(items > N_EXP):
                with pe.Fori(N_EXP, items) as i:
                    head(i)
                    middle(i)
                    last_down(i)
                    combine(i)

        @block.scalar
        def _(act):
            def split(u, turns, used):
                act.wait_ge(s_raw[u % RAW], turns)
                if used is not None:
                    act.wait_ge(s_used, used)
                act.copy(w_hi[:, u % SPLIT, :], raw_ring[:, u % RAW, :]).then_inc(s_hi, 1)

            def static(u):
                split(u, 32 * raw_turn(u), u - SPLIT + 1 if u >= SPLIT else None)

            def norm(n):
                if n == 0:
                    act.wait_ge(s_x, 16)
                for ch in range(2):
                    if n:
                        act.wait_ge(s_xs, xs_before(n) - 2 + 2 * ch)
                    for t in range(TB):
                        a = (2 * ch + t) * COL
                        act.activation(squares[:, a:a + COL], xs[:, t, ch * COL:(ch + 1) * COL], ACT.Square,
                                       accum_out=ssq[:, ch, t:t + 1]).then_inc(s_ssq, 1)
                act.wait_ge(s_var, n + 1)
                act.activation(std[:], var[:], ACT.Sqrt).then_inc(s_std, 1)

            def round_transposed(call, half):
                for b in (2 * half, 2 * half + 1):
                    act.wait_ge(s_tr, 4 * call + b + 1)
                    act.copy(t_hi[:, 2 * b:2 * b + 2, :].rearrange("p k t -> p (k t)"), tr_bank(call, b)[:]).then_inc(s_trh, 1)

            def project_copy(l, cg, used):
                act.wait_ge(s_used, used)
                if cg == 0:
                    act.wait_ge(s_rstd, 2 * l + 1)
                for t in range(TB):
                    src, scale = bank[(2 * cg + t) % 4], rstd[:, t:t + 1]
                    if cg < QKV_CG:
                        for a, what, to, n in in_pieces(cg):
                            dst, src_a = (qk if what == "qk" else val)[:, t, to:to + n], src[:, a:a + n]
                            if cg == 0:
                                nq = HEADS["A"] * DH
                                act.activation(dst[:, 0:nq].rearrange("p (i s c) -> p s i c", s=2, c=DH),
                                               src_a[:, 0:nq].rearrange("p (s i c) -> p s i c", s=2, c=DH),
                                               ACT.Copy, scale=scale)
                                dst, src_a = dst[:, nq:n], src_a[:, nq:n]
                            last = act.activation(dst, src_a, ACT.Copy, scale=scale)
                    else:
                        if cg == IN_CG - 1 and t == 1:
                            act.wait_ge(s_rope, 3 * l + 3)
                        a = (cg - QKV_CG) * COL
                        last = act.activation(gates[:, t, a:a + COL], src[:], ACT.Copy, scale=scale)
                    last.then_inc(s_evac, 1)

            def qk_copy(l, b):
                act.wait_ge(s_qkt, QKT_BANKS * l + b + 1)
                act.copy(qkT[:, 2 * b:2 * b + 2, :].rearrange("p k t -> p (k t)"), bank[4 + b % 4][:]).then_inc(s_qkc, 1)

            def exponentials(l, k):
                br, t, heads = STEPS[k]
                n = (t + 1) * P
                act.wait_ge(s_nm, NSTEP * l + k + 1)
                for j in range(len(heads)):
                    s = score[k % 3][:, j * n:(j + 1) * n]
                    last = act.activation(s, s, ACT.Exp, bias=nmx[:, k % 4, j:j + 1], accum_out=den[:, k % 4, j:j + 1])
                if br == "A":
                    nh = len(heads)
                    last = act.activation(sink_e[:, k % 4, 0:nh], sink_d[:, k % 4, 0:nh], ACT.Exp)
                last.then_inc(s_p, 1)

            def prob_copy(l, k):
                _, t, heads = STEPS[k]
                n = len(heads) * (t + 1) * P
                act.wait_ge(s_pt, NSTEP * l + k + 1)
                if k:
                    act.wait_ge(s_pv, NSTEP * l + k)
                act.copy(probT[:, 0:n], bank[6][:, 0:n]).then_inc(s_ptc, 1)

            def mixer(l):
                u = unit0(l)
                for half in range(2):
                    round_transposed(4 * l, half)
                norm(2 * l)
                for j in range(2 * IN_CG):
                    if j >= ATT_SLOT:
                        for r in (2 * (j - ATT_SLOT), 2 * (j - ATT_SLOT) + 1):
                            if r < NSTEP:
                                exponentials(l, r)
                            if 0 <= r - LAG_PT < NSTEP:
                                prob_copy(l, r - LAG_PT)
                    if j % 2 == 1:
                        project_copy(l, j // 2, u + j + 1)
                    if j in QKT_SLOT:
                        for b in range(*QKT_SLOT[j]):
                            qk_copy(l, b)
                    static(u + j + SPLIT)
                for half in range(2):
                    round_transposed(4 * l + 1, half)
                for ch in range(2):
                    for t in range(TB):
                        g = gates[:, t, :].rearrange("p (b c) -> p b c", b=3)[:, :, ch * COL:(ch + 1) * COL]
                        act.activation(g, g, ACT.Sigmoid).then_inc(s_gate, 1)
                for j in range(U_BR, U_OUT):
                    static(u + j + SPLIT)
                for half in range(2):
                    round_transposed(4 * l + 2, half)
                    for j in (2 * half, 2 * half + 1):
                        static(u + U_OUT + j + SPLIT)

            def silu(par, tbs, used):
                act.wait_ge(s_used, used)
                for t in range(tbs):
                    scale = rstd[:, t:t + 1] if tbs > 1 else 1.0
                    last = act.activation(sil[:, par, t, :], bank[2 * par + t if tbs > 1 else par][:, 0:FG], ACT.Silu,
                                          scale=scale)
                last.then_inc(s_sil, 1)

            def round_act(par, tbs, ready):
                n = 2 * tbs * P
                act.wait_ge(s_at, ready)
                act.copy(aT_hi[:, par, 0:n], bank[2 * par if tbs > 1 else par][:, 0:n]).then_inc(s_ath, 1)

            def turn(split_at, k, par, tbs, uval, done, last=False):
                if k:
                    round_act(1 - par, tbs, done)
                split_at(3)
                silu(par, tbs, uval + 2)
                if not last:
                    split_at(4)
                    if k:
                        split_at(5)

            for u in range(SPLIT):
                static(u)
            mixer(0)
            act.wait_ge(s_const, 64)
            act.copy(router_hi[:], router[:]).then_inc(s_rw, 1)
            for half in range(2):
                round_transposed(3, half)
            norm(1)
            act.wait_ge(s_rstd, 2)
            n = MIX_UNITS
            for g in range(3):
                turn(lambda j: static(n + j), g, g % 2, TB, n, g)
                n += 3 if g else 2
            with act.Fori(0, (DENSE_G - 3) // 2) as pair:
                for q in range(2):
                    v = n + 3 * q
                    turn(lambda j: split(v + j, pair * 32 + 32 * raw_turn(v + j), pair * RAW + (v + j - SPLIT + 1)),
                         1, (3 + q) % 2, TB, pair * RAW + v, pair * 2 + (3 + q))
            n += 3 * (DENSE_G - 3)
            round_act((DENSE_G - 1) % 2, TB, DENSE_G)
            static(n + SPLIT)
            mixer(1)
            for half in range(2):
                round_transposed(7, half)
            norm(3)
            act.wait_ge(s_log, 1)
            act.wait_ge(s_rstd, 4)
            for t in range(TB):
                act.activation(htok_hi[:, t, :], h_tok[:, t, :], ACT.Copy, scale=rstd[:, t:t + 1]).then_inc(s_hth, 1)
            act.wait_ge(s_rexpin, 1)
            act.activation(r_e, r_c, ACT.Exp).then_inc(s_rexp, 1)

            def split_at(i, j, pair=None):
                turns, used = moe_turn(i, j) * 32, moe_unit(i, j - SPLIT + 1)
                if pair is not None:
                    turns, used = pair * 32 + turns, pair * RAW + used
                split(MOE_U0 + j, turns, used)

            def round_gathered(i):
                for b in range(2):
                    act.wait_ge(s_ga, i * 2 + (b + 1))
                    act.copy(xg_hi[:, 4 * b:4 * b + 4, :].rearrange("p k t -> p (k t)"), bank[4 + b][:]).then_inc(s_gah, 1)

            def head(i):
                if not isinstance(i, int):
                    for j in range(SPLIT):
                        split_at(i, j)
                round_gathered(i)
                turn(lambda j: split_at(i, j), 0, 0, 1, moe_unit(i, 0), ff0(i))

            def middle(i):
                turn(lambda j: split_at(i, 2 + j), 1, 1, 1, moe_unit(i, 2), ff0(i) + 1)
                act.wait_ge(s_bk, i + 1)
                act.copy(back_hi[:], bank[4][:, 0:T]).then_inc(s_bkh, 1)
                with act.Fori(0, EXPERT_G // 2 - 2) as pair:
                    for q in range(2):
                        v = 5 + 3 * q
                        turn(lambda j: split_at(i, v + j, pair), 1, q, 1, pair * RAW + moe_unit(i, v), pair * 2 + (ff0(i) + (2 + q)))
                turn(lambda j: split_at(i, TAIL - 3 + j), 1, 0, 1, moe_unit(i, TAIL - 3), ff0(i) + (EXPERT_G - 2))
                turn(lambda j: split_at(i, TAIL + j), 1, 1, 1, moe_unit(i, TAIL), ff0(i) + (EXPERT_G - 1), last=True)

            def round_output(i):
                act.wait_ge(s_used, moe_unit(i, ITEM_UNITS))
                for ch in range(2):
                    act.copy(y_hi[:, ch * COL:(ch + 1) * COL], bank[2 + ch][:]).then_inc(s_yh, 1)

            head(0)
            with act.Fori(0, N_EXP - 1) as i:
                middle(i)
                split_at(i, ITEM_UNITS)
                split_at(i, ITEM_UNITS + 1)
                round_gathered(i + 1)
                round_act(1, 1, ff0(i + 1))
                round_output(i)
                split_at(i, ITEM_UNITS + 2)
                turn(lambda j: split_at(i, ITEM_UNITS + j), 0, 0, 1, moe_unit(i, ITEM_UNITS), ff0(i + 1))
            middle(N_EXP - 1)
            round_act(1, 1, ff0(N_EXP))
            round_output(N_EXP - 1)
            act.wait_ge(s_meta, 1)
            items = act.value_load(meta[0:1, 0:1], min_val=N_EXP, max_val=ITEMS)
            with act.If(items > N_EXP):
                with act.Fori(N_EXP, items) as i:
                    head(i)
                    middle(i)
                    round_act(1, 1, ff0(i + 1))
                    round_output(i)
            act.wait_ge(s_xs, xs_before_item(items))
            for t in range(TB):
                act.activation(squares[:, t * D:(t + 1) * D], xs[:, t, :], ACT.Square, accum_out=ssq[:, 0, t:t + 1]).then_inc(s_ssq, 1)
            act.wait_ge(s_var, 5)
            act.activation(std[:], var[:], ACT.Sqrt).then_inc(s_std, 1)

        @block.vector
        def _(dve):
            steps = [0]

            def link(ins):
                steps[0] += 1
                ins.then_inc(s_dve, 1)
                dve.wait_ge(s_dve, steps[0])

            def each(a, n):
                return a.rearrange("p (k o) -> p k o", o=1).broadcast_to([P, a.shape[1], n])

            def over(a, n):
                return a.rearrange("p (o k) -> p o k", o=1).broadcast_to([P, n, a.shape[1]])

            def split(u, rounded):
                dve.wait_ge(s_hi, rounded)
                s = u % SPLIT
                dve.tensor_tensor(w_lo[:, s, :], raw_ring[:, u % RAW, :], w_hi[:, s, :].bitcast(F32),
                                  ALU.subtract).then_inc(s_lo, 1)

            def static(u):
                split(u, u + 1)

            def norm(n):
                dve.wait_ge(s_ssq, 4 * n + 4)
                link(dve.tensor_tensor(ssum[:], ssq[:, 0, :], ssq[:, 1, :], ALU.add))
                dve.tensor_scalar(var[:], ssum[:], 1.0 / D, EPS, ALU.mult, ALU.add).then_inc(s_var, 1)
                dve.wait_ge(s_std, n + 1)
                dve.reciprocal(rstd[:], std[:]).then_inc(s_rstd, 1)

            def times_gain(n, ch):
                if ch == 0:
                    dve.wait_ge(*((s_gain, 16 * n) if n else (s_gain0, 16)))
                if n:
                    dve.wait_ge(s_xs, 4 * n - 2 + 2 * ch)
                a = slice(ch * COL, (ch + 1) * COL)
                for t in range(TB):
                    dve.tensor_tensor(h_tok[:, t, a], xs[:, t, a], gain[:, a], ALU.mult).then_inc(s_xg, 1)

            def split_transposed(call, half):
                for b in (2 * half, 2 * half + 1):
                    dve.wait_ge(s_trh, 4 * call + b + 1)
                    to = slice(2 * b, 2 * b + 2)
                    dve.tensor_tensor(t_lo[:, to, :].rearrange("p k t -> p (k t)"), tr_bank(call, b)[:],
                                      t_hi[:, to, :].bitcast(F32).rearrange("p k t -> p (k t)"),
                                      ALU.subtract).then_inc(s_trl, 1)

            def apply_rope(l, br):
                end = IN_AT[br] + (HEADS[br] + KV[br]) * DH
                dve.wait_ge(s_evac, 2 * IN_CG * l + 2 * -(-end // COL))
                heads = HEADS[br] + KV[br]
                n = 8 if heads == 8 else heads // 2
                half = DH // 2
                for t in range(TB):
                    for a in range(QK_AT[br], QK_AT[br] + heads * DH, n * DH):
                        z = qk[:, t, a:a + n * DH].rearrange("p (n c) -> p n c", n=n)
                        tmp = rope_tmp[:, 0:n * DH].rearrange("p (n c) -> p n c", n=n)
                        cos, sin = rope[:, t, 0, :], rope[:, t, 1, :]
                        dve.tensor_tensor(tmp[:, :, 0:half], z[:, :, half:DH], over(sin[:, 0:half], n), ALU.mult)
                        link(dve.tensor_tensor(tmp[:, :, half:DH], z[:, :, 0:half], over(sin[:, half:DH], n), ALU.mult))
                        link(dve.tensor_tensor(z, z, over(cos, n), ALU.mult))
                        link(dve.tensor_tensor(z, z, tmp, ALU.add))
                dve.sem_inc(s_rope, 1)

            def mask_and_max(l, k):
                br, t, heads = STEPS[k]
                nh, n, b = len(heads), (t + 1) * P, k % 4
                dve.wait_ge(s_sc, NSTEP * l + k + 1)
                if k >= 3:
                    dve.wait_ge(s_pt, NSTEP * l + k - 2)
                for j in range(nh):
                    last = dve.tensor_tensor_reduce(score[k % 3][:, j * n:(j + 1) * n], bank[4 + k % 2][:, j * n:(j + 1) * n],
                                                    mask[:, "ABC".index(br), T - n:T], SCALE, -3e38, ALU.add, ALU.max,
                                                    mx[:, b, j:j + 1])
                last.then_inc(s_sm, 1)
                dve.wait_ge(s_sm, NSTEP * l + k + 1)
                if br == "A":
                    sk = sinks[:, l, heads[0]:heads[0] + nh]
                    link(dve.tensor_tensor(mx[:, b, 0:nh], mx[:, b, 0:nh], sk, ALU.max))
                    dve.tensor_tensor(sink_d[:, b, 0:nh], sk, mx[:, b, 0:nh], ALU.subtract)
                dve.tensor_scalar(nmx[:, b, 0:nh], mx[:, b, 0:nh], -1.0, None, ALU.mult).then_inc(s_nm, 1)

            def reciprocals(l, k):
                br, t, heads = STEPS[k]
                nh, b = len(heads), k % 4
                dve.wait_ge(s_p, NSTEP * l + k + 1)
                if k >= 4:
                    dve.wait_ge(s_o, NSTEP * l + k - 3)
                if br == "A":
                    link(dve.tensor_tensor(den[:, b, 0:nh], den[:, b, 0:nh], sink_e[:, b, 0:nh], ALU.add))
                link(dve.reciprocal(rden[:, b, 0:nh], den[:, b, 0:nh]))

            def outputs(l, k):
                br, t, heads = STEPS[k]
                nh, b = len(heads), k % 4
                dve.wait_ge(s_pv, NSTEP * l + k + 1)
                a = O_AT[br] + heads[0] * DH
                dve.tensor_tensor(o_tok[:, t, a:a + nh * DH].rearrange("p (h c) -> p h c", h=nh),
                                  bank[7][:, 0:nh * DH].rearrange("p (h c) -> p h c", h=nh),
                                  each(rden[:, b, 0:nh], DH), ALU.mult).then_inc(s_o, 1)

            def merge(l, ch, t):
                dve.wait_ge(s_gate, 4 * l + 2 * ch + t + 1)
                g = [gates[:, t, b * D + ch * COL:b * D + (ch + 1) * COL] for b in range(3)]
                for b in range(3):
                    last = dve.tensor_tensor(g[b], g[b], bank[(6 * ch + 3 * t + b) % 8][:], ALU.mult)
                link(last)
                link(dve.tensor_tensor(g[0], g[0], g[1], ALU.add))
                dve.tensor_tensor(g[0], g[0], g[2], ALU.add).then_inc(s_mg, 1)

            def add_to_stream(t, ch, src):
                a = xs[:, t, ch * COL:(ch + 1) * COL]
                dve.tensor_tensor(a, a, src[:], ALU.add).then_inc(s_xs, 1)

            def mixer(l):
                u = unit0(l)
                for half in range(2):
                    split_transposed(4 * l, half)
                norm(2 * l)
                for j in range(2 * IN_CG):
                    if j in ROPE_SLOT:
                        apply_rope(l, ROPE_SLOT[j])
                    if j >= ATT_SLOT:
                        for r in (2 * (j - ATT_SLOT), 2 * (j - ATT_SLOT) + 1):
                            if r < NSTEP:
                                mask_and_max(l, r)
                            if 0 <= r - LAG_PT < NSTEP:
                                reciprocals(l, r - LAG_PT)
                            if 0 <= r - LAG_PV < NSTEP:
                                outputs(l, r - LAG_PV)
                    static(u + j + SPLIT)
                for half in range(2):
                    split_transposed(4 * l + 1, half)
                for j in range(U_BR, U_OUT):
                    static(u + j + SPLIT)
                    if j == U_BR + 1:
                        dve.wait_ge(s_used, u + j + 1)
                        for t in range(TB):
                            merge(l, 0, t)
                dve.wait_ge(s_trh, 16 * l + 10)
                split_transposed(4 * l + 2, 0)
                dve.wait_ge(s_used, u + U_OUT)
                for t in range(TB):
                    merge(l, 1, t)
                static(u + U_OUT + SPLIT)
                static(u + U_OUT + 1 + SPLIT)
                split_transposed(4 * l + 2, 1)
                for ch in range(2):
                    static(u + U_OUT + 2 + ch + SPLIT)
                    dve.wait_ge(s_used, u + U_OUT + 2 + ch + 1)
                    for t in range(TB):
                        add_to_stream(t, ch, out_bank[ch][t])
                    times_gain(2 * l + 1, ch)

            def times_up(par, tbs, done):
                dve.wait_ge(s_sil, done)
                for t in range(tbs):
                    to, s, up = act_tok[:, par, t, :], sil[:, par, t, :], bank[2 * par + t if tbs > 1 else par][:, FG:2 * FG]
                    if tbs > 1:
                        last = dve.scalar_tensor_tensor(out=to, in0=up, scalar=rstd[:, t:t + 1], in1=s, op0=ALU.mult, op1=ALU.mult)
                    else:
                        last = dve.tensor_tensor(to, s, up, ALU.mult)
                last.then_inc(s_act, 1)

            def split_act(par, tbs, ready):
                n = 2 * tbs * P
                dve.wait_ge(s_ath, ready)
                dve.tensor_tensor(aT_lo[:, par, 0:n], bank[2 * par if tbs > 1 else par][:, 0:n],
                                  aT_hi[:, par, 0:n].bitcast(F32), ALU.subtract).then_inc(s_atl, 1)

            def turn(split_at, k, par, tbs, done, last=False):
                if k:
                    split_act(1 - par, tbs, done)
                split_at(3)
                times_up(par, tbs, done + 1)
                if not last:
                    split_at(4)
                    if k:
                        split_at(5)

            dve.wait_ge(s_x, 16)
            for ch in range(2):
                times_gain(0, ch)
            for u in range(SPLIT):
                static(u)
            mixer(0)
            for half in range(2):
                split_transposed(3, half)
            norm(1)
            dve.wait_ge(s_rstd, 2)
            dve.wait_ge(s_rw, 1)
            dve.tensor_tensor(router_lo[:], router[:], router_hi[:].bitcast(F32), ALU.subtract).then_inc(s_rw, 1)
            n = MIX_UNITS
            for g in range(3):
                turn(lambda j: static(n + j), g, g % 2, TB, g)
                n += 3 if g else 2
            with dve.Fori(0, (DENSE_G - 3) // 2) as pair:
                for q in range(2):
                    v = n + 3 * q
                    turn(lambda j: split(v + j, pair * RAW + (v + j + 1)), 1, (3 + q) % 2, TB, pair * 2 + (3 + q))
            n += 3 * (DENSE_G - 3)
            split_act((DENSE_G - 1) % 2, TB, DENSE_G)
            for ch in range(2):
                dve.wait_ge(*((s_used, n + 1) if ch else (s_dh, 1)))
                for t in range(TB):
                    add_to_stream(t, ch, bank[4 + 2 * ch + t])
                times_gain(2, ch)
            static(n + SPLIT)
            mixer(1)
            for half in range(2):
                split_transposed(7, half)
            norm(3)
            dve.wait_ge(s_rstd, 4)

            E = N_EXP
            dve.wait_ge(s_log, 1)
            dve.wait_ge(s_route, 16)
            for t in range(TB):
                link(dve.tensor_scalar(r_log[:, t, :], bank[0][:, t * E:(t + 1) * E], rstd[:, t:t + 1], None, ALU.mult))
            for src, top, chosen in ((r_log, r_m1, r_first), (r_l2, r_m2, r_second)):
                link(dve.tensor_reduce(top, src, AX, ALU.max))
                link(dve.tensor_tensor(r_eq, src, each(top, E), ALU.is_equal))
                link(dve.tensor_tensor(r_t, r_eq, over(c_desc, TB), ALU.mult))
                link(dve.tensor_reduce(r_den, r_t, AX, ALU.max))
                link(dve.tensor_tensor(chosen, r_t, each(r_den, E), ALU.is_equal))
                if src is r_log:
                    link(dve.scalar_tensor_tensor(out=r_l2, in0=r_first, scalar=-3e38, in1=r_log, op0=ALU.mult, op1=ALU.add))
            dve.tensor_tensor(r_sel, r_first, r_second, ALU.add).then_inc(s_sel, 1)
            dve.tensor_tensor(r_c, r_m2, r_m1, ALU.subtract).then_inc(s_rexpin, 1)
            for t in range(TB):
                dve.wait_ge(s_hth, t + 1)
                dve.scalar_tensor_tensor(out=htok_lo[:, t, :], in0=h_tok[:, t, :], scalar=rstd[:, t:t + 1],
                                         in1=htok_hi[:, t, :].bitcast(F32), op0=ALU.mult, op1=ALU.subtract).then_inc(s_htl, 1)
            dve.wait_ge(s_rank, 1)
            rank = bank[7][:, 0:TB * E].rearrange("p (t e) -> p t e", t=TB)
            link(dve.scalar_tensor_tensor(out=r_rank, in0=rank, scalar=1.0, in1=r_sel, op0=ALU.add, op1=ALU.mult))
            link(dve.tensor_scalar(item_slot[:, :, 0:E], r_rank, -1.0, None, ALU.add))

            def weigh_choices():
                dve.wait_ge(s_rexp, 1)
                link(dve.tensor_scalar(r_den, r_e, 1.0, None, ALU.add))
                link(dve.reciprocal(r_w1, r_den))
                link(dve.tensor_tensor(r_w2, r_e, r_w1, ALU.mult))
                dve.tensor_tensor(r_first, r_first, each(r_w1, E), ALU.mult)
                link(dve.tensor_tensor(r_second, r_second, each(r_w2, E), ALU.mult))
                link(dve.tensor_tensor(r_w, r_first, r_second, ALU.add))
                link(dve.tensor_copy(item_w[:, :, 0:E], r_w))

            def overflow_items():
                dve.tensor_scalar(r_slot, r_rank, -1.0 - P, None, ALU.add)
                link(dve.tensor_scalar(r_over, bank[7][:, 2 * E:3 * E], float(P), None, ALU.is_gt))
                link(dve.tensor_tensor_scan(r_cum, c_ones[:, 0:E], r_over, 0.0, ALU.mult, ALU.add))
                dve.tensor_scalar(r_meta[:, 0:1], r_cum[:, E - 1:E], float(E), None, ALU.add)
                for j in range(OVER):
                    link(dve.scalar_tensor_tensor(out=r_hot, in0=r_cum, scalar=float(j + 1), in1=r_over,
                                                  op0=ALU.is_equal, op1=ALU.mult))
                    for src, to in ((r_slot, item_slot), (r_w, item_w)):
                        link(dve.tensor_tensor(r_t, src, over(r_hot, TB), ALU.mult))
                        link(dve.tensor_reduce(to[:, :, E + j], r_t, AX, ALU.add))
                    link(dve.tensor_tensor(r_hot, r_hot, c_expert, ALU.mult))
                    link(dve.tensor_reduce(r_meta[:, 1 + j:2 + j], r_hot, AX, ALU.add))
                dve.tensor_copy(meta[:], r_meta[0:1, :]).then_inc(s_meta, 1)

            def split_at(i, j, pair=None):
                rounded = moe_unit(i, j + 1)
                split(MOE_U0 + j, rounded if pair is None else pair * RAW + rounded)

            def pick_tokens(i):
                for t in range(TB):
                    last = dve.tensor_scalar(pick[:, t, :], c_slot, item_slot[:, t, bass.ds(i, 1)], None, ALU.is_equal)
                last.then_inc(s_pick, 1)

            def weigh_picked(i):
                for t in range(TB):
                    slot, w = item_slot[:, t, bass.ds(i, 1)], item_w[:, t, bass.ds(i, 1)]
                    last = dve.tensor_scalar(pick_w[:, t, :], c_slot, slot, w, ALU.is_equal, ALU.mult)
                last.then_inc(s_pickw, 1)

            def split_gathered(i):
                for b in range(2):
                    dve.wait_ge(s_gah, i * 2 + (b + 1))
                    to = slice(4 * b, 4 * b + 4)
                    dve.tensor_tensor(xg_lo[:, to, :].rearrange("p k t -> p (k t)"), bank[4 + b][:],
                                      xg_hi[:, to, :].bitcast(F32).rearrange("p k t -> p (k t)"),
                                      ALU.subtract).then_inc(s_gal, 1)

            def head(i):
                pick_tokens(i)
                if isinstance(i, int):
                    weigh_choices()
                    weigh_picked(i)
                    split_gathered(i)
                    overflow_items()
                else:
                    weigh_picked(i)
                    for j in range(SPLIT):
                        split_at(i, j)
                    split_gathered(i)
                turn(lambda j: split_at(i, j), 0, 0, 1, ff0(i))

            def middle(i):
                turn(lambda j: split_at(i, 2 + j), 1, 1, 1, ff0(i) + 1)
                dve.wait_ge(s_bkh, i + 1)
                dve.tensor_tensor(back_lo[:], bank[4][:, 0:T], back_hi[:].bitcast(F32), ALU.subtract).then_inc(s_bkl, 1)
                with dve.Fori(0, EXPERT_G // 2 - 2) as pair:
                    for q in range(2):
                        v = 5 + 3 * q
                        turn(lambda j: split_at(i, v + j, pair), 1, q, 1, pair * 2 + (ff0(i) + (2 + q)))
                turn(lambda j: split_at(i, TAIL - 3 + j), 1, 0, 1, ff0(i) + (EXPERT_G - 2))
                turn(lambda j: split_at(i, TAIL + j), 1, 1, 1, ff0(i) + (EXPERT_G - 1), last=True)

            def split_output(i):
                for ch in range(2):
                    dve.wait_ge(s_yh, i * 2 + (ch + 1))
                    a = slice(ch * COL, (ch + 1) * COL)
                    dve.tensor_tensor(y_lo[:, a], bank[2 + ch][:], y_hi[:, a].bitcast(F32), ALU.subtract).then_inc(s_yl, 1)

            def add_output(i):
                for t in range(TB):
                    for ch in range(2):
                        dve.wait_ge(s_cmb, i * 4 + (2 * t + ch + 1))
                        add_to_stream(t, ch, bank[4 + 2 * t + ch])

            head(0)
            with dve.Fori(0, N_EXP - 1) as i:
                middle(i)
                pick_tokens(i + 1)
                weigh_picked(i + 1)
                split_at(i, ITEM_UNITS)
                split_at(i, ITEM_UNITS + 1)
                split_gathered(i + 1)
                split_act(1, 1, ff0(i + 1))
                split_output(i)
                split_at(i, ITEM_UNITS + 2)
                turn(lambda j: split_at(i, ITEM_UNITS + j), 0, 0, 1, ff0(i + 1))
                add_output(i)
            middle(N_EXP - 1)
            split_act(1, 1, ff0(N_EXP))
            split_output(N_EXP - 1)
            add_output(N_EXP - 1)
            dve.wait_ge(s_meta, 1)
            items = dve.value_load(meta[0:1, 0:1], min_val=N_EXP, max_val=ITEMS)
            with dve.If(items > N_EXP):
                with dve.Fori(N_EXP, items) as i:
                    head(i)
                    middle(i)
                    split_act(1, 1, ff0(i + 1))
                    split_output(i)
                    add_output(i)
            dve.wait_ge(s_ssq, 4 * 4 + TB)
            dve.tensor_scalar(var[:], ssq[:, 0, :], 1.0 / D, EPS, ALU.mult, ALU.add).then_inc(s_var, 1)
            dve.wait_ge(s_std, 5)
            dve.reciprocal(rstd[:], std[:]).then_inc(s_rstd, 1)
            dve.wait_ge(s_rstd, 5)
            dve.wait_ge(s_gain, 16 * 4)
            for t in range(TB):
                dve.scalar_tensor_tensor(out=h_tok[:, t, :], in0=xs[:, t, :], scalar=rstd[:, t:t + 1], in1=gain[:],
                                         op0=ALU.mult, op1=ALU.mult).then_inc(s_y, 1)


def _constants():
    i, j = np.arange(P)[:, None] + P, np.arange(T)[None, :]
    gap = i - j
    inside = {
        "A": ((gap >= 0) & (gap <= 127)).astype(np.float64),
        "B": (gap >= 0).astype(np.float64),
        "C": ((gap >= 0) & (gap <= 128)).astype(np.float64) + ((gap >= 0) & (gap % 4 == 0)) + ((gap >= 0) & (gap % 16 == 0)),
    }
    masks = np.stack([np.where(m > 0, np.log(np.maximum(m, 1.0)), NEG) / SCALE for m in inside.values()], axis=1)
    pos = np.arange(T, dtype=np.float32)
    inv = np.float32(10000.0) ** (-np.arange(0, DH, 2, dtype=np.float32) / np.float32(DH))
    ang = pos[:, None] * inv[None, :]
    cos, sin = np.cos(ang), np.sin(ang)
    tables = np.stack([np.concatenate([cos, cos], 1), np.concatenate([-sin, sin], 1)], axis=1)
    tables = tables.reshape(TB, P, 2, DH).transpose(1, 0, 2, 3)
    k = np.arange(P)
    before = (k[:, None] < k[None, :])
    e = np.arange(N_EXP)
    route = np.concatenate([before, np.ones((P, P)), np.tile(k, (P, 1)), np.tile(N_EXP - e, (P, 1)), np.tile(e, (P, 1))], axis=1)
    f = np.float32
    return (np.eye(P, dtype=f), np.ascontiguousarray(masks.astype(f)), np.ascontiguousarray(tables.astype(f)),
            np.ascontiguousarray(route.astype(f)))


def kernel(x, norm_mix, w_in, attn_sinks, w_br_a, w_br_b, w_br_c, w_out, norm_ffn, w_ff_gate, w_ff_up, w_ff_down,
           w_router, w_moe_gate, w_moe_up, w_moe_down, norm_final):
    import concourse.bacc as _bacc
    from concourse.bass_utils import run_bass_kernel_spmd as _run

    ident, masks, tables, route = _constants()
    ins = {
        "x": x, "norm_mix": norm_mix, "w_in": w_in, "attn_sinks": attn_sinks,
        "w_br": np.concatenate([np.asarray(w_br_a), np.asarray(w_br_b), np.asarray(w_br_c)], axis=1),
        "w_out": w_out, "norm_ffn": norm_ffn, "w_ff_gate": w_ff_gate, "w_ff_up": w_ff_up, "w_ff_down": w_ff_down,
        "w_router": w_router, "w_moe_gate": w_moe_gate, "w_moe_up": w_moe_up, "w_moe_down": w_moe_down,
        "norm_final": norm_final, "c_ident": ident, "c_masks": masks, "c_rope": tables, "c_route": route,
    }
    nc = _bacc.Bacc("TRN2", target_bir_lowering=False, num_devices=1)
    arrays, args = {}, []
    for name, a in ins.items():
        a = np.ascontiguousarray(a)
        arrays[f"in_{name}"] = a
        args.append(nc.dram_tensor(f"in_{name}", a.shape, mybir.dt.from_np(a.dtype), kind="ExternalInput").ap())
    args.append(nc.dram_tensor("out_0", (1, T, D), F32, kind="ExternalOutput").ap())
    bass_trunk(nc, *args)
    r = _run(nc, [arrays], core_ids=[0])
    return r.results[0]["out_0"]
```

```python
from contextlib import ExitStack

import numpy as np

import concourse.bass as bass
from concourse import mybir

P = 128
F32 = mybir.dt.float32
F32R = mybir.dt.float32r
I32 = mybir.dt.int32
ALU = mybir.AluOpType
ACT = mybir.ActivationFunctionType
AX = mybir.AxisListType.X

T, D = 256, 1024
TB, KT = T // P, D // P
DEPTH = 2
DH = 64
SCALE = DH ** -0.5
EPS = 1e-5
NEG = -1e30
FF_DENSE, FF_EXPERT, N_EXP = 2816, 3584, 8
COL = 512
FG = 256
UNIT = 4 * COL
RAW, SPLIT = 6, 3

HEADS = {"A": 6, "B": 4, "C": 6}
KV = {"A": 2, "B": 4, "C": 6}
QKV_COLS = sum(HEADS[b] + 2 * KV[b] for b in "ABC") * DH
QK_LEN = sum(HEADS[b] + KV[b] for b in "ABC") * DH
V_LEN = sum(KV[b] for b in "ABC") * DH
QK_AT, V_AT, O_AT, IN_AT = {}, {}, {}, {}
_i = _q = _v = _o = 0
for _b in "ABC":
    IN_AT[_b], QK_AT[_b], V_AT[_b], O_AT[_b] = _i, _q, _v, _o
    _i += (HEADS[_b] + 2 * KV[_b]) * DH
    _q += (HEADS[_b] + KV[_b]) * DH
    _v += KV[_b] * DH
    _o += HEADS[_b] * DH
IN_CG = (QKV_COLS + 3 * D) // COL
QKV_CG = QKV_COLS // COL

U_IN, U_BR, U_OUT = 0, 2 * IN_CG, 2 * IN_CG + 4
MIX_UNITS = U_OUT + 4
DENSE_G, EXPERT_G = FF_DENSE // FG, FF_EXPERT // FG
DENSE_UNITS, ITEM_UNITS = 3 * DENSE_G, 3 * EXPERT_G
MOE_U0 = 2 * MIX_UNITS + DENSE_UNITS
OVER = 3
ITEMS = N_EXP + OVER
TAIL = ITEM_UNITS - 4

QKT_BLOCKS = QK_LEN // (2 * DH)
QKT_BANKS = QKT_BLOCKS // 2

STEPS = [(b, 0, list(range(i, min(i + 4, HEADS[b])))) for b in "ABC" for i in range(0, HEADS[b], 4)]
STEPS += [(b, 1, [i, i + 1]) for b in "ABC" for i in range(0, HEADS[b], 2)]
WARM_START, WARM_HALF, WARM_CHOICE, WARM_RANK = 12, 6, 14, 5
FIRST_HALF_STEPS = 1 + max(k for k, (b, _, hs) in enumerate(STEPS) if O_AT[b] + hs[0] * DH < COL)
LAG_PT, LAG_PV = 2, 3
NSTEP = len(STEPS)
QKT_SLOT = {9: (0, 2), 11: (2, 4), 13: (4, 7)}
ATT_SLOT = 14
ROPE_SLOT = {3: "A", 6: "B", 10: "C"}


def head_place(b, h):
    if b == "A":
        return h % 3, h // 3, 3, h // 3, V_AT[b] + (h // 3) * DH
    first = 4 if b == "B" else 8
    return first + h // 2, h % 2, first + HEADS[b] // 2 + h // 2, h % 2, V_AT[b] + h * DH


def in_pieces(cg):
    out = []
    for b in "ABC":
        nqk, nv = (HEADS[b] + KV[b]) * DH, KV[b] * DH
        for a, n, what, to in ((IN_AT[b], nqk, "qk", QK_AT[b]), (IN_AT[b] + nqk, nv, "v", V_AT[b])):
            lo, hi = max(a, cg * COL), min(a + n, (cg + 1) * COL)
            if lo < hi:
                out.append((lo - cg * COL, what, to + lo - a, hi - lo))
    return out


def raw_turn(u):
    return u // RAW + 1


def bass_trunk(nc, x, norm_mix, w_in, attn_sinks, w_br, w_out, norm_ffn, w_ff_gate, w_ff_up, w_ff_down,
               w_router, w_moe_gate, w_moe_up, w_moe_down, norm_final, c_ident, c_masks, c_rope, c_route, out):
    ctx = ExitStack()
    with ctx:
        def sb(name, shape, dt=F32):
            return ctx.enter_context(nc.sbuf_tensor(name, shape, dt))

        def sem(name):
            return ctx.enter_context(nc.semaphore(name))

        bank = [ctx.enter_context(nc.psum_tensor(f"bank{i}", [P, COL], F32)) for i in range(8)]

        raw_ring = sb("raw_ring", [P, RAW, UNIT])
        w_hi = sb("w_hi", [P, SPLIT, UNIT], F32R)
        w_lo = sb("w_lo", [P, SPLIT, UNIT], F32R)
        xs = sb("xs", [P, TB, D])
        t_hi = sb("t_hi", [P, KT, T], F32R)
        t_lo = sb("t_lo", [P, KT, T], F32R)
        gates = sb("gates", [P, TB, 3 * D])
        work = sb("work", [P, TB * QK_LEN])
        val = sb("val", [P, TB, V_LEN])
        qkT = sb("qkT", [P, QKT_BLOCKS, T])
        qk = work[:, :].rearrange("p (t c) -> p t c", t=TB)
        h_tok = work[:, 0:TB * D].rearrange("p (t c) -> p t c", t=TB)
        o_tok = h_tok
        probT = work[:, TB * D + 2 * COL:TB * D + 3 * COL]
        score3 = sb("score3", [P, COL])
        score = [work[:, TB * D:TB * D + COL], work[:, TB * D + COL:TB * D + 2 * COL], score3[:, :]]
        logits_T = work[0:2 * N_EXP, TB * D:TB * D + T]
        qkT_flat = qkT[:, :, :].rearrange("p k t -> p (k t)")
        gain = qkT_flat[:, 0:D]
        squares = qkT_flat[:, D:3 * D]
        rope_tmp = gates[:, 1, 3 * D - COL:3 * D]
        aT_hi = sb("aT_hi", [P, 2, COL], F32R)
        aT_lo = sb("aT_lo", [P, 2, COL], F32R)
        flat = gates[:, :, :].rearrange("p t c -> p (t c)")
        sil = flat[:, 0:4 * FG].rearrange("p (n t c) -> p n t c", n=2, t=TB)
        act_tok = flat[:, 4 * FG:8 * FG].rearrange("p (n t c) -> p n t c", n=2, t=TB)
        xg_hi = sb("xg_hi", [P, KT, P], F32R)
        xg_lo = sb("xg_lo", [P, KT, P], F32R)
        pick = sb("pick", [P, TB, P], F32R)
        back_hi = sb("back_hi", [P, T], F32R)
        back_lo = sb("back_lo", [P, T], F32R)
        y_hi = aT_hi[:, :, :].rearrange("p n c -> p (n c)")
        y_lo = aT_lo[:, :, :].rearrange("p n c -> p (n c)")
        htok_hi = t_hi[:, :, :].rearrange("p k t -> p (k t)").rearrange("p (t c) -> p t c", t=TB)
        htok_lo = t_lo[:, :, :].rearrange("p k t -> p (k t)").rearrange("p (t c) -> p t c", t=TB)
        pick_w = flat[:, 8 * FG:9 * FG].rearrange("p (t c) -> p t c", t=TB)
        tbl_at = [9 * FG]

        def table(*shape):
            n = int(np.prod(shape))
            a = flat[:, tbl_at[0]:tbl_at[0] + n]
            tbl_at[0] += n
            return a.rearrange("p (t e) -> p t e", t=shape[0]) if len(shape) == 2 else a

        r_log, r_eq, r_l2, r_first, r_second, r_sel, r_w, r_rank, r_slot, r_t = (table(TB, N_EXP) for _ in range(10))
        r_m1, r_m2, r_c, r_e, r_den, r_w1, r_w2 = (table(TB) for _ in range(7))
        r_over, r_cum, r_hot = (table(N_EXP) for _ in range(3))
        r_meta = table(4)
        item_slot, item_w = table(TB, ITEMS), table(TB, ITEMS)
        meta = sb("meta", [1, 4], I32)
        ident = sb("ident", [P, P])
        mask = sb("mask", [P, 3, T])
        rope = sb("rope", [P, TB, 2, DH])
        sinks = sb("sinks", [P, DEPTH, HEADS["A"]])
        router = sb("router", [P, KT, N_EXP])
        router_parts = sb("router_parts", [P, KT, 2 * N_EXP], F32R)
        router_hi, router_lo = router_parts[:, :, 0:N_EXP], router_parts[:, :, N_EXP:2 * N_EXP]
        route = val[:, :, :].rearrange("p t c -> p (t c)")[:, 0:3 * P + 2 * N_EXP]
        c_before, c_ones, c_slot = route[:, 0:P], route[:, P:2 * P], route[:, 2 * P:3 * P]
        c_desc, c_expert = route[:, 3 * P:3 * P + N_EXP], route[:, 3 * P + N_EXP:3 * P + 2 * N_EXP]
        unread = sb("unread", [P, 1])
        ssq = sb("ssq", [P, 2, TB])
        ssum, var, std, rstd = (sb(n, [P, TB]) for n in ("ssum", "var", "std", "rstd"))
        mx, nmx, den, sink_d, sink_e, rden = (sb(n, [P, 4, 4]) for n in ("mx", "nmx", "den", "sink_d", "sink_e", "rden"))

        s_x = [sem(f"s_x{ch}") for ch in range(2)]
        s_ident = sem("s_ident")
        s_const = sem("s_const")
        s_gain0 = sem("s_gain0")
        s_gain = sem("s_gain")
        s_route = sem("s_route")
        s_raw = [sem(f"s_raw{i}") for i in range(RAW)]
        s_hi = sem("s_hi")
        s_lo = sem("s_lo")
        s_used = sem("s_used")
        s_ssq = sem("s_ssq")
        s_var = sem("s_var")
        s_std = sem("s_std")
        s_rstd = sem("s_rstd")
        s_xg = sem("s_xg")
        s_y = [sem(f"s_y{ch}") for ch in range(2)]
        s_tr = sem("s_tr")
        s_trh = sem("s_trh")
        s_trl = sem("s_trl")
        s_evac = sem("s_evac")
        s_rope = sem("s_rope")
        s_qkt = sem("s_qkt")
        s_qkc = sem("s_qkc")
        s_sc = sem("s_sc")
        s_half = sem("s_half")
        s_sm = sem("s_sm")
        s_nm = sem("s_nm")
        s_p = sem("s_p")
        s_pt = sem("s_pt")
        s_ptc = sem("s_ptc")
        s_pv = sem("s_pv")
        s_o = sem("s_o")
        s_gate = sem("s_gate")
        s_mg = sem("s_mg")
        s_xs = sem("s_xs")
        s_sil = sem("s_sil")
        s_act = sem("s_act")
        s_at = sem("s_at")
        s_ath = sem("s_ath")
        s_atl = sem("s_atl")
        s_rw = sem("s_rw")
        s_logT = sem("s_logT")
        s_logc = sem("s_logc")
        s_log = sem("s_log")
        s_rexp = sem("s_rexp")
        s_rexpin = sem("s_rexpin")
        s_sel = sem("s_sel")
        s_rank = sem("s_rank")
        s_count = sem("s_count")
        s_over = sem("s_over")
        s_pool = sem("s_pool")
        s_meta = sem("s_meta")
        s_hth = sem("s_hth")
        s_htl = sem("s_htl")
        s_pick = sem("s_pick")
        s_pickw = sem("s_pickw")
        s_ga = sem("s_ga")
        s_gah = sem("s_gah")
        s_gal = sem("s_gal")
        s_bk = sem("s_bk")
        s_bkh = sem("s_bkh")
        s_bkl = sem("s_bkl")
        s_yh = sem("s_yh")
        s_yl = sem("s_yl")
        s_cmb = sem("s_cmb")
        s_dh = sem("s_dh")
        s_dve = sem("s_dve")
        s_out = sem("s_out")

        def tr_bank(call, b):
            return bank[((4, 5, 2, 3), (4, 5, 6, 7), (4, 5, 2, 3), (0, 1, 2, 3))[call % 4][b]]

        out_bank = [[bank[4], bank[5]], [bank[6], bank[7]]]

        def norm_call(n):
            return 4 * (n // 2) + 3 * (n % 2)

        block = ctx.enter_context(nc.Block())

        def unit0(l):
            return l * (MIX_UNITS + DENSE_UNITS)

        def moe_unit(i, j):
            return i * ITEM_UNITS + (MOE_U0 + j)

        def moe_turn(i, j):
            return i * (ITEM_UNITS // RAW) + raw_turn(MOE_U0 + j)

        def ff0(i):
            return i * EXPERT_G + DENSE_G

        def xs_before(n):
            return 4 * n

        def xs_before_item(i):
            return i * 4 + 12

        @block.sync
        def _(sp):
            def row(a, n):
                return a.rearrange("(o c) -> o c", o=1).broadcast_to([P, n])

            def load_x(ch):
                a = slice(ch * COL, (ch + 1) * COL)
                sp.dma_start(xs[:, :, a], x[0].rearrange("(t p) c -> p t c", p=P)[:, :, a]).then_inc(s_x[ch], 16)

            load_x(0)
            sp.dma_start(gain, row(norm_mix[0], D)).then_inc(s_gain0, 16)
            sp.dma_start(ident[:], c_ident).then_inc(s_ident, 16)

            def fill(u, turn_value, parts):
                slot = u % RAW
                for k, (to, src) in enumerate(parts(raw_ring[:, slot, :])):
                    if k == 0 and turn_value is not None:
                        sp.wait_ge(s_lo, turn_value)
                    sp.dma_start(to, src).then_inc(s_raw[slot], 16)

            def square(w, kh, cg):
                def parts(dst):
                    v = dst.rearrange("p (k c) -> p k c", k=4)
                    rows = w.rearrange("(k p) c -> p k c", p=P)
                    return [(v[:, q:q + 2, :], rows[:, 4 * kh + q:4 * kh + q + 2, cg * COL:(cg + 1) * COL]) for q in (0, 2)]
                return parts

            def gate_up(wg, wu, kh, g):
                def parts(dst):
                    v = dst.rearrange("p (k s c) -> p k s c", k=4, s=2)
                    return [(v[:, :, s, :], w.rearrange("(k p) c -> p k c", p=P)[:, 4 * kh:4 * kh + 4, bass.ds(g * FG, FG)])
                            for s, w in enumerate((wg, wu))]
                return parts

            def down(wd, g):
                def parts(dst):
                    v = dst.rearrange("p (f c) -> p f c", f=2)
                    return [(v[:, f, :], wd[bass.ds(g * FG + f * P, P), :]) for f in range(2)]
                return parts

            def static(u, parts):
                fill(u, u - RAW + 1 if u >= RAW else None, parts)

            def mixer_stream(l):
                u = unit0(l)
                for cg in range(IN_CG):
                    if l == 0 and cg == 2:
                        for to, src in ((rope[:], c_rope), (mask[:], c_masks),
                                        (sinks[:].rearrange("p l h -> p (l h)"),
                                         row(attn_sinks.rearrange("l h -> (l h)"), DEPTH * HEADS["A"])),
                                        (router[:], w_router[0].rearrange("(k p) e -> p k e", p=P))):
                            sp.dma_start(to, src).then_inc(s_const, 16)
                    for kh in range(2):
                        static(u + U_IN + 2 * cg + kh, square(w_in[l], kh, cg))
                        if l == 0 and cg == 0 and kh == 0:
                            load_x(1)
                for ch in range(2):
                    for kh in range(2):
                        static(u + U_BR + 2 * ch + kh, square(w_br[l], kh, ch))
                for kh in range(2):
                    for ch in range(2):
                        static(u + U_OUT + 2 * kh + ch, square(w_out[l], kh, ch))

            mixer_stream(0)
            wg, wu, wd = w_ff_gate[0], w_ff_up[0], w_ff_down[0]
            n = MIX_UNITS
            for g in range(3):
                static(n, gate_up(wg, wu, 0, g))
                static(n + 1, gate_up(wg, wu, 1, g))
                n += 2
                if g:
                    static(n, down(wd, g - 1))
                    n += 1
            with sp.Fori(0, (DENSE_G - 3) // 2) as pair:
                for q in range(2):
                    g = pair * 2 + (3 + q)
                    for j, parts in enumerate((gate_up(wg, wu, 0, g), gate_up(wg, wu, 1, g), down(wd, g - 1))):
                        fill(n + 3 * q + j, pair * RAW + (n + 3 * q + j - RAW + 1), parts)
            n += 3 * (DENSE_G - 3)
            static(n, down(wd, DENSE_G - 1))
            mixer_stream(1)

            def item_stream(i, e):
                wg, wu, wd = w_moe_gate[0, e], w_moe_up[0, e], w_moe_down[0, e]

                def at(j, parts):
                    fill(MOE_U0 + j, moe_unit(i, j - RAW + 1), parts)

                at(0, gate_up(wg, wu, 0, 0))
                at(1, gate_up(wg, wu, 1, 0))
                at(2, gate_up(wg, wu, 0, 1))
                at(3, gate_up(wg, wu, 1, 1))
                at(4, down(wd, 0))
                with sp.Fori(0, EXPERT_G // 2 - 1) as pair:
                    for q in range(2):
                        g = pair * 2 + (2 + q)
                        for j, parts in enumerate((gate_up(wg, wu, 0, g), gate_up(wg, wu, 1, g), down(wd, g - 1))):
                            j += 5 + 3 * q
                            fill(MOE_U0 + j, pair * RAW + moe_unit(i, j - RAW + 1), parts)
                at(ITEM_UNITS - 1, down(wd, EXPERT_G - 1))

            with sp.Fori(0, N_EXP) as e:
                item_stream(e, e)
            sp.wait_ge(s_meta, 1)
            items = sp.value_load(meta[0:1, 0:1], min_val=N_EXP, max_val=ITEMS)
            with sp.If(items > N_EXP):
                with sp.Fori(N_EXP, items) as i:
                    e = sp.value_load(meta[0:1, bass.ds(i - (N_EXP - 1), 1)], min_val=0, max_val=N_EXP - 1)
                    item_stream(i, e)
            for t in range(TB):
                for ch in range(2):
                    a = slice(ch * COL, (ch + 1) * COL)
                    sp.wait_ge(s_y[ch], t + 1)
                    sp.dma_start(out[0, t * P:(t + 1) * P, a], h_tok[:, t, a]).then_inc(s_out, 16)
            sp.wait_ge(s_out, 16 * 2 * TB)

        @block.gpsimd
        def _(pool):
            def row(a, n):
                return a.rearrange("(o c) -> o c", o=1).broadcast_to([P, n])

            for n, g in ((1, norm_ffn[0]), (2, norm_mix[1]), (3, norm_ffn[1]), (4, norm_final)):
                pool.wait_ge(s_xg, 4 * n)
                if n % 2:
                    pool.wait_ge(s_o, NSTEP * (n + 1) // 2)
                pool.dma_start(gain, row(g, D)).then_inc(s_gain, 16)
                if n == 3:
                    pool.dma_start(route, c_route).then_inc(s_route, 16)

            E = N_EXP
            steps = [0]

            def link(ins):
                steps[0] += 1
                ins.then_inc(s_pool, 1)
                pool.wait_ge(s_pool, steps[0])

            def over(a, n):
                return a.rearrange("p (o k) -> p o k", o=1).broadcast_to([P, n, a.shape[1]])

            def sum_experts(to, a):
                n = N_EXP // 2
                while n > 1:
                    link(pool.tensor_tensor(a[..., 0:n], a[..., 0:n], a[..., n:2 * n], ALU.add))
                    n //= 2
                link(pool.tensor_tensor(to, a[..., 0:1], a[..., 1:2], ALU.add))

            pool.wait_ge(s_hth, 1)
            link(pool.tensor_scalar(h_tok[:, 0, :], h_tok[:, 0, :], rstd[:, 0:1], None, ALU.mult))
            pool.tensor_tensor(htok_lo[:, 0, :], h_tok[:, 0, :], htok_hi[:, 0, :].bitcast(F32), ALU.subtract).then_inc(s_htl, 1)

            pool.wait_ge(s_over, 1)
            pool.tensor_scalar(r_meta[:, 0:1], r_cum[:, E - 1:E], float(E), None, ALU.add)
            link(pool.tensor_scalar(r_slot, r_rank, -1.0 - P, None, ALU.add))
            for j in range(OVER):
                link(pool.tensor_scalar(r_hot, r_cum, float(j + 1), None, ALU.is_equal))
                link(pool.tensor_tensor(r_hot, r_hot, r_over, ALU.mult))
                for src, to in ((r_slot, item_slot), (r_w, item_w)):
                    link(pool.tensor_tensor(r_t, src, over(r_hot, TB), ALU.mult))
                    sum_experts(to[:, :, E + j:E + j + 1], r_t)
                link(pool.tensor_tensor(r_hot, r_hot, c_expert, ALU.mult))
                sum_experts(r_meta[:, 1 + j:2 + j], r_hot)
            pool.tensor_copy(meta[:], r_meta[0:1, :]).then_inc(s_meta, 1)

        @block.tensor
        def _(pe):
            def product(to, l_hi, l_lo, r_hi, r_lo, first, last):
                pe.matmul(to, l_hi, r_hi, start=first, stop=False)
                pe.matmul(to, l_hi, r_lo, start=False, stop=False)
                return pe.matmul(to, l_lo, r_hi, start=False, stop=last)

            def tile(u, k):
                s = u % SPLIT
                return w_hi[:, s, k * COL:(k + 1) * COL], w_lo[:, s, k * COL:(k + 1) * COL]

            def square(u, kh, banks, between=None):
                pe.wait_ge(s_lo, u + 1)
                for t, to in enumerate(banks):
                    for k in range(4):
                        if between:
                            between(t, k)
                        kt = 4 * kh + k
                        last = product(to[:], t_hi[:, kt, t * P:(t + 1) * P], t_lo[:, kt, t * P:(t + 1) * P],
                                       *tile(u, k), kt == 0, kt == KT - 1)
                    if t == TB - 1:
                        last.then_inc(s_used, 1)
                    if between:
                        between(t, 4)

            def transpose_act(call, half, src):
                for b in (2 * half, 2 * half + 1):
                    for k in range(2):
                        for t in range(TB):
                            last = pe.transpose(tr_bank(call, b)[:, (2 * k + t) * P:(2 * k + t + 1) * P],
                                                src[:, t, (2 * b + k) * P:(2 * b + k + 1) * P], ident[:])
                    last.then_inc(s_tr, 1)

            warm = w_hi[:, 0, 0:COL]

            def transpose_stream(n, halves=(0, 1)):
                for half in halves:
                    if n == 3 and half:
                        keep_warm(WARM_HALF, bank[4], warm)
                    pe.wait_ge(s_xg, 4 * n + 2 * half + 2)
                    transpose_act(norm_call(n), half, h_tok)
                pe.wait_ge(s_trl, 4 * norm_call(n) + 2)

            def keep_warm(n, free, filled):
                for _ in range(n):
                    pe.matmul(free[:], filled[:, 0:P], filled, start=True, stop=True)

            def qk_bank(l, b):
                if b == 0:
                    pe.wait_ge(s_rope, 3 * l + 1)
                if b == 2:
                    pe.wait_ge(s_rope, 3 * l + 2)
                if b == 4:
                    pe.wait_ge(s_rope, 3 * l + 3)
                if b >= 4:
                    pe.wait_ge(s_qkc, QKT_BANKS * l + b - 3)
                for j in range(2):
                    at = (2 * b + j) * 2 * DH
                    for t in range(TB):
                        last = pe.transpose(bank[4 + b % 4][:, (2 * j + t) * P:(2 * j + t + 1) * P],
                                            qk[:, t, at:at + 2 * DH], ident[:])
                last.then_inc(s_qkt, 1)

            def halves_before(l, k):
                both = [len({head_place(b, h)[1] for h in hs}) > 1 for b, _, hs in STEPS]
                return l * sum(both) + sum(both[:k])

            def scores(l, k, part):
                br, t, heads = STEPS[k]
                n = (t + 1) * P
                places = [(j, *head_place(br, h)[:4]) for j, h in enumerate(heads)]
                halves = sorted({qh for _, _, qh, _, _ in places})
                if part >= len(halves):
                    return
                if part == 0:
                    if k == 0:
                        pe.wait_ge(s_qkc, QKT_BANKS * (l + 1))
                    if k >= 2:
                        pe.wait_ge(s_sm, NSTEP * l + k - 1)
                else:
                    pe.wait_ge(s_half, halves_before(l, k) + 1)
                for j, qb, qh, kb, kh in places:
                    if qh == halves[part]:
                        last = pe.matmul(bank[4 + k % 2][:, j * n:(j + 1) * n], qkT[qh * DH:(qh + 1) * DH, qb, t * P:(t + 1) * P],
                                         qkT[kh * DH:(kh + 1) * DH, kb, 0:n], start=True, stop=True)
                last.then_inc(s_sc if part == len(halves) - 1 else s_half, 1)

            def prob_transpose(l, k):
                _, t, heads = STEPS[k]
                pe.wait_ge(s_p, NSTEP * l + k + 1)
                if k:
                    pe.wait_ge(s_ptc, NSTEP * l + k)
                for b in range(len(heads) * (t + 1)):
                    last = pe.transpose(bank[6][:, b * P:(b + 1) * P], score[k % 3][:, b * P:(b + 1) * P], ident[:])
                last.then_inc(s_pt, 1)

            def weigh_values(l, k):
                br, t, heads = STEPS[k]
                pe.wait_ge(s_ptc, NSTEP * l + k + 1)
                if k:
                    pe.wait_ge(s_o, NSTEP * l + k)
                for j, h in enumerate(heads):
                    v = head_place(br, h)[4]
                    for kb in range(t + 1):
                        b = j * (t + 1) + kb
                        last = pe.matmul(bank[7][:, j * DH:(j + 1) * DH], probT[:, b * P:(b + 1) * P],
                                         val[:, kb, v:v + DH], start=kb == 0, stop=kb == t)
                last.then_inc(s_pv, 1)

            def attention_part(l, r, k):
                if k == 0 and r < NSTEP:
                    scores(l, r, 0)
                if k == 1 and r < NSTEP:
                    scores(l, r, 1)
                if k == 4 and 0 <= r - LAG_PV < NSTEP:
                    weigh_values(l, r - LAG_PV)
                if k == 4 and 0 <= r - LAG_PT < NSTEP:
                    prob_transpose(l, r - LAG_PT)

            def mixer(l):
                u = unit0(l)
                if l == 0:
                    pe.wait_ge(s_ident, 16)
                transpose_stream(2 * l, (0, 1) if l else (0,))
                if l == 0:
                    keep_warm(WARM_START, bank[7], t_hi[:, 0:2, :].rearrange("p k t -> p (k t)"))
                for j in range(2 * IN_CG):
                    cg = j // 2
                    if j == 1:
                        pe.wait_ge(s_trl, 16 * l + 4)
                    if j % 2 == 0 and cg >= 2:
                        pe.wait_ge(s_evac, 2 * IN_CG * l + 2 * (cg - 2) + 2)

                    def between(t, k):
                        if (l, j, t, k) == (0, 0, 0, 4):
                            transpose_stream(0, (1,))
                        if j >= ATT_SLOT:
                            attention_part(l, 2 * (j - ATT_SLOT) + t, k)
                        if (j, t, k) == (2 * IN_CG - 1, 0, 4):
                            pe.wait_ge(s_o, NSTEP * l + FIRST_HALF_STEPS)
                            pe.wait_ge(s_sm, NSTEP * (l + 1))
                            transpose_act(4 * l + 1, 0, o_tok)

                    square(u + j, j % 2, [bank[(2 * cg + t) % 4] for t in range(TB)], between)
                    if j in QKT_SLOT:
                        for b in range(*QKT_SLOT[j]):
                            qk_bank(l, b)
                pe.wait_ge(s_o, NSTEP * (l + 1))
                transpose_act(4 * l + 1, 1, o_tok)
                bounds = (0, 3, 5, 8)
                for j in range(4):
                    ch, kh = j // 2, j % 2
                    if j < 2:
                        pe.wait_ge(s_trl, 16 * l + 4 + 2 * kh + 2)
                    pe.wait_ge(s_lo, u + U_BR + j + 1)
                    for t in ((1, 0) if j == 0 else (0, 1)):
                        if j == 0:
                            pe.wait_ge(s_evac, 2 * IN_CG * (l + 1) - (2 if t else 0))
                        if ch and t == 1 and kh == 0:
                            pe.wait_ge(s_mg, 4 * l + 1)
                        if ch and kh == 1:
                            pe.wait_ge(s_mg, 4 * l + 1 + t)
                        for kt in range(4 * kh, 4 * kh + 4):
                            br = next(b for b in range(3) if kt < bounds[b + 1])
                            last = product(bank[(6 * ch + 3 * t + br) % 8][:], t_hi[:, kt, t * P:(t + 1) * P],
                                           t_lo[:, kt, t * P:(t + 1) * P], *tile(u + U_BR + j, kt % 4),
                                           kt == bounds[br], kt == bounds[br + 1] - 1)
                        if j == 3 and t == 0:
                            pe.wait_ge(s_mg, 4 * l + 2)
                            transpose_act(4 * l + 2, 0, gates)
                    last.then_inc(s_used, 1)
                pe.wait_ge(s_trl, 16 * l + 8 + 2)
                square(u + U_OUT, 0, out_bank[0])
                pe.wait_ge(s_mg, 4 * l + 3)

                def second_half(t, k):
                    if (t, k) == (0, 4):
                        pe.wait_ge(s_mg, 4 * l + 4)
                        transpose_act(4 * l + 2, 1, gates)

                square(u + U_OUT + 1, 0, out_bank[1], second_half)
                pe.wait_ge(s_trl, 16 * l + 8 + 4)
                for ch in range(2):
                    square(u + U_OUT + 2 + ch, 1, out_bank[ch])

            def gate_up(u, kh, par, tbs, l_hi, l_lo, ready):
                pe.wait_ge(s_lo, ready)
                for t in range(tbs):
                    for k in range(4):
                        kt = 4 * kh + k
                        last = product(bank[2 * par + t if tbs > 1 else par][:], l_hi[:, kt, t * P:(t + 1) * P],
                                       l_lo[:, kt, t * P:(t + 1) * P], *tile(u, k), kt == 0, kt == KT - 1)
                last.then_inc(s_used, 1)

            def act_transpose(par, tbs, ready):
                pe.wait_ge(s_act, ready)
                for f in range(2):
                    for t in range(tbs):
                        last = pe.transpose(bank[2 * par if tbs > 1 else par][:, (tbs * f + t) * P:(tbs * f + t + 1) * P],
                                            act_tok[:, par, t, f * P:(f + 1) * P], ident[:])
                last.then_inc(s_at, 1)

            def down(u, par, tbs, acc, ready_a, ready, first, last_group, halves=False):
                pe.wait_ge(s_atl, ready_a)
                pe.wait_ge(s_lo, ready)
                for ch in range(2):
                    for t in range(tbs):
                        for f in range(2):
                            a = (tbs * f + t) * P
                            last = product(acc(t, ch)[:], aT_hi[:, par, a:a + P], aT_lo[:, par, a:a + P],
                                           *tile(u, 2 * f + ch), first and f == 0, last_group and f == 1)
                    if halves and ch == 0:
                        last.then_inc(s_dh, 1)
                last.then_inc(s_used, 1)

            def group(u, uval, par, tbs, acc, l_hi, l_lo, done, k, first, parts=None):
                gate_up(u, 0, par, tbs, l_hi, l_lo, uval + 1)
                if parts is not None:
                    pe.wait_ge(*parts)
                if k:
                    act_transpose(1 - par, tbs, done)
                gate_up(u + 1, 1, par, tbs, l_hi, l_lo, uval + 2)
                if k:
                    down(u + 2, 1 - par, tbs, acc, done, uval + 3, first, False)

            mixer(0)
            transpose_stream(1)

            def acc2(t, ch):
                return bank[4 + 2 * ch + t]

            n = MIX_UNITS
            for g in range(3):
                group(n, n, g % 2, TB, acc2, t_hi, t_lo, g, g, g == 1, (s_trl, 4 * 3 + 4) if g == 0 else None)
                n += 3 if g else 2
            with pe.Fori(0, (DENSE_G - 3) // 2) as pair:
                for q in range(2):
                    group(n + 3 * q, pair * RAW + (n + 3 * q), (3 + q) % 2, TB, acc2, t_hi, t_lo, pair * 2 + (3 + q), 1, False)
            n += 3 * (DENSE_G - 3)
            act_transpose((DENSE_G - 1) % 2, TB, DENSE_G)
            down(n, (DENSE_G - 1) % 2, TB, acc2, DENSE_G, n + 1, False, True, halves=True)

            mixer(1)
            transpose_stream(3)
            pe.wait_ge(s_rw, 2)
            n_log = 2 * N_EXP
            for kt in range(KT):
                if kt == KT // 2:
                    pe.wait_ge(s_trl, 4 * 7 + 4)
                pe.matmul(bank[0][0:n_log, 0:T], router_parts[:, kt, :], t_hi[:, kt, :], start=kt == 0, stop=False)
                last = pe.matmul(bank[0][0:n_log, 0:T], router_parts[:, kt, :], t_lo[:, kt, :], start=False, stop=kt == KT - 1)
            last.then_inc(s_logT, 1)
            pe.wait_ge(s_logc, 1)
            for t in range(TB):
                last = pe.transpose(bank[1][:, t * n_log:(t + 1) * n_log], logits_T[:, t * P:(t + 1) * P],
                                    ident[0:n_log, 0:n_log])
            last.then_inc(s_log, 1)
            keep_warm(WARM_CHOICE, bank[6], warm)
            pe.wait_ge(s_sel, 1)
            pe.wait_ge(s_route, 16)
            E = N_EXP
            pe.matmul(bank[7][:, 0:E], c_before, r_sel[:, 0, :], start=True, stop=True)
            pe.matmul(bank[7][:, E:2 * E], c_ones, r_sel[:, 0, :], start=True, stop=False)
            pe.matmul(bank[7][:, E:2 * E], c_before, r_sel[:, 1, :], start=False, stop=True).then_inc(s_rank, 1)
            pe.matmul(bank[3][:, 0:E], c_ones, r_sel[:, 0, :], start=True, stop=False)
            pe.matmul(bank[3][:, 0:E], c_ones, r_sel[:, 1, :], start=False, stop=True).then_inc(s_count, 1)
            keep_warm(WARM_RANK, bank[6], warm)
            pe.wait_ge(s_htl, TB)

            def acc1(t, ch):
                return bank[2 + ch]

            def gather(i):
                pe.wait_ge(s_pick, i + 1)
                for b in range(2):
                    for j in range(4):
                        d = 4 * b + j
                        to = bank[4 + b][:, j * P:(j + 1) * P]
                        for t in range(TB):
                            pe.matmul(to, htok_hi[:, t, d * P:(d + 1) * P], pick[:, t, :], start=t == 0, stop=False)
                            last = pe.matmul(to, htok_lo[:, t, d * P:(d + 1) * P], pick[:, t, :], start=False, stop=t == 1)
                    last.then_inc(s_ga, 1)

            def first_group(i, j):
                pe.wait_ge(s_gal, i * 2 + 1)
                group(MOE_U0 + j, moe_unit(i, 0), 0, 1, acc1, xg_hi, xg_lo, ff0(i), 0, False, (s_gal, i * 2 + 2))

            def head(i):
                pe.wait_ge(s_xs, xs_before_item(i))
                gather(i)
                first_group(i, 0)

            def middle(i):
                group(MOE_U0 + 2, moe_unit(i, 2), 1, 1, acc1, xg_hi, xg_lo, ff0(i) + 1, 1, True)
                pe.wait_ge(s_xs, xs_before_item(i))
                pe.wait_ge(s_pickw, i + 1)
                for t in range(TB):
                    last = pe.transpose(bank[4][:, t * P:(t + 1) * P], pick_w[:, t, :], ident[:])
                last.then_inc(s_bk, 1)
                with pe.Fori(0, EXPERT_G // 2 - 1) as pair:
                    for q in range(2):
                        group(MOE_U0 + 5 + 3 * q, pair * RAW + moe_unit(i, 5 + 3 * q), q, 1, acc1, xg_hi, xg_lo,
                              pair * 2 + (ff0(i) + (2 + q)), 1, False)

            def last_down(i):
                down(MOE_U0 + ITEM_UNITS - 1, 1, 1, acc1, ff0(i + 1), moe_unit(i, ITEM_UNITS), False, True)

            def combine(i):
                pe.wait_ge(s_bkl, i + 1)
                for ch in range(2):
                    pe.wait_ge(s_yl, i * 2 + (ch + 1))
                    for t in range(TB):
                        product(bank[4 + 2 * ch + t][:], back_hi[:, t * P:(t + 1) * P], back_lo[:, t * P:(t + 1) * P],
                                y_hi[:, ch * COL:(ch + 1) * COL], y_lo[:, ch * COL:(ch + 1) * COL],
                                True, True).then_inc(s_cmb, 1)

            head(0)
            with pe.Fori(0, N_EXP - 1) as i:
                middle(i)
                pe.wait_ge(s_bkl, i + 1)
                act_transpose(1, 1, ff0(i + 1))
                gather(i + 1)
                last_down(i)
                first_group(i + 1, ITEM_UNITS)
                combine(i)
            middle(N_EXP - 1)
            act_transpose(1, 1, ff0(N_EXP))
            last_down(N_EXP - 1)
            combine(N_EXP - 1)
            pe.wait_ge(s_meta, 1)
            items = pe.value_load(meta[0:1, 0:1], min_val=N_EXP, max_val=ITEMS)
            with pe.If(items > N_EXP):
                with pe.Fori(N_EXP, items) as i:
                    head(i)
                    middle(i)
                    act_transpose(1, 1, ff0(i + 1))
                    last_down(i)
                    combine(i)

        @block.scalar
        def _(act):
            def split(u, turns, used):
                act.wait_ge(s_raw[u % RAW], turns)
                if used is not None:
                    act.wait_ge(s_used, used)
                act.copy(w_hi[:, u % SPLIT, :], raw_ring[:, u % RAW, :]).then_inc(s_hi, 1)

            def static(u):
                split(u, 32 * raw_turn(u), u - SPLIT + 1 if u >= SPLIT else None)

            def fetch_table(func):
                act.activation(unread[:], ident[:, 0:1], func)

            def norm_squares(n, ch):
                act.wait_ge(*((s_xs, xs_before(n) - 2 + 2 * ch) if n else (s_x[ch], 16)))
                for t in range(TB):
                    a = (2 * ch + t) * COL
                    act.activation(squares[:, a:a + COL], xs[:, t, ch * COL:(ch + 1) * COL], ACT.Square,
                                   accum_out=ssq[:, ch, t:t + 1]).then_inc(s_ssq, 1)

            def norm_root(n):
                act.wait_ge(s_var, n + 1)
                act.activation(std[:], var[:], ACT.Sqrt).then_inc(s_std, 1)

            def round_transposed(call, half):
                for b in (2 * half, 2 * half + 1):
                    act.wait_ge(s_tr, 4 * call + b + 1)
                    act.copy(t_hi[:, 2 * b:2 * b + 2, :].rearrange("p k t -> p (k t)"), tr_bank(call, b)[:]).then_inc(s_trh, 1)

            def project_copy(l, cg, used):
                act.wait_ge(s_used, used)
                if cg == 0:
                    act.wait_ge(s_rstd, 2 * l + 1)
                for t in range(TB):
                    src, scale = bank[(2 * cg + t) % 4], rstd[:, t:t + 1]
                    if cg < QKV_CG:
                        for a, what, to, n in in_pieces(cg):
                            dst, src_a = (qk if what == "qk" else val)[:, t, to:to + n], src[:, a:a + n]
                            if cg == 0:
                                nq = HEADS["A"] * DH
                                act.activation(dst[:, 0:nq].rearrange("p (i s c) -> p s i c", s=2, c=DH),
                                               src_a[:, 0:nq].rearrange("p (s i c) -> p s i c", s=2, c=DH),
                                               ACT.Copy, scale=scale)
                                dst, src_a = dst[:, nq:n], src_a[:, nq:n]
                            last = act.activation(dst, src_a, ACT.Copy, scale=scale)
                    else:
                        if cg == IN_CG - 1 and t == 1:
                            act.wait_ge(s_rope, 3 * l + 3)
                        a = (cg - QKV_CG) * COL
                        last = act.activation(gates[:, t, a:a + COL], src[:], ACT.Copy, scale=scale)
                    last.then_inc(s_evac, 1)

            def sigmoids(l, ch):
                act.wait_ge(s_evac, 2 * IN_CG * (l + 1) - 2 + 2 * ch)
                for t in range(TB):
                    g = gates[:, t, :].rearrange("p (b c) -> p b c", b=3)[:, :, ch * COL:(ch + 1) * COL]
                    act.activation(g, g, ACT.Sigmoid).then_inc(s_gate, 1)

            def qk_copy(l, b):
                act.wait_ge(s_qkt, QKT_BANKS * l + b + 1)
                act.copy(qkT[:, 2 * b:2 * b + 2, :].rearrange("p k t -> p (k t)"), bank[4 + b % 4][:]).then_inc(s_qkc, 1)

            def exponentials(l, k):
                br, t, heads = STEPS[k]
                n = (t + 1) * P
                act.wait_ge(s_nm, NSTEP * l + k + 1)
                for j in range(len(heads)):
                    s = score[k % 3][:, j * n:(j + 1) * n]
                    last = act.activation(s, s, ACT.Exp, bias=nmx[:, k % 4, j:j + 1], accum_out=den[:, k % 4, j:j + 1])
                if br == "A":
                    nh = len(heads)
                    last = act.activation(sink_e[:, k % 4, 0:nh], sink_d[:, k % 4, 0:nh], ACT.Exp)
                last.then_inc(s_p, 1)

            def prob_copy(l, k):
                _, t, heads = STEPS[k]
                n = len(heads) * (t + 1) * P
                act.wait_ge(s_pt, NSTEP * l + k + 1)
                if k:
                    act.wait_ge(s_pv, NSTEP * l + k)
                act.copy(probT[:, 0:n], bank[6][:, 0:n]).then_inc(s_ptc, 1)

            def mixer(l):
                u = unit0(l)
                norm_squares(2 * l, 0)
                norm_squares(2 * l, 1)
                norm_root(2 * l)
                for j in range(2 * IN_CG):
                    if j >= ATT_SLOT:
                        for r in (2 * (j - ATT_SLOT), 2 * (j - ATT_SLOT) + 1):
                            if r < NSTEP:
                                exponentials(l, r)
                            if 0 <= r - LAG_PT < NSTEP:
                                prob_copy(l, r - LAG_PT)
                    if j == 2 * IN_CG - 1:
                        round_transposed(4 * l + 1, 0)
                    if j % 2 == 1:
                        project_copy(l, j // 2, u + j + 1)
                    if j in QKT_SLOT:
                        for b in range(*QKT_SLOT[j]):
                            qk_copy(l, b)
                    if j == 2 * IN_CG - 1:
                        round_transposed(4 * l + 1, 1)
                    static(u + j + SPLIT)
                    if j == 2 * IN_CG - 2:
                        sigmoids(l, 0)
                sigmoids(l, 1)
                for j in range(U_BR, MIX_UNITS):
                    if j == U_BR + 3:
                        round_transposed(4 * l + 2, 0)
                    if j == U_OUT + 1:
                        round_transposed(4 * l + 2, 1)
                    if j == MIX_UNITS - 1:
                        norm_squares(2 * l + 1, 0)
                        fetch_table(ACT.Sqrt)
                        if l == 0:
                            static(u + j + SPLIT)
                        for half in range(2):
                            round_transposed(4 * l + 3, half)
                        norm_squares(2 * l + 1, 1)
                        norm_root(2 * l + 1)
                    else:
                        static(u + j + SPLIT)

            def silu(par, tbs, used):
                act.wait_ge(s_used, used)
                for t in range(tbs):
                    scale = rstd[:, t:t + 1] if tbs > 1 else 1.0
                    last = act.activation(sil[:, par, t, :], bank[2 * par + t if tbs > 1 else par][:, 0:FG], ACT.Silu,
                                          scale=scale)
                last.then_inc(s_sil, 1)

            def round_act(par, tbs, ready):
                n = 2 * tbs * P
                act.wait_ge(s_at, ready)
                act.copy(aT_hi[:, par, 0:n], bank[2 * par if tbs > 1 else par][:, 0:n]).then_inc(s_ath, 1)

            def turn(split_at, k, par, tbs, uval, done, last=False, down_too=True):
                if k:
                    round_act(1 - par, tbs, done)
                split_at(3)
                silu(par, tbs, uval + 2)
                if not last:
                    split_at(4)
                    if k and down_too:
                        split_at(5)

            round_transposed(0, 0)
            static(0)
            static(1)
            round_transposed(0, 1)
            static(2)
            mixer(0)
            act.wait_ge(s_const, 64)
            act.copy(router_hi, router[:]).then_inc(s_rw, 1)
            act.wait_ge(s_rstd, 2)
            n = MIX_UNITS
            for g in range(3):
                turn(lambda j: static(n + j), g, g % 2, TB, n, g)
                n += 3 if g else 2
            with act.Fori(0, (DENSE_G - 5) // 2) as pair:
                for q in range(2):
                    v = n + 3 * q
                    turn(lambda j: split(v + j, pair * 32 + 32 * raw_turn(v + j), pair * RAW + (v + j - SPLIT + 1)),
                         1, (3 + q) % 2, TB, pair * RAW + v, pair * 2 + (3 + q))
            n += 3 * (DENSE_G - 5)
            for g in (DENSE_G - 2, DENSE_G - 1):
                turn(lambda j: static(n + j), 1, g % 2, TB, n, g, down_too=g < DENSE_G - 1)
                n += 3
            round_act((DENSE_G - 1) % 2, TB, DENSE_G)
            static(n + SPLIT - 1)
            static(n + SPLIT)
            for half in range(2):
                round_transposed(4, half)
            mixer(1)
            act.wait_ge(s_logT, 1)
            act.wait_ge(s_rstd, 4)
            for t in range(TB):
                act.activation(htok_hi[:, t, :], h_tok[:, t, :], ACT.Copy, scale=rstd[:, t:t + 1]).then_inc(s_hth, 1)
            static(MOE_U0 + SPLIT - 1)
            act.wait_ge(s_rexpin, 1)
            act.activation(r_e, r_c, ACT.Exp).then_inc(s_rexp, 1)
            fetch_table(ACT.Silu)

            def split_at(i, j, pair=None):
                turns, used = moe_turn(i, j) * 32, moe_unit(i, j - SPLIT + 1)
                if pair is not None:
                    turns, used = pair * 32 + turns, pair * RAW + used
                split(MOE_U0 + j, turns, used)

            def round_gathered(i):
                for b in range(2):
                    act.wait_ge(s_ga, i * 2 + (b + 1))
                    act.copy(xg_hi[:, 4 * b:4 * b + 4, :].rearrange("p k t -> p (k t)"), bank[4 + b][:]).then_inc(s_gah, 1)

            def head(i):
                if not isinstance(i, int):
                    for j in range(SPLIT):
                        split_at(i, j)
                round_gathered(i)
                turn(lambda j: split_at(i, j), 0, 0, 1, moe_unit(i, 0), ff0(i))

            def middle(i):
                turn(lambda j: split_at(i, 2 + j), 1, 1, 1, moe_unit(i, 2), ff0(i) + 1)
                act.wait_ge(s_bk, i + 1)
                act.copy(back_hi[:], bank[4][:, 0:T]).then_inc(s_bkh, 1)
                with act.Fori(0, EXPERT_G // 2 - 2) as pair:
                    for q in range(2):
                        v = 5 + 3 * q
                        turn(lambda j: split_at(i, v + j, pair), 1, q, 1, pair * RAW + moe_unit(i, v), pair * 2 + (ff0(i) + (2 + q)))
                turn(lambda j: split_at(i, TAIL - 3 + j), 1, 0, 1, moe_unit(i, TAIL - 3), ff0(i) + (EXPERT_G - 2))
                turn(lambda j: split_at(i, TAIL + j), 1, 1, 1, moe_unit(i, TAIL), ff0(i) + (EXPERT_G - 1), last=True)

            def round_output(i):
                act.wait_ge(s_used, moe_unit(i, ITEM_UNITS))
                for ch in range(2):
                    act.copy(y_hi[:, ch * COL:(ch + 1) * COL], bank[2 + ch][:]).then_inc(s_yh, 1)

            head(0)
            with act.Fori(0, N_EXP - 1) as i:
                middle(i)
                split_at(i, ITEM_UNITS)
                round_act(1, 1, ff0(i + 1))
                split_at(i, ITEM_UNITS + 1)
                round_gathered(i + 1)
                round_output(i)
                split_at(i, ITEM_UNITS + 2)
                turn(lambda j: split_at(i, ITEM_UNITS + j), 0, 0, 1, moe_unit(i, ITEM_UNITS), ff0(i + 1))
            middle(N_EXP - 1)
            round_act(1, 1, ff0(N_EXP))
            round_output(N_EXP - 1)
            act.wait_ge(s_meta, 1)
            items = act.value_load(meta[0:1, 0:1], min_val=N_EXP, max_val=ITEMS)
            with act.If(items > N_EXP):
                with act.Fori(N_EXP, items) as i:
                    head(i)
                    middle(i)
                    round_act(1, 1, ff0(i + 1))
                    round_output(i)
            fetch_table(ACT.Sqrt)
            for ch in range(2):
                for t in range(TB):
                    act.wait_ge(s_xs, xs_before_item(items - 1) + (2 * ch + t + 1))
                    a = (2 * ch + t) * COL
                    act.activation(squares[:, a:a + COL], xs[:, t, ch * COL:(ch + 1) * COL], ACT.Square,
                                   accum_out=ssq[:, ch, t:t + 1]).then_inc(s_ssq, 1)
            act.wait_ge(s_var, 5)
            act.activation(std[:], var[:], ACT.Sqrt).then_inc(s_std, 1)
            act.wait_ge(s_rstd, 5)
            act.wait_ge(s_xg, 4 * 4 + 2)
            for t in range(TB):
                act.activation(h_tok[:, t, 0:COL], h_tok[:, t, 0:COL], ACT.Copy, scale=rstd[:, t:t + 1]).then_inc(s_y[0], 1)

        @block.vector
        def _(dve):
            steps = [0]

            def link(ins):
                steps[0] += 1
                ins.then_inc(s_dve, 1)
                dve.wait_ge(s_dve, steps[0])

            def each(a, n):
                return a.rearrange("p (k o) -> p k o", o=1).broadcast_to([P, a.shape[1], n])

            def over(a, n):
                return a.rearrange("p (o k) -> p o k", o=1).broadcast_to([P, n, a.shape[1]])

            def split(u, rounded):
                dve.wait_ge(s_hi, rounded)
                s = u % SPLIT
                dve.tensor_tensor(w_lo[:, s, :], raw_ring[:, u % RAW, :], w_hi[:, s, :].bitcast(F32),
                                  ALU.subtract).then_inc(s_lo, 1)

            def static(u):
                split(u, u + 1)

            def norm(n):
                dve.wait_ge(s_ssq, 4 * n + 4)
                link(dve.tensor_tensor(ssum[:], ssq[:, 0, :], ssq[:, 1, :], ALU.add))
                dve.tensor_scalar(var[:], ssum[:], 1.0 / D, EPS, ALU.mult, ALU.add).then_inc(s_var, 1)
                dve.wait_ge(s_std, n + 1)
                dve.reciprocal(rstd[:], std[:]).then_inc(s_rstd, 1)

            def times_gain(n, ch, wait_stream=True):
                if ch == 0:
                    dve.wait_ge(*((s_gain, 16 * n) if n else (s_gain0, 16)))
                if wait_stream:
                    dve.wait_ge(*((s_xs, 4 * n - 2 + 2 * ch) if n else (s_x[ch], 16)))
                a = slice(ch * COL, (ch + 1) * COL)
                for t in range(TB):
                    dve.tensor_tensor(h_tok[:, t, a], xs[:, t, a], gain[:, a], ALU.mult).then_inc(s_xg, 1)

            def split_transposed(call, half):
                for b in (2 * half, 2 * half + 1):
                    dve.wait_ge(s_trh, 4 * call + b + 1)
                    to = slice(2 * b, 2 * b + 2)
                    dve.tensor_tensor(t_lo[:, to, :].rearrange("p k t -> p (k t)"), tr_bank(call, b)[:],
                                      t_hi[:, to, :].bitcast(F32).rearrange("p k t -> p (k t)"),
                                      ALU.subtract).then_inc(s_trl, 1)

            def split_before_transposed(u, call, half):
                if half:
                    split_transposed(call, 0)
                static(u)
                if half:
                    split_transposed(call, 1)

            def apply_rope(l, br):
                end = IN_AT[br] + (HEADS[br] + KV[br]) * DH
                dve.wait_ge(s_evac, 2 * IN_CG * l + 2 * -(-end // COL))
                heads = HEADS[br] + KV[br]
                n = 8 if heads == 8 else heads // 2
                half = DH // 2
                for t in range(TB):
                    for a in range(QK_AT[br], QK_AT[br] + heads * DH, n * DH):
                        z = qk[:, t, a:a + n * DH].rearrange("p (n c) -> p n c", n=n)
                        tmp = rope_tmp[:, 0:n * DH].rearrange("p (n c) -> p n c", n=n)
                        cos, sin = rope[:, t, 0, :], rope[:, t, 1, :]
                        dve.tensor_tensor(tmp[:, :, 0:half], z[:, :, half:DH], over(sin[:, 0:half], n), ALU.mult)
                        link(dve.tensor_tensor(tmp[:, :, half:DH], z[:, :, 0:half], over(sin[:, half:DH], n), ALU.mult))
                        link(dve.tensor_tensor(z, z, over(cos, n), ALU.mult))
                        link(dve.tensor_tensor(z, z, tmp, ALU.add))
                dve.sem_inc(s_rope, 1)

            def mask_and_max(l, k):
                br, t, heads = STEPS[k]
                nh, n, b = len(heads), (t + 1) * P, k % 4
                dve.wait_ge(s_sc, NSTEP * l + k + 1)
                if k >= 3:
                    dve.wait_ge(s_pt, NSTEP * l + k - 2)
                for j in range(nh):
                    last = dve.tensor_tensor_reduce(score[k % 3][:, j * n:(j + 1) * n], bank[4 + k % 2][:, j * n:(j + 1) * n],
                                                    mask[:, "ABC".index(br), T - n:T], SCALE, -3e38, ALU.add, ALU.max,
                                                    mx[:, b, j:j + 1])
                last.then_inc(s_sm, 1)
                dve.wait_ge(s_sm, NSTEP * l + k + 1)
                if br == "A":
                    sk = sinks[:, l, heads[0]:heads[0] + nh]
                    link(dve.tensor_tensor(mx[:, b, 0:nh], mx[:, b, 0:nh], sk, ALU.max))
                    dve.tensor_tensor(sink_d[:, b, 0:nh], sk, mx[:, b, 0:nh], ALU.subtract)
                dve.tensor_scalar(nmx[:, b, 0:nh], mx[:, b, 0:nh], -1.0, None, ALU.mult).then_inc(s_nm, 1)

            def reciprocals(l, k):
                br, t, heads = STEPS[k]
                nh, b = len(heads), k % 4
                dve.wait_ge(s_p, NSTEP * l + k + 1)
                if k >= 4:
                    dve.wait_ge(s_o, NSTEP * l + k - 3)
                if br == "A":
                    link(dve.tensor_tensor(den[:, b, 0:nh], den[:, b, 0:nh], sink_e[:, b, 0:nh], ALU.add))
                link(dve.reciprocal(rden[:, b, 0:nh], den[:, b, 0:nh]))

            def outputs(l, k):
                br, t, heads = STEPS[k]
                nh, b = len(heads), k % 4
                dve.wait_ge(s_pv, NSTEP * l + k + 1)
                a = O_AT[br] + heads[0] * DH
                dve.tensor_tensor(o_tok[:, t, a:a + nh * DH].rearrange("p (h c) -> p h c", h=nh),
                                  bank[7][:, 0:nh * DH].rearrange("p (h c) -> p h c", h=nh),
                                  each(rden[:, b, 0:nh], DH), ALU.mult).then_inc(s_o, 1)

            def merge(l, ch, t):
                dve.wait_ge(s_gate, 4 * l + 2 * ch + t + 1)
                g = [gates[:, t, b * D + ch * COL:b * D + (ch + 1) * COL] for b in range(3)]
                for b in range(3):
                    last = dve.tensor_tensor(g[b], g[b], bank[(6 * ch + 3 * t + b) % 8][:], ALU.mult)
                link(last)
                link(dve.tensor_tensor(g[0], g[0], g[1], ALU.add))
                dve.tensor_tensor(g[0], g[0], g[2], ALU.add).then_inc(s_mg, 1)

            def add_to_stream(t, ch, src):
                a = xs[:, t, ch * COL:(ch + 1) * COL]
                dve.tensor_tensor(a, a, src[:], ALU.add).then_inc(s_xs, 1)

            def mixer(l):
                u = unit0(l)
                norm(2 * l)
                for j in range(2 * IN_CG):
                    if j in ROPE_SLOT:
                        apply_rope(l, ROPE_SLOT[j])
                    if j >= ATT_SLOT:
                        for r in (2 * (j - ATT_SLOT), 2 * (j - ATT_SLOT) + 1):
                            if r < NSTEP:
                                mask_and_max(l, r)
                            if 0 <= r - LAG_PT < NSTEP:
                                reciprocals(l, r - LAG_PT)
                            if 0 <= r - LAG_PV < NSTEP:
                                outputs(l, r - LAG_PV)
                    if j == 2 * IN_CG - 1:
                        for half in range(2):
                            split_transposed(4 * l + 1, half)
                    static(u + j + SPLIT)
                static(u + U_BR + SPLIT)
                dve.wait_ge(s_used, u + U_BR + 2)
                for t in range(TB):
                    merge(l, 0, t)
                static(u + U_BR + 1 + SPLIT)
                static(u + U_BR + 2 + SPLIT)
                split_transposed(4 * l + 2, 0)
                dve.wait_ge(s_used, u + U_OUT)
                for t in range(TB):
                    merge(l, 1, t)
                static(u + U_BR + 3 + SPLIT)
                split_transposed(4 * l + 2, 1)
                static(u + U_OUT + SPLIT)
                static(u + U_OUT + 1 + SPLIT)
                for ch in range(2):
                    dve.wait_ge(s_used, u + U_OUT + 2 + ch + 1)
                    for t in range(TB):
                        add_to_stream(t, ch, out_bank[ch][t])
                    times_gain(2 * l + 1, ch)
                    if l and ch:
                        for half in range(2):
                            split_transposed(4 * l + 3, half)
                    else:
                        split_before_transposed(u + U_OUT + 2 + ch + SPLIT, 4 * l + 3, ch)

            def times_up(par, tbs, done):
                dve.wait_ge(s_sil, done)
                for t in range(tbs):
                    to, s, up = act_tok[:, par, t, :], sil[:, par, t, :], bank[2 * par + t if tbs > 1 else par][:, FG:2 * FG]
                    if tbs > 1:
                        last = dve.scalar_tensor_tensor(out=to, in0=up, scalar=rstd[:, t:t + 1], in1=s, op0=ALU.mult, op1=ALU.mult)
                    else:
                        last = dve.tensor_tensor(to, s, up, ALU.mult)
                last.then_inc(s_act, 1)

            def split_act(par, tbs, ready):
                n = 2 * tbs * P
                dve.wait_ge(s_ath, ready)
                dve.tensor_tensor(aT_lo[:, par, 0:n], bank[2 * par if tbs > 1 else par][:, 0:n],
                                  aT_hi[:, par, 0:n].bitcast(F32), ALU.subtract).then_inc(s_atl, 1)

            def turn(split_at, k, par, tbs, done, last=False, down_too=True):
                if k:
                    split_act(1 - par, tbs, done)
                split_at(3)
                times_up(par, tbs, done + 1)
                if not last:
                    split_at(4)
                    if k and down_too:
                        split_at(5)

            times_gain(0, 0)
            split_transposed(0, 0)
            static(0)
            times_gain(0, 1)
            static(1)
            split_transposed(0, 1)
            static(2)
            mixer(0)
            norm(1)
            dve.wait_ge(s_rstd, 2)
            dve.wait_ge(s_rw, 1)
            dve.tensor_tensor(router_lo, router[:], router_hi.bitcast(F32), ALU.subtract).then_inc(s_rw, 1)
            n = MIX_UNITS
            for g in range(3):
                turn(lambda j: static(n + j), g, g % 2, TB, g)
                n += 3 if g else 2
            with dve.Fori(0, (DENSE_G - 5) // 2) as pair:
                for q in range(2):
                    v = n + 3 * q
                    turn(lambda j: split(v + j, pair * RAW + (v + j + 1)), 1, (3 + q) % 2, TB, pair * 2 + (3 + q))
            n += 3 * (DENSE_G - 5)
            for g in (DENSE_G - 2, DENSE_G - 1):
                turn(lambda j: static(n + j), 1, g % 2, TB, g, down_too=g < DENSE_G - 1)
                n += 3
            split_act((DENSE_G - 1) % 2, TB, DENSE_G)
            static(n + SPLIT - 1)
            for ch in range(2):
                dve.wait_ge(*((s_used, n + 1) if ch else (s_dh, 1)))
                for t in range(TB):
                    add_to_stream(t, ch, bank[4 + 2 * ch + t])
                times_gain(2, ch)
            split_before_transposed(n + SPLIT, 4, 1)
            mixer(1)
            norm(3)
            dve.wait_ge(s_rstd, 4)

            E = N_EXP
            dve.wait_ge(s_logT, 1)
            dve.tensor_copy(logits_T, bank[0][0:2 * E, 0:T]).then_inc(s_logc, 1)
            dve.wait_ge(s_log, 1)
            dve.wait_ge(s_route, 16)
            for part, to in ((1, r_t), (0, r_log)):
                for t in range(TB):
                    src, scale = bank[1][:, (2 * t + part) * E:(2 * t + part + 1) * E], rstd[:, t:t + 1]
                    if part:
                        last = dve.tensor_scalar(to[:, t, :], src, scale, None, ALU.mult)
                    else:
                        last = dve.scalar_tensor_tensor(out=to[:, t, :], in0=src, scalar=scale, in1=r_t[:, t, :],
                                                        op0=ALU.mult, op1=ALU.add)
                link(last)
            for src, top, chosen in ((r_log, r_m1, r_first), (r_l2, r_m2, r_second)):
                link(dve.tensor_reduce(top, src, AX, ALU.max))
                link(dve.tensor_tensor(r_eq, src, each(top, E), ALU.is_equal))
                link(dve.tensor_tensor(r_t, r_eq, over(c_desc, TB), ALU.mult))
                link(dve.tensor_reduce(r_den, r_t, AX, ALU.max))
                link(dve.tensor_tensor(chosen, r_t, each(r_den, E), ALU.is_equal))
                if src is r_log:
                    link(dve.scalar_tensor_tensor(out=r_l2, in0=r_first, scalar=-3e38, in1=r_log, op0=ALU.mult, op1=ALU.add))
            dve.tensor_tensor(r_sel, r_first, r_second, ALU.add).then_inc(s_sel, 1)
            dve.tensor_tensor(r_c, r_m2, r_m1, ALU.subtract).then_inc(s_rexpin, 1)
            dve.wait_ge(s_hth, 2)
            dve.scalar_tensor_tensor(out=htok_lo[:, 1, :], in0=h_tok[:, 1, :], scalar=rstd[:, 1:2],
                                     in1=htok_hi[:, 1, :].bitcast(F32), op0=ALU.mult, op1=ALU.subtract).then_inc(s_htl, 1)
            dve.wait_ge(s_rank, 1)
            rank = bank[7][:, 0:TB * E].rearrange("p (t e) -> p t e", t=TB)
            link(dve.scalar_tensor_tensor(out=r_rank, in0=rank, scalar=1.0, in1=r_sel, op0=ALU.add, op1=ALU.mult))
            link(dve.tensor_scalar(item_slot[:, :, 0:E], r_rank, -1.0, None, ALU.add))

            def weigh_choices():
                dve.wait_ge(s_rexp, 1)
                link(dve.tensor_scalar(r_den, r_e, 1.0, None, ALU.add))
                link(dve.reciprocal(r_w1, r_den))
                link(dve.tensor_tensor(r_w2, r_e, r_w1, ALU.mult))
                dve.tensor_tensor(r_first, r_first, each(r_w1, E), ALU.mult)
                link(dve.tensor_tensor(r_second, r_second, each(r_w2, E), ALU.mult))
                link(dve.tensor_tensor(r_w, r_first, r_second, ALU.add))
                link(dve.tensor_copy(item_w[:, :, 0:E], r_w))
                dve.wait_ge(s_count, 1)
                link(dve.tensor_scalar(r_over, bank[3][:, 0:E], float(P), None, ALU.is_gt))
                dve.tensor_tensor_scan(r_cum, c_ones[:, 0:E], r_over, 0.0, ALU.mult, ALU.add).then_inc(s_over, 1)

            def split_at(i, j, pair=None):
                rounded = moe_unit(i, j + 1)
                split(MOE_U0 + j, rounded if pair is None else pair * RAW + rounded)

            def pick_tokens(i):
                for t in range(TB):
                    last = dve.tensor_scalar(pick[:, t, :], c_slot, item_slot[:, t, bass.ds(i, 1)], None, ALU.is_equal)
                last.then_inc(s_pick, 1)

            def weigh_picked(i):
                for t in range(TB):
                    slot, w = item_slot[:, t, bass.ds(i, 1)], item_w[:, t, bass.ds(i, 1)]
                    last = dve.tensor_scalar(pick_w[:, t, :], c_slot, slot, w, ALU.is_equal, ALU.mult)
                last.then_inc(s_pickw, 1)

            def split_gathered(i, banks=(0, 1)):
                for b in banks:
                    dve.wait_ge(s_gah, i * 2 + (b + 1))
                    to = slice(4 * b, 4 * b + 4)
                    dve.tensor_tensor(xg_lo[:, to, :].rearrange("p k t -> p (k t)"), bank[4 + b][:],
                                      xg_hi[:, to, :].bitcast(F32).rearrange("p k t -> p (k t)"),
                                      ALU.subtract).then_inc(s_gal, 1)

            def head(i):
                pick_tokens(i)
                if isinstance(i, int):
                    static(MOE_U0 + SPLIT - 1)
                    split_gathered(i, (0,))
                    weigh_choices()
                    weigh_picked(i)
                    split_gathered(i, (1,))
                else:
                    weigh_picked(i)
                    for j in range(SPLIT):
                        split_at(i, j)
                    split_gathered(i)
                turn(lambda j: split_at(i, j), 0, 0, 1, ff0(i))

            def middle(i, has_next=False):
                turn(lambda j: split_at(i, 2 + j), 1, 1, 1, ff0(i) + 1)
                dve.wait_ge(s_bkh, i + 1)
                dve.tensor_tensor(back_lo[:], bank[4][:, 0:T], back_hi[:].bitcast(F32), ALU.subtract).then_inc(s_bkl, 1)
                with dve.Fori(0, EXPERT_G // 2 - 2) as pair:
                    for q in range(2):
                        v = 5 + 3 * q
                        turn(lambda j: split_at(i, v + j, pair), 1, q, 1, pair * 2 + (ff0(i) + (2 + q)))
                turn(lambda j: split_at(i, TAIL - 3 + j), 1, 0, 1, ff0(i) + (EXPERT_G - 2))
                if has_next:
                    pick_tokens(i + 1)
                    weigh_picked(i + 1)
                turn(lambda j: split_at(i, TAIL + j), 1, 1, 1, ff0(i) + (EXPERT_G - 1), last=True)

            def split_output(i):
                for ch in range(2):
                    dve.wait_ge(s_yh, i * 2 + (ch + 1))
                    a = slice(ch * COL, (ch + 1) * COL)
                    dve.tensor_tensor(y_lo[:, a], bank[2 + ch][:], y_hi[:, a].bitcast(F32), ALU.subtract).then_inc(s_yl, 1)

            def add_output(i):
                for ch in range(2):
                    for t in range(TB):
                        dve.wait_ge(s_cmb, i * 4 + (2 * ch + t + 1))
                        add_to_stream(t, ch, bank[4 + 2 * ch + t])

            head(0)
            with dve.Fori(0, N_EXP - 1) as i:
                middle(i, has_next=True)
                split_at(i, ITEM_UNITS)
                split_act(1, 1, ff0(i + 1))
                split_at(i, ITEM_UNITS + 1)
                split_gathered(i + 1)
                split_output(i)
                split_at(i, ITEM_UNITS + 2)
                turn(lambda j: split_at(i, ITEM_UNITS + j), 0, 0, 1, ff0(i + 1))
                add_output(i)
            middle(N_EXP - 1)
            split_act(1, 1, ff0(N_EXP))
            split_output(N_EXP - 1)
            add_output(N_EXP - 1)
            dve.wait_ge(s_meta, 1)
            items = dve.value_load(meta[0:1, 0:1], min_val=N_EXP, max_val=ITEMS)
            with dve.If(items > N_EXP):
                with dve.Fori(N_EXP, items) as i:
                    head(i)
                    middle(i)
                    split_act(1, 1, ff0(i + 1))
                    split_output(i)
                    add_output(i)
            dve.wait_ge(s_xs, xs_before_item(items - 1) + 4)
            times_gain(4, 0, False)
            norm(4)
            dve.wait_ge(s_rstd, 5)
            for t in range(TB):
                dve.scalar_tensor_tensor(out=h_tok[:, t, COL:D], in0=xs[:, t, COL:D], scalar=rstd[:, t:t + 1],
                                         in1=gain[:, COL:D], op0=ALU.mult, op1=ALU.mult).then_inc(s_y[1], 1)


def _constants():
    i, j = np.arange(P)[:, None] + P, np.arange(T)[None, :]
    gap = i - j
    inside = {
        "A": ((gap >= 0) & (gap <= 127)).astype(np.float64),
        "B": (gap >= 0).astype(np.float64),
        "C": ((gap >= 0) & (gap <= 128)).astype(np.float64) + ((gap >= 0) & (gap % 4 == 0)) + ((gap >= 0) & (gap % 16 == 0)),
    }
    masks = np.stack([np.where(m > 0, np.log(np.maximum(m, 1.0)), NEG) / SCALE for m in inside.values()], axis=1)
    pos = np.arange(T, dtype=np.float32)
    inv = np.float32(10000.0) ** (-np.arange(0, DH, 2, dtype=np.float32) / np.float32(DH))
    ang = pos[:, None] * inv[None, :]
    cos, sin = np.cos(ang), np.sin(ang)
    tables = np.stack([np.concatenate([cos, cos], 1), np.concatenate([-sin, sin], 1)], axis=1)
    tables = tables.reshape(TB, P, 2, DH).transpose(1, 0, 2, 3)
    k = np.arange(P)
    before = (k[:, None] < k[None, :])
    e = np.arange(N_EXP)
    route = np.concatenate([before, np.ones((P, P)), np.tile(k, (P, 1)), np.tile(N_EXP - e, (P, 1)), np.tile(e, (P, 1))], axis=1)
    f = np.float32
    return (np.eye(P, dtype=f), np.ascontiguousarray(masks.astype(f)), np.ascontiguousarray(tables.astype(f)),
            np.ascontiguousarray(route.astype(f)))


def kernel(x, norm_mix, w_in, attn_sinks, w_br_a, w_br_b, w_br_c, w_out, norm_ffn, w_ff_gate, w_ff_up, w_ff_down,
           w_router, w_moe_gate, w_moe_up, w_moe_down, norm_final):
    import concourse.bacc as _bacc
    from concourse.bass_utils import run_bass_kernel_spmd as _run

    ident, masks, tables, route = _constants()
    ins = {
        "x": x, "norm_mix": norm_mix, "w_in": w_in, "attn_sinks": attn_sinks,
        "w_br": np.concatenate([np.asarray(w_br_a), np.asarray(w_br_b), np.asarray(w_br_c)], axis=1),
        "w_out": w_out, "norm_ffn": norm_ffn, "w_ff_gate": w_ff_gate, "w_ff_up": w_ff_up, "w_ff_down": w_ff_down,
        "w_router": w_router, "w_moe_gate": w_moe_gate, "w_moe_up": w_moe_up, "w_moe_down": w_moe_down,
        "norm_final": norm_final, "c_ident": ident, "c_masks": masks, "c_rope": tables, "c_route": route,
    }
    nc = _bacc.Bacc("TRN2", target_bir_lowering=False, num_devices=1)
    arrays, args = {}, []
    for name, a in ins.items():
        a = np.ascontiguousarray(a)
        arrays[f"in_{name}"] = a
        args.append(nc.dram_tensor(f"in_{name}", a.shape, mybir.dt.from_np(a.dtype), kind="ExternalInput").ap())
    args.append(nc.dram_tensor("out_0", (1, T, D), F32, kind="ExternalOutput").ap())
    bass_trunk(nc, *args)
    r = _run(nc, [arrays], core_ids=[0])
    return r.results[0]["out_0"]
```
